# Optimizing a Trainium2 kernel written in Bass

```python
import math
import jax
import jax.numpy as jnp
from jax import lax
import numpy as np
import jax, jax.numpy as jnp

D_MODEL = 2048
BATCH = 1
SEQ = 256
DEPTH = 2

N_A_LAYERS = DEPTH // 2
N_B_LAYERS = DEPTH - N_A_LAYERS

SSM_WIDTH = D_MODEL // 2
SSM_GROUP = 16
SSM_GROUPS = SSM_WIDTH // SSM_GROUP
SSM_STATE = 64
DT_MIN = 0.001
DT_MAX = 0.1

N_HEADS = 16
HEAD_DIM = 128
N_KV_HEADS = 4
HEADS_PER_KV = N_HEADS // N_KV_HEADS
ATTN_WIDTH = N_HEADS * HEAD_DIM
KV_WIDTH = N_KV_HEADS * HEAD_DIM
N_BRANCH = 3
CMP_BLOCK = 32
CMP_STRIDE = 16
SEL_BLOCK = 64
N_SELECT = 16
WINDOW = 512
Q_BLOCK = 64
B_IN_WIDTH = ATTN_WIDTH * (1 + N_BRANCH) + N_BRANCH * N_HEADS

LN_EPS = 1e-5
DEEPNORM_ALPHA = (2 * DEPTH) ** 0.25
DEEPNORM_BETA = (8 * DEPTH) ** -0.25
MASK_VALUE = -1e30
FORCE_SCORE = 1e6


def layer_norm(x, g, b):
    x32 = x.astype(jnp.float32)
    mu = jnp.mean(x32, axis=-1, keepdims=True)
    var = jnp.mean(jnp.square(x32 - mu), axis=-1, keepdims=True)
    return ((x32 - mu) * lax.rsqrt(var + LN_EPS) * g.astype(jnp.float32) + b.astype(jnp.float32)).astype(x.dtype)

def _complex_linear_combine(e1, e2):
    a1r, a1i, b1r, b1i = e1
    a2r, a2i, b2r, b2i = e2
    return (a2r * a1r - a2i * a1i,
            a2r * a1i + a2i * a1r,
            a2r * b1r - a2i * b1i + b2r,
            a2r * b1i + a2i * b1r + b2i)

def s5_mixer(x, w_in, lam_re, lam_im, log_dt, b_re, b_im, c_re, c_im, d_skip, w_glu, b_glu, w_out):
    bsz, seq, _ = x.shape
    f32 = jnp.float32
    u, z = jnp.split(x @ w_in, 2, axis=-1)
    lr = lam_re.astype(f32)
    li = lam_im.astype(f32)
    dt = jnp.exp(log_dt.astype(f32))[:, None]
    mag = jnp.exp(lr * dt)
    ar = mag * jnp.cos(li * dt)
    ai = mag * jnp.sin(li * dt)
    inv_abs2 = 1.0 / (lr * lr + li * li)
    cr = ((ar - 1.0) * lr + ai * li) * inv_abs2
    ci = (ai * lr - (ar - 1.0) * li) * inv_abs2
    br = b_re.astype(f32)
    bi = b_im.astype(f32)
    bbar_r = cr[..., None] * br - ci[..., None] * bi
    bbar_i = cr[..., None] * bi + ci[..., None] * br
    ug = jnp.swapaxes(u, 0, 1).astype(f32).reshape(seq, bsz, SSM_GROUPS, SSM_GROUP)
    bu_r = jnp.einsum('lbgc,gpc->lbgp', ug, bbar_r)
    bu_i = jnp.einsum('lbgc,gpc->lbgp', ug, bbar_i)
    a_shape = (seq, 1, SSM_GROUPS, SSM_STATE)
    _, _, h_r, h_i = lax.associative_scan(
        _complex_linear_combine,
        (jnp.broadcast_to(ar, a_shape), jnp.broadcast_to(ai, a_shape), bu_r, bu_i),
        axis=0)
    y = (jnp.einsum('gcp,lbgp->lbgc', c_re.astype(f32), h_r)
         - jnp.einsum('gcp,lbgp->lbgc', c_im.astype(f32), h_i))
    y = jnp.swapaxes(y.reshape(seq, bsz, SSM_WIDTH), 0, 1).astype(x.dtype) + d_skip * u
    g = jax.nn.gelu(y)
    y = g * jax.nn.sigmoid(g @ w_glu + b_glu)
    return (y * jax.nn.silu(z)) @ w_out

def shared_kv(h, kv_w, pos_k, w1_k, w2_k, pos_v, w1_v, w2_v):
    bsz, seq, _ = h.shape
    kv = (h @ kv_w).reshape(bsz, seq, 2 * N_BRANCH, N_KV_HEADS, HEAD_DIM)
    k_c, v_c, k_s, v_s, k_w, v_w = [kv[:, :, i] for i in range(2 * N_BRANCH)]
    n_cmp = (seq - CMP_BLOCK) // CMP_STRIDE + 1
    idx = jnp.arange(n_cmp)[:, None] * CMP_STRIDE + jnp.arange(CMP_BLOCK)[None, :]

    def compress(t, pos, w1, w2):
        blk = t[:, idx] + pos[None, None, :, None, :]
        blk = jnp.moveaxis(blk, 3, 2).reshape(bsz, n_cmp, N_KV_HEADS, CMP_BLOCK * HEAD_DIM)
        return jax.nn.gelu(blk @ w1) @ w2

    return (compress(k_c, pos_k, w1_k, w2_k), compress(v_c, pos_v, w1_v, w2_v), k_s, v_s, k_w, v_w)

def masked_softmax(s, valid):
    s = jnp.where(valid, s, MASK_VALUE)
    m = jnp.max(s, axis=-1, keepdims=True)
    e = jnp.where(valid, jnp.exp(s - m), 0.0)
    return e / jnp.maximum(jnp.sum(e, axis=-1, keepdims=True), 1e-30)

def nsa_attention(q, k_cmp, v_cmp, k_slc, v_slc, k_win, v_win):
    bsz, seq = q.shape[:2]
    dtype = q.dtype
    f32 = jnp.float32
    n_q = seq // Q_BLOCK
    n_cmp = k_cmp.shape[1]
    n_sblk = seq // SEL_BLOCK
    n_sel = min(N_SELECT, n_sblk)
    scale = HEAD_DIM ** -0.5
    cmp_start = jnp.arange(n_cmp) * CMP_STRIDE
    cmp_end = cmp_start + CMP_BLOCK - 1
    sel_start = jnp.arange(n_sblk) * SEL_BLOCK
    overlap = ((cmp_start[:, None] < sel_start[None, :] + SEL_BLOCK)
               & (cmp_end[:, None] >= sel_start[None, :])).astype(f32)
    kb_s = k_slc.reshape(bsz, n_sblk, SEL_BLOCK, N_KV_HEADS, HEAD_DIM).transpose(0, 3, 1, 2, 4)
    vb_s = v_slc.reshape(bsz, n_sblk, SEL_BLOCK, N_KV_HEADS, HEAD_DIM).transpose(0, 3, 1, 2, 4)
    k_w_pad = jnp.pad(k_win, ((0, 0), (WINDOW, 0), (0, 0), (0, 0)))
    v_w_pad = jnp.pad(v_win, ((0, 0), (WINDOW, 0), (0, 0), (0, 0)))
    qg = q.reshape(bsz, n_q, Q_BLOCK, N_KV_HEADS, HEADS_PER_KV, HEAD_DIM).transpose(1, 0, 2, 3, 4, 5)
    gather_blocks = jax.vmap(jax.vmap(lambda blocks, ids: blocks[ids]))
    blk_ids = jnp.arange(n_sblk)

    def block_fn(args):
        i, qb = args
        t = i * Q_BLOCK + jnp.arange(Q_BLOCK)
        qb = qb * scale
        s = jnp.einsum('bqghd,bngd->bghqn', qb, k_cmp).astype(f32)
        p_cmp = masked_softmax(s, cmp_end[None, :] <= t[:, None])
        o_cmp = jnp.einsum('bghqn,bngd->bqghd', p_cmp.astype(dtype), v_cmp)
        imp = jnp.einsum('bghqn,nj->bgqj', p_cmp, overlap)
        cur = t // SEL_BLOCK
        future = blk_ids[None, :] > cur[:, None]
        forced = ((blk_ids[None, :] == 0) | (blk_ids[None, :] == cur[:, None])
                  | (blk_ids[None, :] == cur[:, None] - 1))
        imp = jnp.where(future, MASK_VALUE, jnp.where(forced, FORCE_SCORE, imp))
        _, sel = lax.top_k(imp, n_sel)
        ks = gather_blocks(kb_s, sel).reshape(bsz, N_KV_HEADS, Q_BLOCK, n_sel * SEL_BLOCK, HEAD_DIM)
        vs = gather_blocks(vb_s, sel).reshape(bsz, N_KV_HEADS, Q_BLOCK, n_sel * SEL_BLOCK, HEAD_DIM)
        pos = (sel[..., None] * SEL_BLOCK + jnp.arange(SEL_BLOCK)).reshape(bsz, N_KV_HEADS, Q_BLOCK, n_sel * SEL_BLOCK)
        valid = (pos <= t[None, None, :, None])[:, :, None]
        s = jnp.einsum('bqghd,bgqkd->bghqk', qb, ks).astype(f32)
        p = masked_softmax(s, valid)
        o_slc = jnp.einsum('bghqk,bgqkd->bqghd', p.astype(dtype), vs)
        kw = lax.dynamic_slice_in_dim(k_w_pad, i * Q_BLOCK, WINDOW + Q_BLOCK, axis=1)
        vw = lax.dynamic_slice_in_dim(v_w_pad, i * Q_BLOCK, WINDOW + Q_BLOCK, axis=1)
        kpos = i * Q_BLOCK - WINDOW + jnp.arange(WINDOW + Q_BLOCK)
        valid = ((kpos[None, :] <= t[:, None]) & (kpos[None, :] > t[:, None] - WINDOW)
                 & (kpos[None, :] >= 0))
        s = jnp.einsum('bqghd,bkgd->bghqk', qb, kw).astype(f32)
        p = masked_softmax(s, valid)
        o_win = jnp.einsum('bghqk,bkgd->bqghd', p.astype(dtype), vw)
        return o_cmp, o_slc, o_win

    o_cmp, o_slc, o_win = lax.map(block_fn, (jnp.arange(n_q), qg))

    def unblock(o):
        return o.transpose(1, 0, 2, 3, 4, 5).reshape(bsz, seq, N_HEADS, HEAD_DIM)

    return (unblock(o_cmp), unblock(o_slc), unblock(o_win))

def nsa_mixer(x, w_in, w_out, shared):
    bsz, seq, _ = x.shape
    proj = x @ w_in
    q = proj[..., :ATTN_WIDTH].reshape(bsz, seq, N_HEADS, HEAD_DIM)
    z = proj[..., ATTN_WIDTH:ATTN_WIDTH * (1 + N_BRANCH)].reshape(bsz, seq, N_BRANCH, N_HEADS, HEAD_DIM)
    gate = jax.nn.sigmoid(proj[..., ATTN_WIDTH * (1 + N_BRANCH):].reshape(bsz, seq, N_BRANCH, N_HEADS))
    o = jnp.stack(nsa_attention(q, *shared), axis=2)
    y = jnp.sum(gate[..., None] * o * jax.nn.silu(z), axis=2).reshape(bsz, seq, ATTN_WIDTH)
    return y @ w_out

def first_inputs(seed: int = 0) -> dict:
    key = jax.random.key(seed)
    ks = jax.random.split(key, 24)
    nrm = jax.random.normal
    f32 = jnp.float32
    na, nb = N_A_LAYERS, N_B_LAYERS
    g, p, c, e = SSM_GROUPS, SSM_STATE, SSM_GROUP, SSM_WIDTH
    lam_im0 = math.pi * jnp.arange(p, dtype=f32)
    return {
        "x": nrm(ks[0], (BATCH, SEQ, D_MODEL), f32),
        "a_w_in": nrm(ks[1], (na, D_MODEL, 2 * e), f32) * D_MODEL ** -0.5,
        "a_lam_re": -0.5 + 0.01 * nrm(ks[2], (na, g, p), f32),
        "a_lam_im": lam_im0 + 0.01 * nrm(ks[3], (na, g, p), f32),
        "a_log_dt": jax.random.uniform(ks[4], (na, g), f32, math.log(DT_MIN), math.log(DT_MAX)),
        "a_b_re": nrm(ks[5], (na, g, p, c), f32) * (2 * c) ** -0.5,
        "a_b_im": nrm(ks[6], (na, g, p, c), f32) * (2 * c) ** -0.5,
        "a_c_re": nrm(ks[7], (na, g, c, p), f32) * p ** -0.5,
        "a_c_im": nrm(ks[8], (na, g, c, p), f32) * p ** -0.5,
        "a_d": nrm(ks[9], (na, e), f32),
        "a_w_glu": nrm(ks[10], (na, e, e), f32) * e ** -0.5,
        "a_b_glu": 0.01 * nrm(ks[11], (na, e), f32),
        "a_w_out": nrm(ks[12], (na, e, D_MODEL), f32) * e ** -0.5 * DEEPNORM_BETA,
        "kv_w": nrm(ks[13], (D_MODEL, 2 * N_BRANCH * KV_WIDTH), f32) * D_MODEL ** -0.5,
        "cmp_pos_k": 0.02 * nrm(ks[14], (CMP_BLOCK, HEAD_DIM), f32),
        "cmp_w1_k": nrm(ks[15], (CMP_BLOCK * HEAD_DIM, HEAD_DIM), f32) * (CMP_BLOCK * HEAD_DIM) ** -0.5,
        "cmp_w2_k": nrm(ks[16], (HEAD_DIM, HEAD_DIM), f32) * HEAD_DIM ** -0.5,
        "cmp_pos_v": 0.02 * nrm(ks[17], (CMP_BLOCK, HEAD_DIM), f32),
        "cmp_w1_v": nrm(ks[18], (CMP_BLOCK * HEAD_DIM, HEAD_DIM), f32) * (CMP_BLOCK * HEAD_DIM) ** -0.5,
        "cmp_w2_v": nrm(ks[19], (HEAD_DIM, HEAD_DIM), f32) * HEAD_DIM ** -0.5,
        "b_w_in": nrm(ks[20], (nb, D_MODEL, B_IN_WIDTH), f32) * D_MODEL ** -0.5,
        "b_w_out": nrm(ks[21], (nb, ATTN_WIDTH, D_MODEL), f32) * ATTN_WIDTH ** -0.5 * DEEPNORM_BETA,
        "ln_g": 1.0 + 0.01 * nrm(ks[22], (DEPTH, D_MODEL), f32),
        "ln_b": 0.01 * nrm(ks[23], (DEPTH, D_MODEL), f32),
    }

def first_block(x, a_w_in, a_lam_re, a_lam_im, a_log_dt, a_b_re, a_b_im, a_c_re, a_c_im, a_d,
              a_w_glu, a_b_glu, a_w_out, kv_w, cmp_pos_k, cmp_w1_k, cmp_w2_k, cmp_pos_v,
              cmp_w1_v, cmp_w2_v, b_w_in, b_w_out, ln_g, ln_b):
    shared = None
    for layer in range(DEPTH):
        if layer < N_A_LAYERS:
            i = layer
            y = s5_mixer(x, a_w_in[i], a_lam_re[i], a_lam_im[i], a_log_dt[i], a_b_re[i], a_b_im[i],
                         a_c_re[i], a_c_im[i], a_d[i], a_w_glu[i], a_b_glu[i], a_w_out[i])
        else:
            i = layer - N_A_LAYERS
            y = nsa_mixer(x, b_w_in[i], b_w_out[i], shared)
        x = layer_norm(DEEPNORM_ALPHA * x + y, ln_g[layer], ln_b[layer])
        if layer == N_A_LAYERS - 1:
            shared = shared_kv(x, kv_w, cmp_pos_k, cmp_w1_k, cmp_w2_k, cmp_pos_v, cmp_w1_v, cmp_w2_v)
    return x


N_RET_HEADS = D_MODEL // (2 * HEAD_DIM)
N_NA_HEADS = D_MODEL // (2 * HEAD_DIM)
N_DIFF_HEADS = D_MODEL // (2 * HEAD_DIM)
N_X_HEADS = 4
X_HEAD_DIM = 128
N_MEM = 256
GRID_W = 64
NA_WIN_ROWS = 8
NA_WIN_COLS = 16
RET_CHUNK = 128
ATTN_BLOCK = 128
FFN_HIDDEN = -((-8 * D_MODEL) // (3 * 256)) * 256
RMS_EPS = 1e-6


def rms_norm(x, g):
    xf = x.astype(jnp.float32)
    y = xf * lax.rsqrt(jnp.mean(xf * xf, axis=-1, keepdims=True) + RMS_EPS)
    return (y * g.astype(jnp.float32)).astype(x.dtype)

def alibi_slopes(n):
    return 2.0 ** (-8.0 * jnp.arange(1, n + 1, dtype=jnp.float32) / n)

def chunk_retention(q, k, v, log_gamma, include_diag):
    b, h, s, d = q.shape
    dv = v.shape[-1]
    n = s // RET_CHUNK

    def to_chunks(t):
        return t.reshape(b, h, n, RET_CHUNK, t.shape[-1]).transpose(2, 0, 1, 3, 4)

    idx = jnp.arange(RET_CHUNK, dtype=jnp.float32)
    diff = idx[:, None] - idx[None, :]
    mask = (diff >= 0) if include_diag else (diff > 0)
    d_intra = jnp.where(mask, jnp.exp(log_gamma[:, None, None] * jnp.maximum(diff, 0.0)), 0.0)
    q_decay = jnp.exp(log_gamma[:, None] * (idx + 1.0))[:, :, None]
    k_decay = jnp.exp(log_gamma[:, None] * (RET_CHUNK - 1.0 - idx))[:, :, None]
    c_decay = jnp.exp(log_gamma * RET_CHUNK)[:, None, None]

    def step(state, qkv):
        qc, kc, vc = qkv
        scores = jnp.einsum('bhid,bhjd->bhij', qc, kc) * d_intra
        inner = jnp.einsum('bhij,bhje->bhie', scores, vc)
        cross = jnp.einsum('bhid,bhde->bhie', qc * q_decay, state)
        state = state * c_decay + jnp.einsum('bhjd,bhje->bhde', kc * k_decay, vc)
        return state, inner + cross

    state0 = jnp.zeros((b, h, d, dv), jnp.float32)
    _, out = lax.scan(step, state0, (to_chunks(q), to_chunks(k), to_chunks(v)))
    return out.transpose(1, 2, 0, 3, 4).reshape(b, h, s, dv)

def neighborhood_attention(q, k, v, rpb):
    b, h, s, d = q.shape
    rows = s // GRID_W
    wr = min(NA_WIN_ROWS, rows)
    qg = q.reshape(b, h, rows, GRID_W, d)
    kg = k.reshape(b, h, rows, GRID_W, d)
    vg = v.reshape(b, h, rows, GRID_W, d)
    col = jnp.arange(GRID_W)
    cs = jnp.clip(col - NA_WIN_COLS // 2, 0, GRID_W - NA_WIN_COLS)
    colidx = cs[:, None] + jnp.arange(NA_WIN_COLS)[None, :]
    dc_idx = colidx - col[:, None] + NA_WIN_COLS - 1
    scale = HEAD_DIM ** -0.5

    def row_fn(r):
        rs = jnp.clip(r - wr // 2, 0, rows - wr)
        krow = lax.dynamic_slice_in_dim(kg, rs, wr, axis=2)
        vrow = lax.dynamic_slice_in_dim(vg, rs, wr, axis=2)
        kw = krow[:, :, :, colidx, :]
        vw = vrow[:, :, :, colidx, :]
        qr = lax.dynamic_index_in_dim(qg, r, axis=2, keepdims=False)
        logits = jnp.einsum('bhcd,bhrcjd->bhcrj', qr, kw).astype(jnp.float32) * scale
        dr_idx = rs + jnp.arange(wr) - r + NA_WIN_ROWS - 1
        bias = rpb[:, dr_idx][:, :, dc_idx].astype(jnp.float32)
        logits = logits + bias.transpose(0, 2, 1, 3)[None]
        p = jax.nn.softmax(logits.reshape(b, h, GRID_W, wr * NA_WIN_COLS), axis=-1)
        p = p.reshape(b, h, GRID_W, wr, NA_WIN_COLS)
        return jnp.einsum('bhcrj,bhrcjd->bhcd', p, vw.astype(jnp.float32)).astype(v.dtype)

    out = lax.map(row_fn, jnp.arange(rows))
    return out.transpose(1, 2, 0, 3, 4).reshape(b, h, s, d)

def retention_na_mixer(h, w_in, dec_f, dec_b, ret_g, na_q_g, na_k_g, rpb, w_out):
    b, s, _ = h.shape
    proj = h @ w_in
    rq, rk, rv, rg, nq, nk, nv = jnp.split(proj, 7, axis=-1)

    def heads(t):
        return t.reshape(b, s, -1, HEAD_DIM).transpose(0, 2, 1, 3)

    f32 = jnp.float32
    rq = heads(rq).astype(f32)
    rk = heads(rk).astype(f32) * (HEAD_DIM ** -0.5)
    rv = heads(rv).astype(f32)
    lg_f = jax.nn.log_sigmoid(dec_f.astype(f32))
    lg_b = jax.nn.log_sigmoid(dec_b.astype(f32))
    fwd = chunk_retention(rq, rk, rv, lg_f, True)
    bwd = jnp.flip(chunk_retention(jnp.flip(rq, 2), jnp.flip(rk, 2), jnp.flip(rv, 2), lg_b, False), 2)
    ret = rms_norm(fwd + bwd, ret_g)
    ret = ret.transpose(0, 2, 1, 3).reshape(b, s, -1).astype(h.dtype) * jax.nn.silu(rg)

    na = neighborhood_attention(rms_norm(heads(nq), na_q_g), rms_norm(heads(nk), na_k_g), heads(nv), rpb)
    na = na.transpose(0, 2, 1, 3).reshape(b, s, -1)
    return jnp.concatenate([ret, na], axis=-1) @ w_out

def diff_attention_mixer(h, w_in, q_g, k_g, lq1, lk1, lq2, lk2, out_g, w_out, layer_idx):
    b, s, _ = h.shape
    f32 = jnp.float32
    proj = h @ w_in
    q, k, v = jnp.split(proj, 3, axis=-1)
    q = rms_norm(q.reshape(b, s, N_DIFF_HEADS, 2, HEAD_DIM), q_g).transpose(3, 0, 2, 1, 4)
    k = rms_norm(k.reshape(b, s, N_DIFF_HEADS, 2, HEAD_DIM), k_g).transpose(3, 0, 2, 1, 4)
    vf = v.reshape(b, s, N_DIFF_HEADS, 2 * HEAD_DIM).transpose(0, 2, 1, 3).astype(f32)
    lam_init = 0.8 - 0.6 * math.exp(-0.3 * layer_idx)
    lam = (jnp.exp(jnp.sum(lq1.astype(f32) * lk1.astype(f32)))
           - jnp.exp(jnp.sum(lq2.astype(f32) * lk2.astype(f32))) + lam_init)
    slopes = alibi_slopes(N_DIFF_HEADS)
    scale = HEAD_DIM ** -0.5
    nb = s // ATTN_BLOCK
    qb = q.reshape(2, b, N_DIFF_HEADS, nb, ATTN_BLOCK, HEAD_DIM).transpose(3, 0, 1, 2, 4, 5)
    key_pos = jnp.arange(s, dtype=f32)

    def block_fn(args):
        qblk, bi = args
        qpos = (bi * ATTN_BLOCK + jnp.arange(ATTN_BLOCK)).astype(f32)
        alibi = -slopes[:, None, None] * jnp.abs(qpos[:, None] - key_pos[None, :])
        logits = jnp.einsum('cbhqd,cbhkd->cbhqk', qblk, k).astype(f32) * scale + alibi
        p = jax.nn.softmax(logits, axis=-1)
        a = p[0] - lam * p[1]
        return jnp.einsum('bhqk,bhke->bhqe', a, vf)

    out = lax.map(block_fn, (qb, jnp.arange(nb)))
    out = out.transpose(1, 2, 0, 3, 4).reshape(b, N_DIFF_HEADS, s, 2 * HEAD_DIM)
    out = rms_norm(out, out_g) * (1.0 - lam_init)
    out = out.transpose(0, 2, 1, 3).reshape(b, s, -1).astype(h.dtype)
    return out @ w_out

def memory_cross_attention(h, m, w_q, w_kv, w_o, q_g, k_g):
    b, s, _ = h.shape
    nm = m.shape[1]
    q = rms_norm((h @ w_q).reshape(b, s, N_X_HEADS, X_HEAD_DIM), q_g)
    kv = (m @ w_kv).reshape(b, nm, 2, N_X_HEADS, X_HEAD_DIM)
    k = rms_norm(kv[:, :, 0], k_g)
    v = kv[:, :, 1]
    logits = jnp.einsum('bshd,bmhd->bhsm', q, k).astype(jnp.float32) * (X_HEAD_DIM ** -0.5)
    p = jax.nn.softmax(logits, axis=-1)
    o = jnp.einsum('bhsm,bmhd->bshd', p, v.astype(jnp.float32)).astype(h.dtype)
    return o.reshape(b, s, -1) @ w_o

def swiglu_ffn(h, w_in, w_out):
    g, u = jnp.split(h @ w_in, 2, axis=-1)
    return (jax.nn.silu(g) * u) @ w_out

def second_inputs(seed: int = 0) -> dict:
    key = jax.random.key(seed)
    ks = list(jax.random.split(key, 32))
    n_even = (DEPTH + 1) // 2
    n_odd = DEPTH // 2
    f32 = jnp.float32

    def w(k, shape, fan_in):
        return jax.random.normal(k, shape, f32) * (fan_in ** -0.5)

    def gain(k, shape):
        return 1.0 + 0.02 * jax.random.normal(k, shape, f32)

    def small(k, shape, sc):
        return sc * jax.random.normal(k, shape, f32)

    ab_width = (N_RET_HEADS + N_NA_HEADS) * HEAD_DIM
    ab_in_cols = 4 * N_RET_HEADS * HEAD_DIM + 3 * N_NA_HEADS * HEAD_DIM
    c_width = N_DIFF_HEADS * 2 * HEAD_DIM
    x_width = N_X_HEADS * X_HEAD_DIM
    base_logit = jnp.asarray(np.log(2.0 ** (5 + np.arange(N_RET_HEADS)) - 1.0), f32)

    return {
        "x": jax.random.normal(ks[0], (BATCH, SEQ, D_MODEL), f32),
        "mem": jax.random.normal(ks[1], (BATCH, N_MEM, D_MODEL), f32),
        "norm_mix_g": gain(ks[2], (DEPTH, D_MODEL)),
        "norm_xattn_g": gain(ks[3], (DEPTH, D_MODEL)),
        "norm_mem_g": gain(ks[4], (DEPTH, D_MODEL)),
        "norm_ffn_g": gain(ks[5], (DEPTH, D_MODEL)),
        "w_in_ab": w(ks[6], (n_even, D_MODEL, ab_in_cols), D_MODEL),
        "ret_decay_fwd": base_logit[None] + small(ks[7], (n_even, N_RET_HEADS), 0.05),
        "ret_decay_bwd": base_logit[None] + small(ks[8], (n_even, N_RET_HEADS), 0.05),
        "ret_out_g": gain(ks[9], (n_even, HEAD_DIM)),
        "na_q_g": gain(ks[10], (n_even, HEAD_DIM)),
        "na_k_g": gain(ks[11], (n_even, HEAD_DIM)),
        "na_rpb": small(ks[12], (n_even, N_NA_HEADS, 2 * NA_WIN_ROWS - 1, 2 * NA_WIN_COLS - 1), 0.1),
        "w_out_ab": w(ks[13], (n_even, ab_width, D_MODEL), ab_width),
        "w_in_c": w(ks[14], (n_odd, D_MODEL, 3 * c_width), D_MODEL),
        "diff_q_g": gain(ks[15], (n_odd, HEAD_DIM)),
        "diff_k_g": gain(ks[16], (n_odd, HEAD_DIM)),
        "lambda_q1": small(ks[17], (n_odd, HEAD_DIM), 0.1),
        "lambda_k1": small(ks[18], (n_odd, HEAD_DIM), 0.1),
        "lambda_q2": small(ks[19], (n_odd, HEAD_DIM), 0.1),
        "lambda_k2": small(ks[20], (n_odd, HEAD_DIM), 0.1),
        "diff_out_g": gain(ks[21], (n_odd, 2 * HEAD_DIM)),
        "w_out_c": w(ks[22], (n_odd, c_width, D_MODEL), c_width),
        "w_xq": w(ks[23], (DEPTH, D_MODEL, x_width), D_MODEL),
        "w_xkv": w(ks[24], (DEPTH, D_MODEL, 2 * x_width), D_MODEL),
        "w_xo": w(ks[25], (DEPTH, x_width, D_MODEL), x_width),
        "xq_g": gain(ks[26], (DEPTH, X_HEAD_DIM)),
        "xk_g": gain(ks[27], (DEPTH, X_HEAD_DIM)),
        "w_ffn_in": w(ks[28], (DEPTH, D_MODEL, 2 * FFN_HIDDEN), D_MODEL),
        "w_ffn_out": w(ks[29], (DEPTH, FFN_HIDDEN, D_MODEL), FFN_HIDDEN),
    }

def second_block(x, mem, norm_mix_g, norm_xattn_g, norm_mem_g, norm_ffn_g,
              w_in_ab, ret_decay_fwd, ret_decay_bwd, ret_out_g, na_q_g, na_k_g, na_rpb, w_out_ab,
              w_in_c, diff_q_g, diff_k_g, lambda_q1, lambda_k1, lambda_q2, lambda_k2, diff_out_g, w_out_c,
              w_xq, w_xkv, w_xo, xq_g, xk_g, w_ffn_in, w_ffn_out):
    for i in range(DEPTH):
        j = i // 2
        h = rms_norm(x, norm_mix_g[i])
        if i % 2 == 0:
            x = x + retention_na_mixer(h, w_in_ab[j], ret_decay_fwd[j], ret_decay_bwd[j], ret_out_g[j],
                                       na_q_g[j], na_k_g[j], na_rpb[j], w_out_ab[j])
        else:
            x = x + diff_attention_mixer(h, w_in_c[j], diff_q_g[j], diff_k_g[j], lambda_q1[j], lambda_k1[j],
                                         lambda_q2[j], lambda_k2[j], diff_out_g[j], w_out_c[j], i)
        m = rms_norm(mem, norm_mem_g[i])
        x = x + memory_cross_attention(rms_norm(x, norm_xattn_g[i]), m, w_xq[i], w_xkv[i], w_xo[i], xq_g[i], xk_g[i])
        x = x + swiglu_ffn(rms_norm(x, norm_ffn_g[i]), w_ffn_in[i], w_ffn_out[i])
    return x


def setup_inputs(seed=0):
    out = dict(first_inputs(seed))
    for name, value in second_inputs(seed + 1).items():
        if name != "x":
            out[name + "_2"] = value
    return out


def reference(
    x, a_w_in, a_lam_re, a_lam_im, a_log_dt, a_b_re, a_b_im, a_c_re, a_c_im, a_d, a_w_glu,
    a_b_glu, a_w_out, kv_w, cmp_pos_k, cmp_w1_k, cmp_w2_k, cmp_pos_v, cmp_w1_v, cmp_w2_v,
    b_w_in, b_w_out, ln_g, ln_b, mem_2, norm_mix_g_2, norm_xattn_g_2, norm_mem_g_2,
    norm_ffn_g_2, w_in_ab_2, ret_decay_fwd_2, ret_decay_bwd_2, ret_out_g_2, na_q_g_2, na_k_g_2,
    na_rpb_2, w_out_ab_2, w_in_c_2, diff_q_g_2, diff_k_g_2, lambda_q1_2, lambda_k1_2,
    lambda_q2_2, lambda_k2_2, diff_out_g_2, w_out_c_2, w_xq_2, w_xkv_2, w_xo_2, xq_g_2, xk_g_2,
    w_ffn_in_2, w_ffn_out_2,
):
    x = first_block(
        x, a_w_in, a_lam_re, a_lam_im, a_log_dt, a_b_re, a_b_im, a_c_re, a_c_im, a_d, a_w_glu,
        a_b_glu, a_w_out, kv_w, cmp_pos_k, cmp_w1_k, cmp_w2_k, cmp_pos_v, cmp_w1_v, cmp_w2_v,
        b_w_in, b_w_out, ln_g, ln_b,
    )
    return second_block(
        x, mem_2, norm_mix_g_2, norm_xattn_g_2, norm_mem_g_2, norm_ffn_g_2, w_in_ab_2,
        ret_decay_fwd_2, ret_decay_bwd_2, ret_out_g_2, na_q_g_2, na_k_g_2, na_rpb_2, w_out_ab_2,
        w_in_c_2, diff_q_g_2, diff_k_g_2, lambda_q1_2, lambda_k1_2, lambda_q2_2, lambda_k2_2,
        diff_out_g_2, w_out_c_2, w_xq_2, w_xkv_2, w_xo_2, xq_g_2, xk_g_2, w_ffn_in_2,
        w_ffn_out_2,
    )


_drawn_inputs = setup_inputs


def setup_inputs(seed=0):
    import zlib

    import numpy as np

    out = dict(_drawn_inputs(seed))
    spreads = {}
    factors = {'a_lam_re': 64.0,
     'a_lam_im': 48.056,
     'a_log_dt': 50.376,
     'a_b_re': 64.0,
     'a_b_im': 64.0,
     'a_c_re': 64.0,
     'a_c_im': 64.0,
     'a_b_glu': 8.0,
     'cmp_pos_k': 8.0,
     'cmp_pos_v': 8.0,
     'norm_xattn_g_2': 8.0,
     'norm_mem_g_2': 8.0,
     'norm_ffn_g_2': 2.766,
     'ret_out_g_2': 5.851,
     'na_q_g_2': 8.0,
     'na_k_g_2': 8.0,
     'na_rpb_2': 3.428,
     'diff_q_g_2': 7.781,
     'diff_k_g_2': 5.177,
     'lambda_k2_2': 3.317,
     'diff_out_g_2': 5.717,
     'xq_g_2': 8.0,
     'xk_g_2': 8.0}
    for name, (base, spread) in spreads.items():
        noise = np.random.default_rng([zlib.crc32(name.encode()), seed]).standard_normal(out[name].shape)
        drawn = base * np.exp(spread * noise) if base else spread * noise
        out[name] = jnp.asarray(drawn.astype(out[name].dtype))
    for name, factor in factors.items():
        out[name] = (out[name] * factor).astype(out[name].dtype)
    return out
```

```python
import math
from contextlib import ExitStack, contextmanager

import numpy as np

import concourse.bass as bass
from concourse import mybir

F32 = mybir.dt.float32
ALU = mybir.AluOpType
ACT = mybir.ActivationFunctionType
AX_X = mybir.AxisListType.X

P = 128
D = 2048
T = 256
MT = T // P
FT = D // P
SLOTS = 4
SLOT = 4096
COLS = 512

SSM_TILES = 8
STATES = 64
GROUP = 16
NH = 16
DH = 128
KVH = 4
BLOCK, STRIDE = 32, 16
NCMP = (T - BLOCK) // STRIDE + 1
BRANCHES = 3
NGATE = BRANCHES * NH
H8 = 8
GRID = 64
ROWS = T // GRID
WIN_R, WIN_C = 8, 16
RPB_R, RPB_C = 2 * WIN_R - 1, 2 * WIN_C - 1
XH = 4
FFN = 5632
FFN_T = FFN // P
FFN_CH = FFN // COLS
DEPTH = 2
ALPHA = (2 * DEPTH) ** 0.25
LN_EPS, RMS_EPS = 1e-5, 1e-6
SCALE = DH ** -0.5
NEG = -1e30
LAM_INIT = 0.8 - 0.6 * math.exp(-0.3)
ROUND = 1.5 * 2.0 ** 23
TWO_PI = 2 * math.pi
PI2_A = 6.28125
PI2_B = float(np.float32(TWO_PI - PI2_A))
PI2_C = float(np.float32(TWO_PI - PI2_A - PI2_B))
TURN = float(np.nextafter(np.float32(TWO_PI), np.float32(0)))


@contextmanager
def rep(eng, n):
    if n == 1:
        yield 0
    else:
        with eng.Fori(0, n) as i:
            yield i


def peeled(eng, n, body):
    body(0)
    with eng.Fori(1, n) as i:
        body(i)


def wait_past(eng, sem, value):
    if not isinstance(value, int) or value > 0:
        eng.wait_ge(sem, value)


class Chain:

    def __init__(self, eng, sem):
        self.eng, self.sem, self.n = eng, sem, 0

    def add(self, ins):
        ins.then_inc(self.sem, 1)
        self.n += 1

    def settle(self):
        self.eng.wait_ge(self.sem, self.n)


class Dense:

    def __init__(self, plan, src, kt, blocks, chunks, style, act, cols=COLS, iters=1):
        self.src, self.kt, self.blocks, self.style, self.act = src, kt, blocks, style, act
        self.cols, self.iters, self.body = cols, iters, chunks // iters
        self.block0, self.chunk0 = plan["blocks"], plan["chunks"]
        plan["blocks"] += chunks * blocks
        plan["chunks"] += chunks
        self.end = plan["chunks"]
        assert iters == 1 or (self.body * blocks % SLOTS == 0 and self.body % 2 == 0)

    def slot(self, c, b):
        return (self.block0 + c * self.blocks + b) % SLOTS

    def pair(self, c):
        return (self.chunk0 + c) % 2

    def blocks_before(self, i, c, b):
        return i * (self.body * self.blocks) + (self.block0 + c * self.blocks + b)

    def pair_uses(self, i, c):
        return i * (self.body // 2) + (self.chunk0 + c) // 2


def program(nc, a, out):
    ctx = ExitStack()
    with ctx:
        def sb(name, *shape):
            return ctx.enter_context(nc.sbuf_tensor(name, list(shape), F32))

        def ps(name, *shape):
            return ctx.enter_context(nc.psum_tensor(name, list(shape), F32))

        def sem(name):
            return ctx.enter_context(nc.semaphore(name))

        ring = sb("ring", P, SLOTS, SLOT)
        xtok = sb("xtok", P, MT, D)
        actT = sb("actT", P, FT, T)
        arena = sb("arena", P, 18944)
        mem_kT = sb("mem_kT", P, DEPTH, XH, T)
        mem_v = sb("mem_v", P, DEPTH, MT, XH * DH)
        score = sb("score", P, 2, 512)
        probT = sb("probT", P, 2, 512)
        ident = sb("ident", P, P)
        flip = sb("flip", P, P)
        mean_of = sb("mean_of", P, P)
        causal = sb("causal", P, MT, T)
        earlier = sb("earlier", P, MT, T)
        later = causal
        time_row = earlier[:, 0, :]
        ssm = causal[:, :, :].rearrange("p m t -> p (m t)").rearrange("p (k j) -> p k j", j=32)
        cmp_mask = sb("cmp_mask", P, MT, NCMP)
        row_ok = sb("row_ok", P, MT)
        group_mask = sb("group_mask", P, 2, 8)
        col_mask = sb("col_mask", P, GRID)
        ldt2 = sb("ldt2", 96, 2)
        colsA = sb("colsA", P, P)
        colsB = sb("colsB", P, P)
        colsC = sb("colsC", P, 64)
        consts = sb("consts", P, 4)
        decay = sb("decay", P, 4, 16)
        lam = sb("lam", P, 8)
        gates = sb("gates", P, MT, NGATE)
        w2 = sb("w2", P, 2, P)
        cmp_hid = sb("cmp_hid", P, 2, KVH * NCMP)
        cmp_bias = sb("cmp_bias", P, 2)
        kcmpT = sb("kcmpT", P, KVH, NCMP)
        vcmp = sb("vcmp", NCMP, KVH, DH)
        rpb_pad = sb("rpb_pad", H8 * RPB_R, P)
        stats = sb("stats", P, MT, 24)
        moments = sb("moments", P, MT, 2)
        mean_sq = sb("mean_sq", P, MT)
        root = sb("root", P, MT)
        rstd = sb("rstd", P, MT)
        neg_max = sb("neg_max", P, 2, MT)
        denom = sb("denom", P, 2, MT)
        factor = sb("factor", P, 2, MT)
        rpb_dram = nc.dram_tensor("rpb_scratch", [H8 * RPB_R, P], F32, kind="Internal").ap()

        acc = ps("acc", P, 4, 512)
        psA = ps("psA", P, 2, 512)
        psB = ps("psB", P, 512)
        psC = ps("psC", P, 512)
        turn_banks = [psA[:, 0, :], psA[:, 1, :], psB[:, :], psC[:, :]]

        def area(at, *shape):
            n = int(np.prod(shape))
            v = arena[:, at:at + n]
            if len(shape) == 2:
                return v.rearrange("p (a b) -> p a b", a=shape[0])
            if len(shape) == 3:
                return v.rearrange("p (a b c) -> p a b c", a=shape[0], b=shape[1])
            return v

        HS = 14848
        hs = area(HS, MT, D)
        rowsA, rowsB, rowsC = area(8192, P), area(8320, P), area(8448, P)[0:64, :]
        memT = [area(0, FT, T), area(4096, FT, T)]
        uT, zT5, gT, yT5 = (area(2048 * k, 8, T) for k in range(4))
        s5_sin, s5_cos, s5_frac, s5_t1, s5_t2, s5_gr, s5_gi, BT = (
            area(8192 + 1024 * k, 4, T) for k in range(8))
        BT = area(8192 + 1024 * 7, 8, P)
        CT = area(8192 + 1024 * 8, 8, P)
        s5_hr = actT[:, 0:4, :]
        s5_hi = actT[:, 4:8, :]
        ZB = actT[:, 8:12, :].rearrange("p a b -> p (a b)").rearrange("p (z s) -> p z s", s=P)
        ZC = actT[:, 12:16, :].rearrange("p a b -> p (a b)").rearrange("p (z s) -> p z s", s=P)
        b_raw = area(17408, 2, 512)
        bbar = score
        c_raw = probT
        kcT = area(0, KVH + 1, T)
        vcT = area(1280, KVH + 1, T)
        ksT = area(2560, KVH, T)
        kwT = area(3584, KVH, T)
        v_slc = area(4608, MT, 512)
        v_win = area(5632, MT, 512)
        qT = area(6656, NH, T)
        zT = area(10752, NH, T)
        gate_w = area(10752, FT, NGATE)
        oT = area(14848, NH, T)
        rqT, rkT, rgT, nqT, nkT = (area(2048 * k, H8, T) for k in range(5))
        rv = area(10240, MT, H8 * DH)
        nv = area(12288, MT, H8 * DH)
        table = area(14336, H8, 2 * T)
        dqT, dkT = area(0, NH, T), area(4096, NH, T)
        dv = area(8192, MT, D)
        doT = area(12288, NH, T)
        xqT = area(0, XH, T)
        xoT = area(1024, XH, T)
        hidT = area(0, FFN_T, T)
        silu_g = area(11264, 4, T)

        A_RE, A_IM, A_DT, A_D, A_BGLU = 0, 32, 64, 96, 104
        (C_RET, C_NAQ, C_NAK, C_DQ, C_DK, C_DO, C_XQ, C_XK, C_LAM) = (
            112, 113, 114, 115, 116, 117, 119, 121, 123)
        G_MIX, G_X, G_MEM, G_FFN = 0, 32, 64, 96

        landed = [sem(f"weights_landed_{s}") for s in range(SLOTS)]
        blocks_done = sem("weight_blocks_done")
        drained = [sem(f"chunks_drained_{p}") for p in range(2)]
        x_landed, mem_landed, consts_landed = sem("x_landed"), sem("mem_landed"), sem("consts_landed")
        ldt_landed, b_landed, ln_landed = sem("ldt_landed"), sem("b_landed"), sem("ln_landed")
        pad_landed, pad_stored, bias_landed = sem("pad_landed"), sem("pad_stored"), sem("bias_landed")
        masks_made, causal_made, lags_made = sem("masks_made"), sem("causal_made"), sem("lags_made")
        ident_made = sem("ident_made")
        pool_step, dve_step, act_step = sem("pool_step"), sem("dve_step"), sem("act_step")
        cols_turned, cols_copied = sem("cols_turned"), sem("cols_copied")
        ms_ready, root_ready, rstd_ready = sem("mean_square_ready"), sem("root_ready"), sem("rstd_ready")
        scaled = sem("rows_scaled")
        ln_done = sem("layer_norm_done")
        turned = sem("tiles_turned")
        turned_dve, turned_act = sem("turned_tiles_drained_by_vector"), sem("turned_tiles_drained_by_scalar")
        sq_ready, mean_ready, hroot_ready, normed = (
            sem("squares_ready"), sem("head_mean_ready"), sem("head_root_ready"), sem("heads_normed"))
        scores_ready, biased, max_ready, exp_ready = (
            sem("scores_ready"), sem("scores_biased"), sem("max_ready"), sem("exp_ready"))
        probs_ready, probs_turned, probT_ready, o_ready, o_used = (
            sem("probs_ready"), sem("probs_turned"), sem("probT_ready"), sem("o_ready"), sem("o_used"))
        branch_summed = sem("branch_summed")
        s5_dt, s5_exp, s5_frac0, s5_trig0 = sem("s5_dt"), sem("s5_theta"), sem("s5_frac0"), sem("s5_trig0")
        z_written, z_turned, z_copied = sem("s5_z_written"), sem("s5_z_turned"), sem("s5_z_copied")
        phase_ready, trig_ready, bu_ready, bu_read = (
            sem("s5_phase_ready"), sem("s5_trig_ready"), sem("s5_bu_ready"), sem("s5_bu_read"))
        h_ready, y_ready, y_summed, gelu_done, glu_mixed = (
            sem("s5_h_ready"), sem("s5_y_ready"), sem("s5_y_summed"), sem("s5_gelu_done"), sem("s5_glu_mixed"))
        pos_ready, cmp_sum, cmp_bias_ready, cmp_hid_ready, cmp_out, cmp_ready = (
            sem("pos_ready"), sem("cmp_sum"), sem("cmp_bias_ready"), sem("cmp_hid_ready"), sem("cmp_out"),
            sem("cmp_ready"))
        gate_w_landed = sem("gate_w_landed")
        gate_sum, gate_ready = sem("gate_sum"), sem("gate_ready")
        lg_abs, lg_ln, lg_ready, lam_prod, lam_sum, lam_exp, lam_ready = (
            sem("lg_abs"), sem("lg_ln"), sem("lg_ready"), sem("lam_prod"), sem("lam_sum"), sem("lam_exp"),
            sem("lam_ready"))
        decay_arg, decay_ready = sem("decay_arg"), sem("decay_ready")
        rs_ready, rs_decayed, ro_ready, ro_copied, gated = (
            sem("ret_scores_ready"), sem("ret_scores_decayed"), sem("ret_o_ready"), sem("ret_o_copied"),
            sem("ret_gated"))
        bias_turned, bias_masked = sem("na_bias_turned"), sem("na_bias_masked")
        out_done = sem("out_done")

        plan = {"blocks": 0, "chunks": 0}

        def columns(w, kt, cols=COLS):
            v = w.rearrange("(t p) n -> p t n", p=P)
            return lambda j, b: v[:, b * kt:(b + 1) * kt, bass.ts(j, cols)]

        def plain(w, kt, cols=COLS, first=0, body=None):
            at = columns(w, kt, cols)
            return lambda i, c, b: at(i * (body or 0) + (first + c), b)

        def tiles(v):
            return lambda k: v[:, k, :]

        kv_mem = []
        for l in range(DEPTH):
            kv_mem.append((
                Dense(plan, plain(a["w_xkv_2"][l], 8), 8, 2, 1, "feat", tiles(memT[l])),
                Dense(plan, plain(a["w_xkv_2"][l], 8, first=1), 8, 2, 1, "tok", tiles(memT[l]))))
        s5_in = Dense(plan, plain(a["a_w_in"][0], 8, body=2), 8, 2, 4, "feat", tiles(actT), iters=2)
        s5_glu = Dense(plan, plain(a["a_w_glu"][0], 8), 8, 1, 2, "feat", tiles(gT))
        s5_out = Dense(plan, plain(a["a_w_out"][0], 8), 8, 1, 4, "tok", tiles(yT5))
        kv = [Dense(plan, plain(a["kv_w"], 8, first=k), 8, 2, 1, style, tiles(actT))
              for k, style in enumerate(["feat", "feat", "feat", "tok", "feat", "tok"])]
        cmp_w1 = [Dense(plan, None, BLOCK, 1, 1, "cmp", None) for _ in range(2)]
        b_q = Dense(plan, plain(a["b_w_in"][0], 8, body=2), 8, 2, 4, "feat", tiles(actT), iters=2)
        b_z = [Dense(plan, plain(a["b_w_in"][0], 8, first=4 * (r + 1), body=2), 8, 2, 4, "feat",
                     tiles(actT), iters=2) for r in range(BRANCHES)]
        b_out = Dense(plan, plain(a["b_w_out"][0], 8, body=2), 8, 2, 4, "tok", tiles(oT), iters=2)

        w_ab = a["w_in_ab_2"][0]

        def ab(first, style, chunks=2):
            return Dense(plan, plain(w_ab, 8, first=first), 8, 2, chunks, style, tiles(actT))

        ab_rq, ab_rk, ab_rv, ab_rg = ab(0, "feat"), ab(2, "feat"), ab(4, "tok"), ab(6, "feat")
        ab_nq, ab_nk, ab_nv = ab(8, "feat"), ab(10, "feat"), ab(12, "tok")
        layers = []

        def tail(l):
            xq = Dense(plan, plain(a["w_xq_2"][l], 8), 8, 2, 1, "feat", tiles(actT))
            xo = Dense(plan, plain(a["w_xo_2"][l], 4), 4, 1, 4, "tok", tiles(xoT))
            w = columns(a["w_ffn_in_2"][l], 8)
            ffn_in = Dense(plan, lambda i, c, b: w(i + c * FFN_CH, b), 8, 2, 2 * FFN_CH, "feat",
                           tiles(actT), iters=FFN_CH)
            ffn_out = Dense(plan, plain(a["w_ffn_out_2"][l], 11, 256, body=2), 11, 4, 8, "tok",
                            tiles(hidT), cols=256, iters=4)
            return xq, xo, ffn_in, ffn_out

        ab_out = Dense(plan, plain(a["w_out_ab_2"][0], 8, body=2), 8, 2, 4, "tok",
                       lambda k: rgT[:, k, :] if k < H8 else rkT[:, k - H8, :], iters=2)
        layers.append(tail(0))
        c_qk = Dense(plan, plain(a["w_in_c_2"][0], 8, body=2), 8, 2, 8, "feat", tiles(actT), iters=4)
        c_v = Dense(plan, plain(a["w_in_c_2"][0], 8, first=8, body=2), 8, 2, 4, "tok", tiles(actT), iters=2)
        c_out = Dense(plan, plain(a["w_out_c_2"][0], 8, body=2), 8, 2, 4, "tok", tiles(doT), iters=2)
        layers.append(tail(1))

        def attn(q, k, K, v, mode, bias=None, gate=None, first=True, last=True, halves=1, **more):
            return dict(q=q, k=k, K=K, v=v, mode=mode, bias=bias, gate=gate, first=first, last=last,
                        halves=halves, **more)

        nsa = []
        for r in range(BRANCHES):
            nsa.append([])
            for h in range(NH):
                g = h // (NH // KVH)
                gate = gates[:, :, r * NH + h:r * NH + h + 1].rearrange("p m o -> p (m o)")
                if r == 0:
                    u = attn(qT[:, h, :], kcmpT[:, g, :], NCMP, lambda t, o, g=g: vcmp[:, g, :], "bias",
                             cmp_mask[:, :, :], gate)
                else:
                    kk, vv = ((ksT, v_slc), (kwT, v_win))[r - 1]
                    u = attn(qT[:, h, :], kk[:, g, :], T,
                             lambda t, o, g=g, vv=vv: vv[:, t, g * DH:(g + 1) * DH], "bias",
                             causal[:, :, :], gate)
                u.update(fin="gate", r=r, h=h)
                nsa[r].append(u)
        na = [attn(nqT[:, h, :], nkT[:, h, :], T, lambda t, o, h=h: nv[:, t, h * DH:(h + 1) * DH], "bias",
                   table[:, h, :].rearrange("p (q k) -> p q k", q=MT), fin="copy", to=rkT[:, h, :])
              for h in range(H8)]
        xat = [[attn(xqT[:, h, :], mem_kT[:, l, h, :], T,
                     lambda t, o, h=h, l=l: mem_v[:, l, t, h * DH:(h + 1) * DH], "plain",
                     fin="copy", to=xoT[:, h, :]) for h in range(XH)] for l in range(DEPTH)]
        dif = [attn(dqT[:, 2 * h + c, :], dkT[:, 2 * h + c, :], T,
                    lambda t, o, h=h: dv[:, t, h * T + o * DH:h * T + (o + 1) * DH], "alibi",
                    bias=2.0 ** (-8.0 * (h + 1) / H8), gate=lam[:, 7:8].to_broadcast([P, MT]) if c else None,
                    first=c == 0, last=c == 1, halves=2, fin="copy", to=doT[:, 2 * h:2 * h + 2, :])
               for h in range(H8) for c in range(2)]
        groups = units = 0
        for part in (nsa[0], nsa[1], nsa[2], na, xat[0], dif, xat[1]):
            for u in part:
                u["n"], u["group"] = units, groups
                units += 1
                groups += u["last"]

        def pairs(v, n, g):
            return [dict(x=v[:, k:k + 2, :], g=[g, g], wide=False) for k in range(0, n, 2)]

        norm_mem = [u for l in range(DEPTH) for u in pairs(mem_kT[:, l], XH, C_XK + l)]
        norm_ab = pairs(rqT, H8, C_RET) + pairs(nqT, H8, C_NAQ) + pairs(nkT, H8, C_NAK)
        norm_x = [pairs(xqT, XH, C_XQ + l) for l in range(DEPTH)]
        norm_c = pairs(dqT, NH, C_DQ) + pairs(dkT, NH, C_DK)
        norm_do = [dict(x=doT[:, k:k + 2, :], g=[C_DO, C_DO + 1], wide=True) for k in range(0, NH, 2)]
        n = 0
        for part in (norm_mem, norm_ab, norm_x[0], norm_c, norm_do, norm_x[1]):
            for u in part:
                u["n"] = n
                n += 1

        TURN_MEM, TURN_X, TURN_LN1, TURN_MIX, TURN_XA, TURN_FFN = (0, 1), 2, 3, (4, 7), (5, 8), (6, 9)
        RMS_MEM, LN1, LN2, RMS_MIX, RMS_XA, RMS_FFN = 0, 1, 2, (3, 6), (4, 7), (5, 8)
        SCALED = {RMS_MEM: 1, RMS_MIX[0]: 2, RMS_XA[0]: 3, RMS_FFN[0]: 4, RMS_MIX[1]: 5, RMS_XA[1]: 6,
                  RMS_FFN[1]: 7}
        IN_FLIGHT = len(turn_banks)

        def await_chunks(eng, ph):
            for last in (ph.end - 2, ph.end - 1):
                eng.wait_ge(drained[last % 2], last // 2 + 1)

        def await_turn(eng, call):
            eng.wait_ge(turned_dve, 8 * (call + 1))
            eng.wait_ge(turned_act, 8 * (call + 1))

        def drain(eng, ph, fn, only=None):
            with rep(eng, ph.iters) as i:
                for c in range(ph.body):
                    if only is None or c in only:
                        eng.wait_ge(blocks_done, ph.blocks_before(i, c, ph.blocks))
                        src = acc[:, 2 * ph.pair(c):2 * ph.pair(c) + 2, 0:ph.cols]
                        fn(i, c, src).then_inc(drained[ph.pair(c)], 1)

        def feat_src(src):
            return src.rearrange("p a (b t) -> p (a b) t", t=T)

        block = ctx.enter_context(nc.Block())

        @block.sync
        def _(sp):
            sp.dma_start(hs, a["mem_2"][0].rearrange("(m p) d -> p m d", p=P)).then_inc(mem_landed, 16)
            sp.dma_start(xtok[:, :, :], a["x"][0].rearrange("(m p) d -> p m d", p=P)).then_inc(x_landed, 16)

            def stream(ph):
                with rep(sp, ph.iters) as i:
                    for c in range(ph.body):
                        for b in range(ph.blocks):
                            s = ph.slot(c, b)
                            if ph.block0 + c * ph.blocks + b >= SLOTS:
                                sp.wait_ge(blocks_done, ph.blocks_before(i, c, b) - (SLOTS - 1))
                            dst = ring[:, s, 0:ph.kt * ph.cols].rearrange("p (t n) -> p t n", t=ph.kt)
                            sp.dma_start(dst, ph.src(i, c, b)).then_inc(landed[s], 16)

            def stream_w1(ph, w):
                s = ph.slot(0, 0)
                sp.wait_ge(blocks_done, ph.block0 - (SLOTS - 1))
                sp.dma_start(ring[:, s, :].rearrange("p (j n) -> p j n", j=BLOCK),
                             w.rearrange("(j p) n -> p j n", p=P)).then_inc(landed[s], 16)

            for l in range(DEPTH):
                for ph in kv_mem[l]:
                    stream(ph)
            for ph in (s5_in, s5_glu, s5_out, *kv):
                stream(ph)
            stream_w1(cmp_w1[0], a["cmp_w1_k"])
            stream_w1(cmp_w1[1], a["cmp_w1_v"])
            for ph in (b_q, *b_z, b_out, ab_rq, ab_rk, ab_rv, ab_rg, ab_nq, ab_nk, ab_nv, ab_out, *layers[0],
                       c_qk, c_v, c_out, *layers[1]):
                stream(ph)
            await_chunks(sp, layers[1][3])
            sp.dma_start(out[0].rearrange("(m p) d -> p m d", p=P), xtok[:, :, :]).then_inc(out_done, 16)
            sp.wait_ge(out_done, 16)

        @block.gpsimd
        def _(pool):
            chain = Chain(pool, pool_step)

            rows = [
                (rowsA[A_RE:A_RE + 32, :], a["a_lam_re"][0].rearrange("(j h) p -> j (h p)", h=2)),
                (rowsA[A_IM:A_IM + 32, :], a["a_lam_im"][0].rearrange("(j h) p -> j (h p)", h=2)),
                (rowsA[A_D:A_D + 8, :], a["a_d"][0].rearrange("(j p) -> j p", p=P)),
                (rowsA[A_BGLU:A_BGLU + 8, :], a["a_b_glu"][0].rearrange("(j p) -> j p", p=P)),
                (rowsA[C_RET:C_RET + 1, :], a["ret_out_g_2"]),
                (rowsA[C_NAQ:C_NAQ + 1, :], a["na_q_g_2"]),
                (rowsA[C_NAK:C_NAK + 1, :], a["na_k_g_2"]),
                (rowsA[C_DQ:C_DQ + 1, :], a["diff_q_g_2"]),
                (rowsA[C_DK:C_DK + 1, :], a["diff_k_g_2"]),
                (rowsA[C_DO:C_DO + 2, :], a["diff_out_g_2"][0].rearrange("(j p) -> j p", p=P)),
                (rowsA[C_XQ:C_XQ + 2, :], a["xq_g_2"]),
                (rowsA[C_XK:C_XK + 2, :], a["xk_g_2"]),
                (rowsA[C_LAM:C_LAM + 1, :], a["lambda_q1_2"]),
                (rowsA[C_LAM + 1:C_LAM + 2, :], a["lambda_k1_2"]),
                (rowsA[C_LAM + 2:C_LAM + 3, :], a["lambda_q2_2"]),
                (rowsA[C_LAM + 3:C_LAM + 4, :], a["lambda_k2_2"]),
                (rowsA[C_LAM + 4:C_LAM + 5, :], a["lambda_k2_2"]),
                (rowsC[0:BLOCK, :], a["cmp_pos_k"]),
                (rowsC[BLOCK:2 * BLOCK, :], a["cmp_pos_v"]),
                (w2[:, 0, :], a["cmp_w2_k"]),
                (w2[:, 1, :], a["cmp_w2_v"]),
                (decay[:, 0, 0:8], a["ret_decay_fwd_2"].partition_broadcast(P).rearrange("p o h -> p (o h)")),
                (decay[:, 0, 8:16], a["ret_decay_bwd_2"].partition_broadcast(P).rearrange("p o h -> p (o h)")),
            ]
            for k, name in enumerate(("norm_mix_g_2", "norm_xattn_g_2", "norm_mem_g_2", "norm_ffn_g_2")):
                rows.append((rowsB[32 * k:32 * k + 32, :], a[name].rearrange("l (j p) -> (l j) p", p=P)))
            pool.dma_start(ldt2[64:96, :], a["a_log_dt"][0].rearrange("(j h) -> j h", h=2)).then_inc(ldt_landed, 16)
            for dst, src in rows:
                pool.dma_start(dst, src).then_inc(consts_landed, 16)
            assert len(rows) == N_CONST

            for ap, value in ((ident[:, :], 0.0), (flip[:, :], 0.0), (mean_of[:, :], 1.0 / P), (consts[:, 0:1], RMS_EPS),
                              (consts[:, 1:2], LN_EPS), (consts[:, 2:3], math.pi / 2), (consts[:, 3:4], 1.0),
                              (cmp_mask[:, :, :], 0.0), (row_ok[:, :], 1.0),
                              (col_mask[:, :], 0.0), (group_mask[:, 0, :], 1.0), (group_mask[:, 1, :], -1.0),
                              (rpb_pad[:, :], 0.0)):
                chain.add(pool.memset(ap, value))
            chain.settle()
            pool.affine_select(out=ident[:, :], in_=ident[:, :], compare_op=ALU.not_equal, fill=1.0, base=0,
                               pattern=[[-1, P]], channel_multiplier=1).then_inc(ident_made, 1)
            for at in (GRID - 1, 3 * GRID - 1):
                chain.add(pool.affine_select(out=flip[:, :], in_=flip[:, :], compare_op=ALU.not_equal, fill=1.0,
                                             base=-at, pattern=[[1, P]], channel_multiplier=1))
                chain.settle()
            pool.dma_start(rpb_pad[:, GRID - WIN_C:GRID - WIN_C + RPB_C],
                           a["na_rpb_2"][0].rearrange("h r c -> (h r) c")).then_inc(pad_landed, 16)
            chain.add(pool.affine_select(out=cmp_mask[:, :, :], in_=cmp_mask[:, :, :], compare_op=ALU.is_ge,
                                         fill=NEG, base=-(BLOCK - 1), pattern=[[P, MT], [-STRIDE, NCMP]],
                                         channel_multiplier=1))
            chain.add(pool.affine_select(out=row_ok[:, :], in_=row_ok[:, :], compare_op=ALU.is_ge, fill=0.0,
                                         base=-(BLOCK - 1), pattern=[[P, MT]], channel_multiplier=1))
            for s in range(2):
                chain.add(pool.affine_select(out=group_mask[:, s, :], in_=group_mask[:, s, :],
                                             compare_op=ALU.is_ge, fill=0.0, base=0, pattern=[[-GROUP, 8]],
                                             channel_multiplier=1))
            chain.settle()
            for s in range(2):
                chain.add(pool.affine_select(out=group_mask[:, s, :], in_=group_mask[:, s, :],
                                             compare_op=ALU.is_ge, fill=0.0, base=GROUP - 1,
                                             pattern=[[GROUP, 8]], channel_multiplier=-1))
            chain.settle()
            edge = GRID - WIN_C
            for q in range(2):
                m = col_mask[GRID * q:GRID * (q + 1), :]
                chain.add(pool.affine_select(out=m[:, 0:edge], in_=m[:, 0:edge], compare_op=ALU.is_ge, fill=NEG,
                                             base=WIN_C // 2, pattern=[[1, edge]], channel_multiplier=-1))
                chain.settle()
            for q in range(2):
                m = col_mask[GRID * q:GRID * (q + 1), WIN_C:GRID]
                chain.add(pool.affine_select(out=m, in_=m, compare_op=ALU.is_ge, fill=NEG,
                                             base=WIN_C // 2 - 1 - WIN_C, pattern=[[-1, edge]],
                                             channel_multiplier=1))
                chain.settle()
            chain.add(pool.iota(time_row, [[1, T]], base=0, channel_multiplier=0,
                                allow_small_or_imprecise_dtypes=True))
            chain.settle()
            pool.engine_nop().then_inc(masks_made, 1)
            pool.wait_ge(pad_landed, 16)
            pool.dma_start(rpb_dram, rpb_pad[:, :]).then_inc(pad_stored, 16)

            await_chunks(pool, kv_mem[1][1])
            pool.wait_ge(normed, len(norm_mem))
            for k, name in enumerate(("a_b_re", "a_b_im")):
                pool.dma_start(b_raw[:, k, :].rearrange("p (j c) -> p j c", c=GROUP),
                               a[name][0].rearrange("(j h) q c -> (h q) j c", h=2)).then_inc(b_landed, 16)
            for k, name in enumerate(("a_c_re", "a_c_im")):
                pool.dma_start(c_raw[:, k, :].rearrange("p (f q) -> p f q", q=STATES),
                               a[name][0].rearrange("(f g) c q -> (g c) f q", f=8)).then_inc(b_landed, 16)

            def load_ln(l):
                for k, name in enumerate(("ln_g", "ln_b")):
                    pool.dma_start(actT[:, 8 * k:8 * k + 8, :].rearrange("p a b -> p (a b)"),
                                   a[name][l:l + 1, :].partition_broadcast(P).rearrange("p o d -> p (o d)"))\
                        .then_inc(ln_landed, 16)

            pool.wait_ge(y_summed, SSM_TILES)
            chain.add(pool.memset(causal[:, :, :], 0.0))
            chain.settle()
            pool.affine_select(out=causal[:, :, :], in_=causal[:, :, :], compare_op=ALU.is_ge, fill=NEG, base=0,
                               pattern=[[P, MT], [-1, T]], channel_multiplier=1).then_inc(causal_made, 1)
            load_ln(0)
            await_chunks(pool, s5_out)
            pool.dma_start(gate_w, a["b_w_in"][0, :, NH * DH * (1 + BRANCHES):].rearrange(
                "(t p) n -> p t n", p=P)).then_inc(gate_w_landed, 16)

            for r in range(1, BRANCHES):
                for h in range(NH):
                    pool.wait_ge(o_used, nsa[r][h]["group"] + 1)
                    pool.tensor_tensor(oT[:, h, :], oT[:, h, :], zT[:, h, :], ALU.add).then_inc(branch_summed, 1)
            chain.add(pool.iota(later[:, :, :], [[-P, MT], [1, T]], base=0, channel_multiplier=-1,
                                allow_small_or_imprecise_dtypes=True))
            chain.settle()
            chain.add(pool.tensor_scalar(earlier[:, :, :], later[:, :, :], -1.0, 0.0, ALU.mult, ALU.max))
            chain.settle()
            pool.tensor_scalar(later[:, :, :], later[:, :, :], 0.0, None, ALU.max).then_inc(lags_made, 1)
            await_chunks(pool, b_z[2])
            load_ln(1)

            pool.wait_ge(pad_stored, 16)
            pool.wait_ge(ro_copied, H8)
            for r in range(ROWS):
                for h in range(H8):
                    src = bass.AP(tensor=rpb_dram.tensor,
                                  offset=(h * RPB_R + WIN_R - 1 - r) * P,
                                  ap=[[1, GRID], [P, ROWS], [1, GRID]])
                    q = r % 2
                    dst = table[GRID * q:GRID * (q + 1), h, (r // 2) * T:(r // 2 + 1) * T]
                    pool.dma_start(dst.rearrange("p (r c) -> p r c", c=GRID), src).then_inc(bias_landed, 16)

        @block.tensor
        def _(pe):
            def turn(call, src):
                for k in range(FT // 2):
                    n = 8 * call + k
                    if n >= IN_FLIGHT:
                        pe.wait_ge((turned_dve, turned_act)[n % 2], 2 * ((n - IN_FLIGHT) // 2 + 1))
                    bank = turn_banks[n % IN_FLIGHT]
                    for f in range(2):
                        for m in range(MT):
                            ins = pe.transpose(bank[:, (f * MT + m) * P:(f * MT + m + 1) * P],
                                               src[:, m, (2 * k + f) * P:(2 * k + f + 1) * P], ident[:, :])
                    ins.then_inc(turned, 1)

            def dense(ph):
                with rep(pe, ph.iters) as i:
                    for c in range(ph.body):
                        if ph.chunk0 + c >= 2:
                            pe.wait_ge(drained[ph.pair(c)], ph.pair_uses(i, c))
                        pair = acc[:, 2 * ph.pair(c):2 * ph.pair(c) + 2, :]
                        w = [ring[:, ph.slot(c, b), 0:ph.kt * ph.cols].rearrange("p (t n) -> p t n", t=ph.kt)
                             for b in range(ph.blocks)]

                        def arrived(b):
                            j = ph.block0 + c * ph.blocks + b
                            pe.wait_ge(landed[ph.slot(c, b)],
                                       i * (16 * ph.body * ph.blocks // SLOTS) + 16 * (j // SLOTS + 1))

                        last_k = ph.blocks * ph.kt - 1
                        if ph.style == "tok":
                            for b in range(ph.blocks):
                                arrived(b)
                                for t in range(ph.kt):
                                    k = b * ph.kt + t
                                    for m in range(MT):
                                        ins = pe.matmul(pair[:, m, 0:ph.cols], ph.act(k)[:, m * P:(m + 1) * P],
                                                        w[b][:, t, :], start=k == 0, stop=k == last_k)
                                ins.then_inc(blocks_done, 1)
                        else:
                            for f in range(COLS // P):
                                for b in range(ph.blocks):
                                    if f == 0:
                                        arrived(b)
                                    for t in range(ph.kt):
                                        k = b * ph.kt + t
                                        ins = pe.matmul(pair[:, f // 2, (f % 2) * T:(f % 2 + 1) * T],
                                                        w[b][:, t, f * P:(f + 1) * P], ph.act(k),
                                                        start=k == 0, stop=k == last_k)
                                    if f == COLS // P - 1:
                                        ins.then_inc(blocks_done, 1)

            def head_means(part):
                for u in part:
                    n = u["n"]
                    pe.wait_ge(sq_ready, n + 1)
                    if n >= 2:
                        pe.wait_ge(hroot_ready, n - 1)
                    sq = score[:, n % 2, :]
                    if u["wide"]:
                        pe.matmul(psA[:, n % 2, 0:T], mean_of[:, :], sq[:, 0:T], start=True, stop=False)
                        ins = pe.matmul(psA[:, n % 2, 0:T], mean_of[:, :], sq[:, T:2 * T], start=False, stop=True)
                    else:
                        ins = pe.matmul(psA[:, n % 2, :], mean_of[:, :], sq, start=True, stop=True)
                    ins.then_inc(mean_ready, 1)

            def attend(part):
                for t in range(len(part) + 2):
                    if t < len(part):
                        u = part[t]
                        n = u["n"]
                        if n >= 2:
                            pe.wait_ge(biased, n - 1)
                        for m in range(MT):
                            ins = pe.matmul(psA[:, n % 2, m * T:m * T + u["K"]], u["q"][:, m * P:(m + 1) * P],
                                            u["k"], start=True, stop=True)
                        ins.then_inc(scores_ready, 1)
                    if 0 <= t - 1 < len(part):
                        u = part[t - 1]
                        n, K = u["n"], u["K"]
                        pe.wait_ge(probs_ready, n + 1)
                        if n >= 1:
                            pe.wait_ge(probT_ready, n)
                        for m in range(MT):
                            for kt in range(-(-K // P)):
                                w = min(P, K - kt * P)
                                ins = pe.transpose(psB[0:w, kt * T + m * P:kt * T + (m + 1) * P],
                                                   score[:, n % 2, m * T + kt * P:m * T + kt * P + w],
                                                   ident[:, :])
                        ins.then_inc(probs_turned, 1)
                    if 0 <= t - 2 < len(part):
                        u = part[t - 2]
                        n, K = u["n"], u["K"]
                        pe.wait_ge(probT_ready, n + 1)
                        if u["first"] and u["group"] >= 1:
                            pe.wait_ge(o_used, u["group"])
                        kts = -(-K // P)
                        for o in range(u["halves"]):
                            for kt in range(kts):
                                w = min(P, K - kt * P)
                                ins = pe.matmul(psC[:, o * T:(o + 1) * T], u["v"](kt, o),
                                                probT[0:w, n % 2, kt * T:(kt + 1) * T],
                                                start=u["first"] and kt == 0 and o == 0,
                                                stop=u["last"] and kt == kts - 1,
                                                skip_group_check=u["halves"] == 2)
                        ins.then_inc(o_ready, 1)

            pe.wait_ge(ident_made, 1)
            pe.wait_ge(consts_landed, 16 * N_CONST)
            pe.wait_ge(s5_dt, 1)
            pe.transpose(psA[:, 0, 0:P], rowsA[:, :], ident[:, :])
            pe.transpose(psA[:, 1, 0:P], rowsB[:, :], ident[:, :])
            pe.transpose(psB[:, 0:64], rowsC[:, :], ident[0:64, 0:64]).then_inc(cols_turned, 1)
            pe.wait_ge(lam_prod, 1)
            pe.wait_ge(masks_made, 1)
            pe.matmul(psC[:, 0:2], mean_of[:, :], lam[:, 0:2], start=True, stop=True).then_inc(lam_sum, 1)

            pe.wait_ge(cols_copied, 3)
            pe.wait_ge(lam_exp, 1)
            pe.wait_ge(scaled, 2 * SCALED[RMS_MEM])
            for l in range(DEPTH):
                turn(TURN_MEM[l], hs)
            pe.wait_ge(x_landed, 16)
            turn(TURN_X, xtok)
            await_turn(pe, TURN_MEM[1])
            for l in range(DEPTH):
                for ph in kv_mem[l]:
                    dense(ph)
            head_means(norm_mem)

            await_turn(pe, TURN_X)
            dense(s5_in)
            await_chunks(pe, s5_in)

            def s5_tile(i):
                pe.wait_ge(z_written, i * 6 + 6)
                wait_past(pe, z_copied, i * 2)
                wait_past(pe, y_summed, i)
                for z in range(8):
                    ins = pe.transpose(psA[:, z // 4, (z % 4) * P:(z % 4 + 1) * P], ZB[:, z, :], ident[:, :])
                ins.then_inc(z_turned, 1)
                for z in range(8):
                    bank = (psB, psC)[z // 4]
                    ins = pe.transpose(bank[:, (z % 4) * P:(z % 4 + 1) * P], ZC[:, z, :], ident[:, :])
                ins.then_inc(z_turned, 1)
                pe.wait_ge(z_copied, i * 2 + 1)
                wait_past(pe, bu_read, i * 4)
                for s in range(2):
                    for j in range(4):
                        ins = pe.matmul(acc[:, 2 * s + j // 2, (j % 2) * T:(j % 2 + 1) * T], BT[:, 4 * s + j, :],
                                        uT[:, bass.ts(i, 1), :].rearrange("p a t -> p (a t)"),
                                        start=True, stop=True)
                ins.then_inc(bu_ready, 1)
                pe.wait_ge(z_copied, i * 2 + 2)
                pe.wait_ge(h_ready, i * 2 + 2)
                for s, hx in enumerate((s5_hr, s5_hi)):
                    for j in range(4):
                        ins = pe.matmul(psB[:, 0:T], CT[:, 4 * s + j, :], hx[:, j, :],
                                        start=s == 0 and j == 0, stop=s == 1 and j == 3)
                ins.then_inc(y_ready, 1)

            peeled(pe, SSM_TILES, s5_tile)
            pe.wait_ge(gelu_done, 1)
            dense(s5_glu)
            pe.wait_ge(glu_mixed, 2)
            dense(s5_out)
            pe.wait_ge(ln_done, 1)
            turn(TURN_LN1, xtok)
            await_turn(pe, TURN_LN1)

            for ph in kv:
                dense(ph)
            await_chunks(pe, kv[5])
            pe.wait_ge(pos_ready, 4)
            for s, (ph, src) in enumerate(zip(cmp_w1, (kcT, vcT))):
                pe.wait_ge(landed[ph.slot(0, 0)], 16 * (ph.block0 // SLOTS + 1))
                w1 = ring[:, ph.slot(0, 0), :].rearrange("p (j n) -> p j n", j=BLOCK)
                for j in range(BLOCK):
                    ins = pe.matmul(psA[:, s, 0:(KVH + 1) * NCMP], w1[:, j, :],
                                    src[:, :, j:j + (NCMP - 1) * STRIDE + 1:STRIDE],
                                    start=j == 0, stop=j == BLOCK - 1)
                ins.then_inc(blocks_done, 1)
            pe.wait_ge(gate_w_landed, 16)
            for m in range(MT):
                for k in range(FT):
                    ins = pe.matmul(psB[:, m * NGATE:(m + 1) * NGATE], actT[:, k, m * P:(m + 1) * P],
                                    gate_w[:, k, :], start=k == 0, stop=k == FT - 1)
            ins.then_inc(gate_sum, 1)
            pe.wait_ge(cmp_hid_ready, 2)
            pe.matmul(psC[:, 0:KVH * NCMP], w2[:, 0, :], cmp_hid[:, 0, :], start=True, stop=True)\
                .then_inc(cmp_out, 1)
            pe.wait_ge(cmp_ready, 1)
            for g in range(KVH):
                ins = pe.matmul(psC[0:NCMP, g * DH:(g + 1) * DH], cmp_hid[:, 1, g * NCMP:(g + 1) * NCMP],
                                w2[:, 1, :], start=True, stop=True)
            ins.then_inc(cmp_out, 1)
            dense(b_q)
            await_chunks(pe, b_q)
            pe.wait_ge(cmp_ready, 2)
            pe.wait_ge(gate_ready, 3)
            for r in range(BRANCHES):
                dense(b_z[r])
                attend(nsa[r])
            pe.wait_ge(o_used, nsa[0][-1]["group"] + 1)
            pe.wait_ge(branch_summed, 2 * NH)
            dense(b_out)

            pe.wait_ge(scaled, 2 * SCALED[RMS_MIX[0]])
            turn(TURN_MIX[0], hs)
            await_turn(pe, TURN_MIX[0])
            for ph in (ab_rq, ab_rk, ab_rv, ab_rg, ab_nq, ab_nk, ab_nv):
                dense(ph)
            await_chunks(pe, ab_nv)
            for t in range(H8 + 1):
                if t < H8:
                    if t >= 2:
                        pe.wait_ge(rs_decayed, t - 1)
                    for m in range(MT):
                        ins = pe.matmul(psA[:, t % 2, m * T:(m + 1) * T], rkT[:, t, m * P:(m + 1) * P],
                                        rqT[:, t, :], start=True, stop=True)
                    ins.then_inc(rs_ready, 1)
                if t >= 1:
                    h = t - 1
                    pe.wait_ge(rs_decayed, h + 1)
                    if h >= 1:
                        pe.wait_ge(ro_copied, h)
                    for m in range(MT):
                        ins = pe.matmul(psC[:, 0:T], rv[:, m, h * DH:(h + 1) * DH],
                                        score[:, h % 2, m * T:(m + 1) * T], start=m == 0, stop=m == MT - 1)
                    ins.then_inc(ro_ready, 1)
            head_means(norm_ab)
            pe.wait_ge(normed, norm_ab[-1]["n"] + 1)
            pe.wait_ge(bias_landed, 16 * ROWS * H8)
            for h in range(H8):
                if h >= 2:
                    pe.wait_ge(bias_masked, h - 1)
                pe.matmul(psA[:, h % 2, :], flip[:, :], table[:, h, :], start=True, stop=True)\
                    .then_inc(bias_turned, 1)
            pe.wait_ge(bias_masked, H8)
            attend(na)
            pe.wait_ge(gated, 1)
            pe.wait_ge(o_used, na[-1]["group"] + 1)
            dense(ab_out)

            def tail_pe(l):
                xq, xo, ffn_in, ffn_out = layers[l]
                pe.wait_ge(scaled, 2 * SCALED[RMS_XA[l]])
                turn(TURN_XA[l], hs)
                await_turn(pe, TURN_XA[l])
                dense(xq)
                head_means(norm_x[l])
                pe.wait_ge(normed, norm_x[l][-1]["n"] + 1)
                attend(xat[l])
                pe.wait_ge(o_used, xat[l][-1]["group"] + 1)
                dense(xo)
                pe.wait_ge(scaled, 2 * SCALED[RMS_FFN[l]])
                turn(TURN_FFN[l], hs)
                await_turn(pe, TURN_FFN[l])
                dense(ffn_in)
                await_chunks(pe, ffn_in)
                dense(ffn_out)

            tail_pe(0)

            pe.wait_ge(scaled, 2 * SCALED[RMS_MIX[1]])
            turn(TURN_MIX[1], hs)
            await_turn(pe, TURN_MIX[1])
            dense(c_qk)
            dense(c_v)
            await_chunks(pe, c_v)
            head_means(norm_c)
            pe.wait_ge(normed, norm_c[-1]["n"] + 1)
            attend(dif)
            head_means(norm_do)
            pe.wait_ge(normed, norm_do[-1]["n"] + 1)
            dense(c_out)
            tail_pe(1)

        @block.scalar
        def _(act):
            chain = Chain(act, act_step)

            def root_of_mean_square(call, eps):
                act.wait_ge(ms_ready, call + 1)
                act.activation(root[:, :], mean_sq[:, :], ACT.Sqrt, bias=consts[:, eps:eps + 1])\
                    .then_inc(root_ready, 1)

            def rms_rows(call, src):
                root_of_mean_square(call, 0)
                act.wait_ge(rstd_ready, call + 1)
                act.activation(hs[:, 1, :], src[:, 1, :], ACT.Identity, scale=rstd[:, 1:2]).then_inc(scaled, 1)

            def turn_out(call, dst, gain=None):
                for k in range(1, FT // 2, 2):
                    n = 8 * call + k
                    act.wait_ge(turned, n + 1)
                    for f in (2 * k, 2 * k + 1):
                        bank = turn_banks[n % IN_FLIGHT][:, (f % 2) * T:(f % 2 + 1) * T]
                        ins = (act.activation(dst[:, f, :], bank, ACT.Identity) if gain is None else
                               act.activation(dst[:, f, :], bank, ACT.Identity,
                                              scale=colsB[:, gain + f:gain + f + 1]))
                        ins.then_inc(turned_act, 1)

            def head_roots(part):
                for t in range(len(part) + 1):
                    if t < len(part):
                        u = part[t]
                        n = u["n"]
                        if n >= 2:
                            act.wait_ge(mean_ready, n - 1)
                        act.activation(score[:, n % 2, :], u["x"].rearrange("p a t -> p (a t)"), ACT.Square)\
                            .then_inc(sq_ready, 1)
                    if t >= 1:
                        u = part[t - 1]
                        n = u["n"]
                        w = T if u["wide"] else 2 * T
                        act.wait_ge(mean_ready, n + 1)
                        if n >= 2:
                            act.wait_ge(normed, n - 1)
                        act.activation(probT[:, n % 2, 0:w], psA[:, n % 2, 0:w], ACT.Sqrt,
                                       bias=consts[:, 0:1], scale=0.5 if u["wide"] else 1.0)\
                            .then_inc(hroot_ready, 1)

            def attend(part):
                for t in range(len(part) + 1):
                    if t < len(part):
                        u = part[t]
                        n = u["n"]
                        act.wait_ge(max_ready, n + 1)
                        for m in range(MT):
                            s = score[:, n % 2, m * T:m * T + u["K"]]
                            act.activation(s, s, ACT.Exp, bias=neg_max[:, n % 2, m:m + 1],
                                           scale=SCALE if u["mode"] == "alibi" else 1.0,
                                           accum_out=denom[:, n % 2, m:m + 1]).then_inc(exp_ready, 1)
                    if t >= 1:
                        u = part[t - 1]
                        n, K = u["n"], u["K"]
                        act.wait_ge(probs_turned, n + 1)
                        if n >= 2:
                            act.wait_ge(o_ready, n - 1)
                        w = min(K, P)
                        size = T * -(-K // P)
                        act.copy(probT[0:w, n % 2, 0:size], psB[0:w, 0:size]).then_inc(probT_ready, 1)

            act.wait_ge(cols_turned, 1)
            act.copy(colsA[:, :], psA[:, 0, 0:P]).then_inc(cols_copied, 1)
            act.copy(colsB[:, :], psA[:, 1, 0:P]).then_inc(cols_copied, 1)
            act.copy(colsC[:, :], psB[:, 0:64]).then_inc(cols_copied, 1)
            act.wait_ge(lam_sum, 1)
            act.activation(lam[:, 2:4], psC[:, 0:2], ACT.Exp, scale=float(P)).then_inc(lam_exp, 1)
            act.wait_ge(lg_abs, 1)
            chain.add(act.activation(decay[:, 2, :], decay[:, 2, :], ACT.Exp, scale=-1.0))
            chain.settle()
            act.activation(decay[:, 2, :], decay[:, 2, :], ACT.Ln, bias=consts[:, 3:4]).then_inc(lg_ln, 1)
            act.wait_ge(cols_copied, 3)
            chain.add(act.activation(ssm[:, 0, :], colsA[:, A_DT:A_DT + 32], ACT.Exp))
            chain.settle()
            act.wait_ge(s5_exp, 1)
            act.activation(ssm[:, 1, :], ssm[:, 1, :], ACT.Exp).then_inc(s5_exp, 1)
            act.wait_ge(s5_frac0, 1)
            act.activation(ssm[:, 4, :], ssm[:, 3, :], ACT.Sin, scale=TURN).then_inc(s5_trig0, 1)
            chain.add(act.activation(ssm[:, 5, :], ssm[:, 3, :], ACT.Abs))
            chain.settle()
            act.activation(ssm[:, 5, :], ssm[:, 5, :], ACT.Sin, scale=-TURN, bias=consts[:, 2:3])\
                .then_inc(s5_trig0, 1)

            rms_rows(RMS_MEM, hs)
            for l in range(DEPTH):
                turn_out(TURN_MEM[l], memT[l], G_MEM + 16 * l)
            turn_out(TURN_X, actT)
            await_chunks(act, kv_mem[1][1])
            head_roots(norm_mem)

            def s5_z(i, c, src):
                at = 4 * c
                return act.activation(zT5[:, at:at + 4, :], feat_src(src), ACT.Silu)

            for c in range(2):
                act.wait_ge(blocks_done, s5_in.blocks_before(1, c, 2))
                s5_z(1, c, acc[:, 2 * s5_in.pair(c):2 * s5_in.pair(c) + 2, :])\
                    .then_inc(drained[s5_in.pair(c)], 1)

            def s5_tile(i):
                act.wait_ge(z_turned, i * 2 + 1)
                wait_past(act, bu_ready, i)
                act.copy(BT, psA[:, :, :].rearrange("p a (b s) -> p (a b) s", s=P)).then_inc(z_copied, 1)
                act.wait_ge(z_turned, i * 2 + 2)
                wait_past(act, y_ready, i)
                act.copy(CT[:, 0:4, :], psB[:, :].rearrange("p (b s) -> p b s", s=P)).then_inc(act_step, 1)
                act.wait_ge(act_step, i * 2 + (chain.n + 1))
                act.copy(CT[:, 4:8, :], psC[:, :].rearrange("p (b s) -> p b s", s=P)).then_inc(z_copied, 1)
                act.wait_ge(phase_ready, i + 1)
                wait_past(act, h_ready, i * 2)
                act.activation(s5_sin, s5_frac, ACT.Sin, scale=TURN).then_inc(trig_ready, 1)
                act.activation(s5_cos, s5_frac, ACT.Abs).then_inc(act_step, 1)
                act.wait_ge(act_step, i * 2 + (chain.n + 2))
                act.activation(s5_cos, s5_cos, ACT.Sin, scale=-TURN, bias=consts[:, 2:3]).then_inc(trig_ready, 1)

            peeled(act, SSM_TILES, s5_tile)
            chain.n += 2 * SSM_TILES
            act.wait_ge(y_summed, SSM_TILES)
            act.activation(gT, gT, ACT.Gelu_apprx_tanh).then_inc(gelu_done, 1)

            for c in range(2):
                act.wait_ge(blocks_done, s5_glu.blocks_before(0, c, 1))
                src = acc[:, 2 * s5_glu.pair(c):2 * s5_glu.pair(c) + 2, :]
                for f in range(4):
                    ft = 4 * c + f
                    ins = act.activation(yT5[:, ft, :], src[:, f // 2, (f % 2) * T:(f % 2 + 1) * T], ACT.Sigmoid,
                                         bias=colsA[:, A_BGLU + ft:A_BGLU + ft + 1])
                    if f < 3:
                        chain.add(ins)
                chain.settle()
                ins.then_inc(drained[s5_glu.pair(c)], 1)
            root_of_mean_square(LN1, 1)
            turn_out(TURN_LN1, actT)

            for s in range(2):
                act.wait_ge(cmp_bias_ready, s + 1)
                act.activation(cmp_hid[:, s, :], psA[:, s, 0:KVH * NCMP], ACT.Gelu_apprx_tanh,
                               bias=cmp_bias[:, s:s + 1]).then_inc(cmp_hid_ready, 1)
            act.wait_ge(gate_sum, 1)
            act.activation(gates[:, :, :], psB[:, 0:MT * NGATE].rearrange("p (m n) -> p m n", m=MT),
                           ACT.Sigmoid).then_inc(gate_ready, 1)
            for r in range(BRANCHES):
                if r >= 2:
                    act.wait_ge(branch_summed, NH * (r - 1))
                if r == 1:
                    act.wait_ge(o_used, nsa[0][-1]["group"] + 1)
                drain(act, b_z[r], lambda i, c, src: act.activation(
                    zT[:, bass.ds(i * 8 + 4 * c, 4), :], feat_src(src), ACT.Silu))
                attend(nsa[r])
            root_of_mean_square(LN2, 1)

            rms_rows(RMS_MIX[0], xtok)
            turn_out(TURN_MIX[0], actT, G_MIX)
            drain(act, ab_rg, lambda i, c, src: act.activation(rgT[:, 4 * c:4 * c + 4, :], feat_src(src), ACT.Silu))
            for h in range(H8):
                act.wait_ge(decay_arg, h + 1)
                act.activation(table[:, h, :], table[:, h, :], ACT.Exp).then_inc(decay_ready, 1)
            act.wait_ge(ro_copied, H8)
            head_roots(norm_ab)
            attend(na)

            def tail_act(l):
                xq, xo, ffn_in, ffn_out = layers[l]
                rms_rows(RMS_XA[l], xtok)
                turn_out(TURN_XA[l], actT, G_X + 16 * l)
                await_chunks(act, xq)
                head_roots(norm_x[l])
                attend(xat[l])
                rms_rows(RMS_FFN[l], xtok)
                turn_out(TURN_FFN[l], actT, G_FFN + 16 * l)

                def silu(i, c, src):
                    act.wait_ge(drained[ffn_in.pair(1)], ffn_in.pair_uses(i, 1))
                    return act.activation(silu_g, feat_src(src), ACT.Silu)

                drain(act, ffn_in, silu, only=[0])

            tail_act(0)
            rms_rows(RMS_MIX[1], xtok)
            turn_out(TURN_MIX[1], actT, G_MIX + 16)
            await_chunks(act, c_v)
            head_roots(norm_c)
            attend(dif)
            act.wait_ge(o_used, dif[-1]["group"] + 1)
            head_roots(norm_do)
            tail_act(1)

        @block.vector
        def _(dve):
            chain = Chain(dve, dve_step)

            def mean_squares(call, src, centred):
                for m in range(MT):
                    for k in range(4):
                        chain.add(dve.bn_stats(stats[:, m, 6 * k:6 * k + 6], src[:, m, k * COLS:(k + 1) * COLS]))
                chain.settle()
                for m in range(MT):
                    chain.add(dve.bn_aggr(moments[:, m, :], stats[:, m, :]))
                chain.settle()
                mean, var = moments[:, :, 0:1].rearrange("p m o -> p (m o)"), \
                    moments[:, :, 1:2].rearrange("p m o -> p (m o)")
                if centred:
                    dve.tensor_copy(mean_sq[:, :], var).then_inc(ms_ready, 1)
                else:
                    chain.add(dve.tensor_tensor(mean_sq[:, :], mean, mean, ALU.mult))
                    chain.settle()
                    dve.tensor_tensor(mean_sq[:, :], mean_sq[:, :], var, ALU.add).then_inc(ms_ready, 1)
                dve.wait_ge(root_ready, call + 1)
                dve.reciprocal(rstd[:, :], root[:, :]).then_inc(rstd_ready, 1)
                dve.wait_ge(rstd_ready, call + 1)

            def rms_rows(call, src):
                mean_squares(call, src, False)
                dve.tensor_scalar(hs[:, 0, :], src[:, 0, :], rstd[:, 0:1], None, ALU.mult).then_inc(scaled, 1)

            def layer_norm(call, l):
                mean_squares(call, xtok, True)
                dve.wait_ge(ln_landed, 32 * (l + 1))
                g = actT[:, 0:8, :].rearrange("p a b -> p (a b)")
                b = actT[:, 8:16, :].rearrange("p a b -> p (a b)")
                for m in range(MT):
                    chain.add(dve.tensor_scalar(xtok[:, m, :], xtok[:, m, :], moments[:, m, 0:1],
                                                rstd[:, m:m + 1], ALU.subtract, ALU.mult))
                for w, op in ((g, ALU.mult), (b, ALU.add)):
                    chain.settle()
                    for m in range(MT):
                        ins = dve.tensor_tensor(xtok[:, m, :], xtok[:, m, :], w, op)
                        if op == ALU.mult or m == 0:
                            chain.add(ins)
                chain.settle()
                ins.then_inc(ln_done, 1)
                dve.wait_ge(ln_done, l + 1)

            def turn_out(call, dst, gain=None):
                for k in range(0, FT // 2, 2):
                    n = 8 * call + k
                    dve.wait_ge(turned, n + 1)
                    for f in (2 * k, 2 * k + 1):
                        bank = turn_banks[n % IN_FLIGHT][:, (f % 2) * T:(f % 2 + 1) * T]
                        ins = (dve.tensor_copy(dst[:, f, :], bank) if gain is None else
                               dve.tensor_scalar(dst[:, f, :], bank, colsB[:, gain + f:gain + f + 1], None,
                                                 ALU.mult))
                        ins.then_inc(turned_dve, 1)

            def head_norm(part):
                for u in part:
                    n = u["n"]
                    w = T if u["wide"] else 2 * T
                    r = probT[:, n % 2, 0:w]
                    dve.wait_ge(hroot_ready, n + 1)
                    chain.add(dve.reciprocal(r, r))
                    chain.settle()
                    if u["wide"]:
                        x = u["x"]
                        for o in range(2):
                            chain.add(dve.scalar_tensor_tensor(
                                out=x[:, o, :], in0=x[:, o, :], scalar=colsA[:, u["g"][o]:u["g"][o] + 1], in1=r,
                                op0=ALU.mult, op1=ALU.mult))
                        chain.settle()
                        dve.tensor_scalar(x, x, 1.0 - LAM_INIT, None, ALU.mult).then_inc(normed, 1)
                    else:
                        x = u["x"].rearrange("p a t -> p (a t)")
                        dve.scalar_tensor_tensor(out=x, in0=x, scalar=colsA[:, u["g"][0]:u["g"][0] + 1], in1=r,
                                                 op0=ALU.mult, op1=ALU.mult).then_inc(normed, 1)

            def attend(part):
                for t in range(len(part) + 3):
                    if t < len(part):
                        u = part[t]
                        n, K = u["n"], u["K"]
                        src = psA[:, n % 2, :].rearrange("p (m k) -> p m k", m=MT)[:, :, 0:K]
                        s = score[:, n % 2, :].rearrange("p (m k) -> p m k", m=MT)[:, :, 0:K]
                        dve.wait_ge(scores_ready, n + 1)
                        if n >= 2:
                            dve.wait_ge(probs_turned, n - 1)
                        if u["mode"] == "bias":
                            ins = dve.scalar_tensor_tensor(out=s, in0=src, scalar=SCALE, in1=u["bias"],
                                                           op0=ALU.mult, op1=ALU.add)
                        elif u["mode"] == "alibi":
                            ins = dve.scalar_tensor_tensor(out=s, in0=later[:, :, :], scalar=-u["bias"] / SCALE,
                                                           in1=src, op0=ALU.mult, op1=ALU.add)
                        else:
                            ins = dve.tensor_scalar(s, src, SCALE, None, ALU.mult)
                        ins.then_inc(biased, 1)
                        dve.wait_ge(biased, n + 1)
                        ins = dve.tensor_reduce(neg_max[:, n % 2, :], s, AX_X, ALU.max, negate=True)
                        if u["mode"] == "alibi":
                            chain.add(ins)
                            chain.settle()
                            ins = dve.tensor_scalar(neg_max[:, n % 2, :], neg_max[:, n % 2, :], SCALE, None,
                                                    ALU.mult)
                        ins.then_inc(max_ready, 1)
                    if 0 <= t - 1 < len(part):
                        u = part[t - 1]
                        n, K = u["n"], u["K"]
                        s = score[:, n % 2, :].rearrange("p (m k) -> p m k", m=MT)[:, :, 0:K]
                        f = factor[:, n % 2, :]
                        dve.wait_ge(exp_ready, MT * (n + 1))
                        chain.add(dve.tensor_scalar(f, denom[:, n % 2, :], 1e-30, None, ALU.max))
                        chain.settle()
                        chain.add(dve.reciprocal(f, f))
                        chain.settle()
                        if u["gate"] is not None:
                            chain.add(dve.tensor_tensor(f, f, u["gate"], ALU.mult))
                            chain.settle()
                        dve.tensor_tensor(s, s, f.unsqueeze(2).to_broadcast([P, MT, K]), ALU.mult)\
                            .then_inc(probs_ready, 1)
                    if 0 <= t - 3 < len(part) and part[t - 3]["last"]:
                        u = part[t - 3]
                        dve.wait_ge(o_ready, u["n"] + 1)
                        if u["fin"] == "gate":
                            h = u["h"]
                            dst = oT if u["r"] == 0 else zT
                            ins = dve.tensor_tensor(dst[:, h, :], psC[:, 0:T], zT[:, h, :], ALU.mult)
                        elif u["halves"] == 2:
                            ins = dve.tensor_copy(u["to"], psC[:, :].rearrange("p (o t) -> p o t", o=2))
                        else:
                            ins = dve.tensor_copy(u["to"], psC[:, 0:T])
                        ins.then_inc(o_used, 1)

            def residual(ph, factor_):
                def add(i, c, src):
                    x = xtok[:, :, bass.ts(i * ph.body + c, ph.cols)]
                    if factor_ == 1.0:
                        return dve.tensor_tensor(x, x, src, ALU.add)
                    return dve.scalar_tensor_tensor(out=x, in0=x, scalar=factor_, in1=src, op0=ALU.mult,
                                                    op1=ALU.add)
                drain(dve, ph, add)
                await_chunks(dve, ph)

            def keep(ph, dst):
                if ph.style == "feat":
                    drain(dve, ph, lambda i, c, src: dve.tensor_copy(
                        dst[:, bass.ds(i * (4 * ph.body) + 4 * c, 4), :], feat_src(src)))
                else:
                    drain(dve, ph, lambda i, c, src: dve.tensor_copy(
                        dst[:, :, bass.ds(i * (COLS * ph.body) + COLS * c, COLS)], src))

            dve.wait_ge(ldt_landed, 16)
            dve.tensor_copy(rowsA[64:96, :].rearrange("j (h p) -> j h p", h=2),
                            ldt2[64:96, :].unsqueeze(2).to_broadcast([32, 2, STATES])).then_inc(s5_dt, 1)
            dve.wait_ge(cols_copied, 3)
            chain.add(dve.tensor_tensor(lam[:, 0:1], colsA[:, C_LAM:C_LAM + 1], colsA[:, C_LAM + 1:C_LAM + 2],
                                        ALU.mult))
            chain.settle()
            dve.tensor_tensor(lam[:, 1:2], colsA[:, C_LAM + 2:C_LAM + 3], colsA[:, C_LAM + 3:C_LAM + 4],
                              ALU.mult).then_inc(lam_prod, 1)
            dve.wait_ge(lam_exp, 1)
            chain.add(dve.tensor_tensor(lam[:, 4:5], lam[:, 3:4], lam[:, 2:3], ALU.subtract))
            chain.settle()
            chain.add(dve.tensor_scalar(lam[:, 7:8], lam[:, 4:5], -LAM_INIT, None, ALU.add))
            dve.wait_ge(consts_landed, 16 * N_CONST)
            chain.add(dve.tensor_scalar(decay[:, 1, :], decay[:, 0, :], -1.0, None, ALU.mult))
            chain.settle()
            dve.tensor_tensor(decay[:, 2, :], decay[:, 0, :], decay[:, 1, :], ALU.max).then_inc(lg_abs, 1)
            dve.wait_ge(lg_ln, 1)
            chain.add(dve.tensor_scalar(decay[:, 3, :], decay[:, 0, :], 0.0, None, ALU.min))
            chain.settle()
            chain.add(dve.tensor_tensor(decay[:, 3, :], decay[:, 3, :], decay[:, 2, :], ALU.subtract))

            def small(out_, x, y, op):
                chain.add(dve.tensor_tensor(ssm[:, out_, :], x, y, op))
                chain.settle()

            def scaled_by(out_, x, s1, s2, op0, op1):
                chain.add(dve.tensor_scalar(ssm[:, out_, :], x, s1, s2, op0, op1))
                chain.settle()

            def V(k):
                return ssm[:, k, :]

            re, im = colsA[:, A_RE:A_RE + 32], colsA[:, A_IM:A_IM + 32]
            dve.wait_ge(act_step, 2)
            dve.tensor_tensor(V(1), re, V(0), ALU.mult).then_inc(s5_exp, 1)
            small(2, im, V(0), ALU.mult)
            scaled_by(6, V(2), 1.0 / TWO_PI, ROUND, ALU.mult, ALU.add)
            scaled_by(6, V(6), ROUND, None, ALU.subtract, ALU.bypass)
            for c in (PI2_A, PI2_B, PI2_C):
                chain.add(dve.scalar_tensor_tensor(out=V(2), in0=V(6), scalar=-c, in1=V(2), op0=ALU.mult,
                                                   op1=ALU.add))
                chain.settle()
            scaled_by(3, V(2), 1.0 / TWO_PI, 0.5, ALU.mult, ALU.min)
            dve.tensor_scalar(V(3), V(3), -0.5, None, ALU.max).then_inc(s5_frac0, 1)
            dve.wait_ge(s5_trig0, 2)
            dve.wait_ge(s5_exp, 2)
            small(7, V(1), V(5), ALU.mult)
            small(8, V(1), V(4), ALU.mult)
            scaled_by(7, V(7), -1.0, None, ALU.add, ALU.bypass)
            small(9, re, re, ALU.mult)
            small(10, im, im, ALU.mult)
            small(9, V(9), V(10), ALU.add)
            chain.add(dve.reciprocal(V(9), V(9)))
            chain.settle()
            small(10, V(7), re, ALU.mult)
            small(11, V(8), im, ALU.mult)
            small(10, V(10), V(11), ALU.add)
            small(12, V(10), V(9), ALU.mult)
            small(10, V(8), re, ALU.mult)
            small(11, V(7), im, ALU.mult)
            small(10, V(10), V(11), ALU.subtract)
            small(13, V(10), V(9), ALU.mult)

            dve.wait_ge(mem_landed, 16)
            rms_rows(RMS_MEM, hs)
            for l in range(DEPTH):
                turn_out(TURN_MEM[l], memT[l], G_MEM + 16 * l)
            dve.wait_ge(x_landed, 16)
            turn_out(TURN_X, actT)
            for l in range(DEPTH):
                keep(kv_mem[l][0], mem_kT[:, l])
                keep(kv_mem[l][1], mem_v[:, l])
            head_norm(norm_mem)

            for c in range(2):
                dve.wait_ge(blocks_done, s5_in.blocks_before(0, c, 2))
                dve.tensor_copy(uT[:, 4 * c:4 * c + 4, :],
                                feat_src(acc[:, 2 * s5_in.pair(c):2 * s5_in.pair(c) + 2, :]))\
                    .then_inc(drained[s5_in.pair(c)], 1)
            dve.wait_ge(b_landed, 64)
            dve.wait_ge(normed, len(norm_mem))
            def per_state(v):
                return v.unsqueeze(2).to_broadcast([P, 32, GROUP])

            def wide(v):
                return v.rearrange("p (j c) -> p j c", c=GROUP)

            br, bi, t0 = wide(b_raw[:, 0, :]), wide(b_raw[:, 1, :]), s5_t1.rearrange("p a t -> p (a t)")[:, 0:512]
            for k, (x, y, op) in enumerate(((br, bi, ALU.subtract), (bi, br, ALU.add))):
                chain.add(dve.tensor_tensor(wide(bbar[:, k, :]), x, per_state(V(12)), ALU.mult))
                chain.add(dve.tensor_tensor(wide(t0), y, per_state(V(13)), ALU.mult))
                chain.settle()
                chain.add(dve.tensor_tensor(bbar[:, k, :], bbar[:, k, :], t0, op))
                chain.settle()
            await_chunks(dve, s5_in)
            chain.add(dve.memset(ZB, 0.0))
            chain.settle()
            dve.wait_ge(masks_made, 1)
            ZBf = ZB.rearrange("p z s -> p (z s)")
            diagonal = 4 * P
            n0 = chain.n
            per = 16

            def s5_tile(i):
                chain.n = i * per + n0
                wait_past(dve, z_turned, i * 2)
                for s in range(2):
                    for half in range(2):
                        rows_ = slice(64 * half, 64 * half + 64)
                        for_tile = ZBf[rows_, s * diagonal:(s + 1) * diagonal]
                        dst = bass.AP(tensor=for_tile.tensor, offset=for_tile.offset + half * GROUP,
                                      ap=[list(for_tile.ap[0]), [P + 2 * GROUP, 4], [1, GROUP]])
                        src = bbar[rows_, s, bass.ds(i * (4 * GROUP), 4 * GROUP)]
                        dve.tensor_copy(dst, src.rearrange("p (j c) -> p j c", c=GROUP)).then_inc(z_written, 1)
                for s in range(2):
                    src = c_raw[:, s, bass.ts(i, STATES)]
                    dve.tensor_tensor(
                        ZC[:, 4 * s:4 * s + 4, :].rearrange("p j (h q) -> p (j h) q", h=2),
                        src.unsqueeze(1).to_broadcast([P, 8, STATES]),
                        group_mask[:, s, :].unsqueeze(2).to_broadcast([P, 8, STATES]), ALU.mult)\
                        .then_inc(z_written, 1)
                wait_past(dve, trig_ready, i * 2)
                chain.add(dve.tensor_tensor(
                    s5_frac, time_row.unsqueeze(1).to_broadcast([P, 4, T]),
                    ssm[:, 3, bass.ts(i, 4)].unsqueeze(2).to_broadcast([P, 4, T]), ALU.mult))
                chain.settle()
                chain.add(dve.tensor_scalar(s5_t1, s5_frac, ROUND, ROUND, ALU.add, ALU.subtract))
                chain.settle()
                dve.tensor_tensor(s5_frac, s5_frac, s5_t1, ALU.subtract).then_inc(phase_ready, 1)
                dve.wait_ge(phase_ready, i + 1)
                dve.wait_ge(bu_ready, i + 1)
                dve.wait_ge(trig_ready, i * 2 + 2)
                bur, bui = feat_src(acc[:, 0:2, :]), feat_src(acc[:, 2:4, :])
                dve.tensor_tensor(s5_gr, bur, s5_cos, ALU.mult).then_inc(bu_read, 1)
                dve.tensor_tensor(s5_t1, bui, s5_sin, ALU.mult).then_inc(bu_read, 1)
                dve.tensor_tensor(s5_gi, bui, s5_cos, ALU.mult).then_inc(bu_read, 1)
                dve.tensor_tensor(s5_t2, bur, s5_sin, ALU.mult).then_inc(bu_read, 1)
                dve.wait_ge(bu_read, i * 4 + 4)
                chain.add(dve.tensor_tensor(s5_gr, s5_gr, s5_t1, ALU.add))
                chain.add(dve.tensor_tensor(s5_gi, s5_gi, s5_t2, ALU.subtract))
                chain.settle()
                for j in range(4):
                    mag = ssm[:, 1, bass.ds(i * 4 + j, 1)].to_broadcast([P, T])
                    for g in (s5_gr, s5_gi):
                        ins = dve.tensor_tensor_scan(g[:, j, :], mag, g[:, j, :], 0.0, ALU.mult, ALU.add)
                        chain.add(ins)
                chain.settle()
                wait_past(dve, y_ready, i)
                chain.add(dve.tensor_tensor(s5_hr, s5_gr, s5_cos, ALU.mult))
                chain.add(dve.tensor_tensor(s5_t1, s5_gi, s5_sin, ALU.mult))
                chain.settle()
                dve.tensor_tensor(s5_hr, s5_hr, s5_t1, ALU.subtract).then_inc(h_ready, 1)
                dve.wait_ge(h_ready, i * 2 + 1)
                chain.add(dve.tensor_tensor(s5_hi, s5_gr, s5_sin, ALU.mult))
                dve.tensor_tensor(s5_t1, s5_gi, s5_cos, ALU.mult).then_inc(dve_step, 1)
                chain.n += 1
                chain.settle()
                dve.tensor_tensor(s5_hi, s5_hi, s5_t1, ALU.add).then_inc(h_ready, 1)
                dve.wait_ge(h_ready, i * 2 + 2)
                dve.wait_ge(y_ready, i + 1)
                dve.scalar_tensor_tensor(
                    out=gT[:, bass.ts(i, 1), :].rearrange("p a t -> p (a t)"),
                    in0=uT[:, bass.ts(i, 1), :].rearrange("p a t -> p (a t)"),
                    scalar=colsA[:, bass.ds(i + A_D, 1)], in1=psB[:, 0:T], op0=ALU.mult, op1=ALU.add)\
                    .then_inc(y_summed, 1)

            peeled(dve, SSM_TILES, s5_tile)
            chain.n = n0 + per * SSM_TILES
            for c in range(2):
                t = slice(4 * c, 4 * c + 4)
                dve.wait_ge(drained[s5_glu.pair(c)], s5_glu.pair_uses(0, c) + 1)
                chain.add(dve.tensor_tensor(yT5[:, t, :], yT5[:, t, :], gT[:, t, :], ALU.mult))
                chain.settle()
                dve.tensor_tensor(yT5[:, t, :], yT5[:, t, :], zT5[:, t, :], ALU.mult).then_inc(glu_mixed, 1)
            residual(s5_out, ALPHA)
            layer_norm(LN1, 0)
            turn_out(TURN_LN1, actT)

            for s, x in enumerate((kcT, vcT)):
                dve.memset(x[:, KVH, BLOCK:T], 0.0).then_inc(pos_ready, 1)
                dve.tensor_copy(x[:, KVH, 0:BLOCK], colsC[:, BLOCK * s:BLOCK * (s + 1)]).then_inc(pos_ready, 1)
            for ph, dst in zip(kv, (kcT, vcT, ksT, v_slc, kwT, v_win)):
                keep(ph, dst)
            for s, ph in enumerate(cmp_w1):
                dve.wait_ge(blocks_done, ph.block0 + 1)
                dve.tensor_copy(cmp_bias[:, s:s + 1], psA[:, s, KVH * NCMP:KVH * NCMP + 1])\
                    .then_inc(cmp_bias_ready, 1)
                dve.wait_ge(cmp_bias_ready, s + 1)
                dve.wait_ge(cmp_hid_ready, s + 1)
                dve.engine_nop().then_inc(drained[ph.pair(0)], 1)
            dve.wait_ge(gate_ready, 1)
            for m in range(MT):
                dve.tensor_scalar(gates[:, m, 0:NH], gates[:, m, 0:NH], row_ok[:, m:m + 1], None, ALU.mult)\
                    .then_inc(gate_ready, 1)
            dve.wait_ge(cmp_out, 1)
            dve.tensor_copy(kcmpT[:, :, :], psC[:, 0:KVH * NCMP].rearrange("p (g n) -> p g n", g=KVH))\
                .then_inc(cmp_ready, 1)
            dve.wait_ge(cmp_out, 2)
            dve.tensor_copy(vcmp[:, :, :], psC[0:NCMP, :].rearrange("p (g n) -> p g n", g=KVH))\
                .then_inc(cmp_ready, 1)
            dve.wait_ge(gate_ready, 3)
            keep(b_q, qT)
            dve.wait_ge(causal_made, 1)
            for r in range(BRANCHES):
                await_chunks(dve, b_z[r])
                attend(nsa[r])
            residual(b_out, ALPHA)
            layer_norm(LN2, 1)

            rms_rows(RMS_MIX[0], xtok)
            turn_out(TURN_MIX[0], actT, G_MIX)
            keep(ab_rq, rqT)
            keep(ab_rk, rkT)
            keep(ab_rv, rv)
            dve.wait_ge(lags_made, 1)
            for h in range(H8):
                d = table[:, h, :]
                chain.add(dve.tensor_scalar(d, later[:, :, :].rearrange("p m t -> p (m t)"), decay[:, 3, h:h + 1],
                                            None, ALU.mult))
                chain.settle()
                dve.scalar_tensor_tensor(out=d, in0=earlier[:, :, :].rearrange("p m t -> p (m t)"),
                                         scalar=decay[:, 3, 8 + h:9 + h], in1=d, op0=ALU.mult, op1=ALU.add)\
                    .then_inc(decay_arg, 1)
            keep(ab_nq, nqT)
            keep(ab_nk, nkT)
            keep(ab_nv, nv)
            for t in range(H8 + 1):
                if t < H8:
                    dve.wait_ge(rs_ready, t + 1)
                    dve.wait_ge(decay_ready, t + 1)
                    if t >= 2:
                        dve.wait_ge(ro_ready, t - 1)
                    dve.scalar_tensor_tensor(out=score[:, t % 2, :], in0=psA[:, t % 2, :], scalar=SCALE,
                                             in1=table[:, t, :], op0=ALU.mult, op1=ALU.mult)\
                        .then_inc(rs_decayed, 1)
                if t >= 1:
                    dve.wait_ge(ro_ready, t)
                    dve.tensor_copy(rqT[:, t - 1, :], psC[:, 0:T]).then_inc(ro_copied, 1)
            dve.wait_ge(ro_copied, H8)
            head_norm(norm_ab)
            dve.wait_ge(normed, norm_ab[-1]["n"] + 1)
            dve.tensor_tensor(rgT, rgT, rqT, ALU.mult).then_inc(gated, 1)
            for h in range(H8):
                dve.wait_ge(bias_turned, h + 1)
                dve.tensor_tensor(table[:, h, :].rearrange("p (n c) -> p n c", c=GRID),
                                  psA[:, h % 2, :].rearrange("p (n c) -> p n c", c=GRID),
                                  col_mask[:, :].unsqueeze(1).to_broadcast([P, MT * ROWS, GRID]), ALU.add)\
                    .then_inc(bias_masked, 1)
            dve.wait_ge(bias_masked, H8)
            attend(na)
            residual(ab_out, 1.0)

            def tail_dve(l):
                xq, xo, ffn_in, ffn_out = layers[l]
                rms_rows(RMS_XA[l], xtok)
                turn_out(TURN_XA[l], actT, G_X + 16 * l)
                keep(xq, xqT)
                await_chunks(dve, xq)
                head_norm(norm_x[l])
                attend(xat[l])
                residual(xo, 1.0)
                rms_rows(RMS_FFN[l], xtok)
                turn_out(TURN_FFN[l], actT, G_FFN + 16 * l)

                def times_up(i, c, src):
                    dve.wait_ge(drained[ffn_in.pair(0)], ffn_in.pair_uses(i, 0) + 1)
                    return dve.tensor_tensor(hidT[:, bass.ts(i, 4), :], silu_g, feat_src(src), ALU.mult)

                drain(dve, ffn_in, times_up, only=[1])
                residual(ffn_out, 1.0)

            tail_dve(0)
            rms_rows(RMS_MIX[1], xtok)
            turn_out(TURN_MIX[1], actT, G_MIX + 16)
            chain.add(dve.tensor_tensor(later[:, :, :], later[:, :, :], earlier[:, :, :], ALU.add))
            chain.settle()
            keep(c_qk, area(0, 2 * NH, T))
            keep(c_v, dv)
            await_chunks(dve, c_v)
            head_norm(norm_c)
            attend(dif)
            dve.wait_ge(o_used, dif[-1]["group"] + 1)
            head_norm(norm_do)
            residual(c_out, 1.0)
            tail_dve(1)


N_CONST = 27
_IN = ['x', 'a_w_in', 'a_lam_re', 'a_lam_im', 'a_log_dt', 'a_b_re', 'a_b_im', 'a_c_re', 'a_c_im', 'a_d',
       'a_w_glu', 'a_b_glu', 'a_w_out', 'kv_w', 'cmp_pos_k', 'cmp_w1_k', 'cmp_w2_k', 'cmp_pos_v', 'cmp_w1_v',
       'cmp_w2_v', 'b_w_in', 'b_w_out', 'ln_g', 'ln_b', 'mem_2', 'norm_mix_g_2', 'norm_xattn_g_2',
       'norm_mem_g_2', 'norm_ffn_g_2', 'w_in_ab_2', 'ret_decay_fwd_2', 'ret_decay_bwd_2', 'ret_out_g_2',
       'na_q_g_2', 'na_k_g_2', 'na_rpb_2', 'w_out_ab_2', 'w_in_c_2', 'diff_q_g_2', 'diff_k_g_2',
       'lambda_q1_2', 'lambda_k1_2', 'lambda_q2_2', 'lambda_k2_2', 'diff_out_g_2', 'w_out_c_2', 'w_xq_2',
       'w_xkv_2', 'w_xo_2', 'xq_g_2', 'xk_g_2', 'w_ffn_in_2', 'w_ffn_out_2']


def kernel(**inputs):
    import numpy as _np
    import concourse.bacc as _bacc
    from concourse.bass_utils import run_bass_kernel_spmd as _run

    nc = _bacc.Bacc("TRN2", target_bir_lowering=False, num_devices=1)
    arrays, aps = {}, {}
    for name in _IN:
        x = _np.ascontiguousarray(inputs[name])
        arrays[f"in_{name}"] = x
        aps[name] = nc.dram_tensor(f"in_{name}", x.shape, mybir.dt.from_np(x.dtype), kind="ExternalInput").ap()
    out = nc.dram_tensor("out_x", (1, T, D), F32, kind="ExternalOutput").ap()
    program(nc, aps, out)
    r = _run(nc, [arrays], core_ids=[0])
    return r.results[0]["out_x"]
```

```python
import math
from contextlib import ExitStack, contextmanager

import numpy as np

import concourse.bass as bass
from concourse import mybir

F32 = mybir.dt.float32
F32R = mybir.dt.float32r
ALU = mybir.AluOpType
ACT = mybir.ActivationFunctionType
AX_X = mybir.AxisListType.X

P = 128
D = 2048
T = 256
MT = T // P
FT = D // P
SLOTS = 4
SPLIT_SLOTS = 2
SLOT = 2048
HALF = SLOT // 2
COLS = 512

SSM_TILES = 8
STATES = 64
GROUP = 16
NH = 16
DH = 128
KVH = 4
BLOCK, STRIDE = 32, 16
NCMP = (T - BLOCK) // STRIDE + 1
BRANCHES = 3
NGATE = BRANCHES * NH
H8 = 8
GRID = 64
ROWS = T // GRID
WIN_R, WIN_C = 8, 16
RPB_R, RPB_C = 2 * WIN_R - 1, 2 * WIN_C - 1
XH = 4
FFN = 5632
FFN_T = FFN // P
FFN_PARTS = (16, 16, 12)
DEPTH = 2
ALPHA = (2 * DEPTH) ** 0.25
LN_EPS, RMS_EPS = 1e-5, 1e-6
SCALE = DH ** -0.5
NEG = -1e30
LAM_INIT = 0.8 - 0.6 * math.exp(-0.3)
ROUND = 1.5 * 2.0 ** 23
TWO_PI = 2 * math.pi
PI2_A = 6.28125
PI2_B = float(np.float32(TWO_PI - PI2_A))
PI2_C = float(np.float32(TWO_PI - PI2_A - PI2_B))
TURN = float(np.nextafter(np.float32(TWO_PI), np.float32(0)))


@contextmanager
def rep(eng, n):
    if n == 1:
        yield 0
    else:
        with eng.Fori(0, n) as i:
            yield i


def peeled(eng, n, body):
    body(0)
    with eng.Fori(1, n) as i:
        body(i)


def wait_past(eng, sem, value):
    if not isinstance(value, int) or value > 0:
        eng.wait_ge(sem, value)


class Chain:

    def __init__(self, eng, sem):
        self.eng, self.sem, self.n = eng, sem, 0

    def add(self, ins):
        ins.then_inc(self.sem, 1)
        self.n += 1

    def settle(self):
        self.eng.wait_ge(self.sem, self.n)


class Dense:

    def __init__(self, plan, src, kt, cols, blocks, chunks, style, iters=1, hidden=False):
        self.src, self.kt, self.cols, self.blocks, self.style = src, kt, cols, blocks, style
        self.iters, self.body, self.hidden = iters, chunks // iters, hidden
        self.block0, self.chunk0 = plan["blocks"], plan["chunks"]
        plan["blocks"] += chunks * blocks
        plan["chunks"] += chunks
        self.end = plan["chunks"]
        assert kt * cols == SLOT
        assert iters == 1 or (self.body * blocks % SLOTS == 0 and self.body % 2 == 0)

    def pair(self, c):
        return (self.chunk0 + c) % 2

    def block(self, c, b):
        return self.block0 + c * self.blocks + b

    def blocks_before(self, i, c, b):
        return i * (self.body * self.blocks) + self.block(c, b)

    def pair_uses(self, i, c):
        return i * (self.body // 2) + (self.chunk0 + c) // 2


class Loose:

    def __init__(self, plan, blocks):
        self.block0, self.blocks = plan["blocks"], blocks
        plan["blocks"] += blocks


def program(nc, a, out):
    ctx = ExitStack()
    with ctx:
        def sb(name, *shape, dt=F32):
            return ctx.enter_context(nc.sbuf_tensor(name, list(shape), dt))

        def ps(name, *shape):
            return ctx.enter_context(nc.psum_tensor(name, list(shape), F32))

        def sem(name):
            return ctx.enter_context(nc.semaphore(name))

        ring = sb("ring", P, SLOTS, SLOT)
        xtok = sb("xtok", P, MT, D)
        wH = sb("wH", P, SPLIT_SLOTS, SLOT, dt=F32R)
        wL = sb("wL", P, SPLIT_SLOTS, SLOT, dt=F32R)
        with nc.sbuf_tensor("s5_scratch", [P, 2 * FT * T], F32) as s5_scratch:
            pass
        actH = sb("actH", P, FT, T, dt=F32R)
        actL = sb("actL", P, FT, T, dt=F32R)
        with ExitStack() as over:
            hidH = over.enter_context(nc.sbuf_tensor("hidH", [P, FFN_PARTS[0], T], F32R))
            hidL = over.enter_context(nc.sbuf_tensor("hidL", [P, FFN_PARTS[0], T], F32R))
            ffn_tmp = over.enter_context(nc.sbuf_tensor("ffn_tmp", [P, 2, 2, T], F32))
        arena = sb("arena", P, 14848)
        mem_kT = sb("mem_kT", P, DEPTH, XH, T)
        mem_v = sb("mem_v", P, DEPTH, MT, XH * DH)
        score = sb("score", P, 2, 512)
        probT = sb("probT", P, 2, 512)
        ident = sb("ident", P, P)
        flip = sb("flip", P, P)
        mean_of = sb("mean_of", P, P)
        causal = sb("causal", P, MT, T)
        earlier = sb("earlier", P, MT, T)
        later = causal
        time_row = earlier[:, 0, :]
        ssm = causal[:, :, :].rearrange("p m t -> p (m t)").rearrange("p (k j) -> p k j", j=32)
        cmp_mask = sb("cmp_mask", P, MT, NCMP)
        row_ok = sb("row_ok", P, MT)
        group_mask = sb("group_mask", P, 2, 8)
        col_mask = sb("col_mask", P, GRID)
        ldt2 = sb("ldt2", 96, 2)
        colsA = sb("colsA", P, P)
        colsB = sb("colsB", P, P)
        colsC = sb("colsC", P, 64)
        consts = sb("consts", P, 4)
        decay = sb("decay", P, 4, 16)
        lam = sb("lam", P, 8)
        gates = sb("gates", P, MT, NGATE)
        w2 = sb("w2", P, 2, P)
        cmp_hid = sb("cmp_hid", P, 2, KVH * NCMP)
        cmp_bias = sb("cmp_bias", P, 2)
        kcmpT = sb("kcmpT", P, KVH, NCMP)
        vcmp = sb("vcmp", NCMP, KVH, DH)
        rpb_pad = sb("rpb_pad", H8 * RPB_R, P)
        stats = sb("stats", P, MT, 24)
        moments = sb("moments", P, MT, 2)
        mean_sq = sb("mean_sq", P, MT)
        root = sb("root", P, MT)
        rstd = sb("rstd", P, MT)
        neg_max = sb("neg_max", P, 2, MT)
        denom = sb("denom", P, 2, MT)
        factor = sb("factor", P, 2, MT)
        rpb_dram = nc.dram_tensor("rpb_scratch", [H8 * RPB_R, P], F32, kind="Internal").ap()

        acc = ps("acc", P, 4, 512)
        psA = ps("psA", P, 2, 512)
        psB = ps("psB", P, 512)
        psC = ps("psC", P, 512)
        turn_banks = [psA[:, 0, :], psA[:, 1, :], psB[:, :], psC[:, :]]

        def area(at, *shape):
            n = int(np.prod(shape))
            v = arena[:, at:at + n]
            if len(shape) == 2:
                return v.rearrange("p (a b) -> p a b", a=shape[0])
            if len(shape) == 3:
                return v.rearrange("p (a b c) -> p a b c", a=shape[0], b=shape[1])
            return v

        def scratch(at, *shape):
            n = int(np.prod(shape))
            return s5_scratch[:, at:at + n].rearrange("p (a b) -> p a b", a=shape[0])

        hs = area(10752, MT, D)
        rowsA, rowsB, rowsC = area(8192, P), area(8320, P), area(8448, P)[0:64, :]
        uT, zT5, gT, glT = (area(2048 * k, 8, T) for k in range(4))
        s5_sin, s5_cos, s5_frac, s5_t1, s5_t2, s5_gr, s5_gi = (
            area(6144 + 1024 * k, 4, T) for k in range(7))
        b_raw = area(13312, 2, 512)
        s5_hr, s5_hi = scratch(0, 4, T), scratch(1024, 4, T)
        ZB, ZC, BT, CT = (scratch(2048 + 1024 * k, 8, P) for k in range(4))
        bbar = score
        c_raw = probT
        ln_rows = area(0, 2, D)
        kcT = area(0, KVH + 1, T)
        vcT = area(1280, KVH + 1, T)
        ksT = area(2560, KVH, T)
        kwT = area(3584, KVH, T)
        v_slc = area(4608, MT, 512)
        v_win = area(5632, MT, 512)
        qT = area(6656, NH // 2, T)
        zT = area(8704, NH // 2, T)
        gate_w = area(8704, FT, NGATE)
        oT = area(10752, NH, T)
        rqT, rkT, rgT = (area(2048 * k, H8, T) for k in range(3))
        rv = area(6144, MT, H8 * DH)
        nqT, nkT, nv = rqT, rkT, rv
        table = area(8192, H8, 2 * T)
        dqT, dkT = area(0, NH, T), area(4096, NH, T)
        dv = area(8192, MT, D)
        xqT = area(0, XH, T)
        xoT = area(1024, XH, T)
        silu_g, hid_f = ffn_tmp[:, 0, :, :], ffn_tmp[:, 1, :, :]

        A_RE, A_IM, A_DT, A_D, A_BGLU = 0, 32, 64, 96, 104
        (C_RET, C_NAQ, C_NAK, C_DQ, C_DK, C_DO, C_XQ, C_XK, C_LAM) = (
            112, 113, 114, 115, 116, 117, 119, 121, 123)
        G_MIX, G_X, G_MEM, G_FFN = 0, 32, 64, 96

        landed = [sem(f"weights_landed_{s}") for s in range(SLOTS)]
        blocks_done = sem("weight_blocks_done")
        drained = [sem(f"chunks_drained_{p}") for p in range(2)]
        x_landed, mem_landed, consts_landed = sem("x_landed"), sem("mem_landed"), sem("consts_landed")
        ldt_landed, b_landed, ln_landed = sem("ldt_landed"), sem("b_landed"), sem("ln_landed")
        pad_landed, pad_stored, bias_landed = sem("pad_landed"), sem("pad_stored"), sem("bias_landed")
        masks_made, causal_made, lags_made = sem("masks_made"), sem("causal_made"), sem("lags_made")
        ident_made = sem("ident_made")
        pool_step, dve_step, act_step = sem("pool_step"), sem("dve_step"), sem("act_step")
        cols_turned, cols_copied = sem("cols_turned"), sem("cols_copied")
        ms_ready, root_ready, rstd_ready = sem("mean_square_ready"), sem("root_ready"), sem("rstd_ready")
        scaled = sem("rows_scaled")
        ln_done = sem("layer_norm_done")
        turned = sem("tiles_turned")
        turned_h, turned_l = sem("turned_tiles_high"), sem("turned_tiles_low")
        h_made, l_made = sem("weight_highs_made"), sem("weight_lows_made")
        act_h, act_l = sem("activation_highs_made"), sem("activation_lows_made")
        hid_h, hid_l = sem("hidden_highs_made"), sem("hidden_lows_made")
        sq_ready, mean_ready, hroot_ready, normed = (
            sem("squares_ready"), sem("head_mean_ready"), sem("head_root_ready"), sem("heads_normed"))
        scores_ready, biased, max_ready, exp_ready = (
            sem("scores_ready"), sem("scores_biased"), sem("max_ready"), sem("exp_ready"))
        probs_ready, probs_turned, probT_ready, o_ready, o_used = (
            sem("probs_ready"), sem("probs_turned"), sem("probT_ready"), sem("o_ready"), sem("o_used"))
        branch_summed = sem("branch_summed")
        s5_dt, s5_exp, s5_frac0, s5_trig0 = sem("s5_dt"), sem("s5_theta"), sem("s5_frac0"), sem("s5_trig0")
        z_written, z_turned, z_copied = sem("s5_z_written"), sem("s5_z_turned"), sem("s5_z_copied")
        phase_ready, trig_ready, bu_ready, bu_read = (
            sem("s5_phase_ready"), sem("s5_trig_ready"), sem("s5_bu_ready"), sem("s5_bu_read"))
        h_ready, y_ready, y_summed, gelu_done, glu_mixed = (
            sem("s5_h_ready"), sem("s5_y_ready"), sem("s5_y_summed"), sem("s5_gelu_done"), sem("s5_glu_mixed"))
        pos_ready, cmp_sum, cmp_bias_ready, cmp_hid_ready, cmp_out, cmp_ready = (
            sem("pos_ready"), sem("cmp_sum"), sem("cmp_bias_ready"), sem("cmp_hid_ready"), sem("cmp_out"),
            sem("cmp_ready"))
        gate_w_landed = sem("gate_w_landed")
        gate_sum, gate_ready = sem("gate_sum"), sem("gate_ready")
        lg_abs, lg_ln, lg_ready, lam_prod, lam_sum, lam_exp, lam_ready = (
            sem("lg_abs"), sem("lg_ln"), sem("lg_ready"), sem("lam_prod"), sem("lam_sum"), sem("lam_exp"),
            sem("lam_ready"))
        decay_arg, decay_ready = sem("decay_arg"), sem("decay_ready")
        rs_ready, rs_decayed, ro_ready, ro_copied, gated = (
            sem("ret_scores_ready"), sem("ret_scores_decayed"), sem("ret_o_ready"), sem("ret_o_copied"),
            sem("ret_gated"))
        bias_turned, bias_masked = sem("na_bias_turned"), sem("na_bias_masked")
        out_done = sem("out_done")

        plan = {"blocks": 0, "chunks": 0}

        def columns(w, kt, cols):
            v = w.rearrange("(t p) n -> p t n", p=P)
            return lambda j, k=0: v[:, k * kt:(k + 1) * kt, bass.ts(j, cols)]

        def feat(w, first, tiles, iters=1):
            at = columns(w, FT, P)
            chunks = tiles // 2
            body = chunks // iters
            return Dense(plan, lambda i, c, b: at(i * (2 * body) + (first + 2 * c + b)), FT, P, 2, chunks,
                         "feat", iters)

        def tok(w, first, chunks, blocks, iters=1, k0=0, hidden=False):
            at = columns(w, 4, COLS)
            body = chunks // iters
            return Dense(plan, lambda i, c, b: at(i * body + (first + c), k0 + b), 4, COLS, blocks, chunks,
                         "tok", iters, hidden)

        kv_mem = [(feat(a["w_xkv_2"][l], 0, XH), tok(a["w_xkv_2"][l], 1, 1, 4)) for l in range(DEPTH)]
        s5_u = feat(a["a_w_in"][0], 0, 8, 2)
        s5_z = feat(a["a_w_in"][0], 8, 8, 2)
        glu_at = columns(a["a_w_glu"][0], 8, 2 * P)
        s5_glu = Dense(plan, lambda i, c, b: glu_at(c), 8, 2 * P, 1, 4, "feat")
        s5_out = tok(a["a_w_out"][0], 0, 4, 2, 2)
        kv = [feat(a["kv_w"], 4 * k, KVH) if style == "feat" else tok(a["kv_w"], k, 1, 4)
              for k, style in enumerate(["feat", "feat", "feat", "tok", "feat", "tok"])]
        cmp_w1 = [Loose(plan, 2) for _ in range(2)]
        b_q, b_z = [], []
        for hh in range(2):
            b_q.append(feat(a["b_w_in"][0], 8 * hh, 8, 2))
            b_z.append([feat(a["b_w_in"][0], NH * (r + 1) + 8 * hh, 8, 2) for r in range(BRANCHES)])
        b_out = tok(a["b_w_out"][0], 0, 4, 4, 2)

        w_ab = a["w_in_ab_2"][0]
        ab_rq, ab_rk = feat(w_ab, 0, 8, 2), feat(w_ab, 8, 8, 2)
        ab_rv, ab_rg = tok(w_ab, 4, 2, 4), feat(w_ab, 24, 8, 2)
        ab_nq, ab_nk, ab_nv = feat(w_ab, 32, 8, 2), feat(w_ab, 40, 8, 2), tok(w_ab, 12, 2, 4)
        ab_out = tok(a["w_out_ab_2"][0], 0, 4, 4, 2)
        layers = []

        def tail(l):
            xq = feat(a["w_xq_2"][l], 0, XH)
            xo = tok(a["w_xo_2"][l], 0, 4, 1)
            at = columns(a["w_ffn_in_2"][l], FT, P)
            parts, k0 = [], 0
            for n in FFN_PARTS:
                def src(i, c, b, k0=k0):
                    return at(i * 2 + (k0 + c * FFN_T + b))
                ffn_in = Dense(plan, src, FT, P, 2, n, "feat", n // 2)
                ffn_out = tok(a["w_ffn_out_2"][l], 0, 4, n // 4, 2 if n % 8 == 0 else 1, k0 // 4, True)
                parts.append((ffn_in, ffn_out))
                k0 += n
            return xq, xo, parts

        layers.append(tail(0))
        c_qk = feat(a["w_in_c_2"][0], 0, 2 * NH, 8)
        c_v = tok(a["w_in_c_2"][0], 8, 4, 4, 2)
        c_out = tok(a["w_out_c_2"][0], 0, 4, 4, 2)
        layers.append(tail(1))

        def attn(q, k, K, v, mode, bias=None, gate=None, first=True, last=True, halves=1, **more):
            return dict(q=q, k=k, K=K, v=v, mode=mode, bias=bias, gate=gate, first=first, last=last,
                        halves=halves, **more)

        nsa = []
        for hh in range(2):
            nsa.append([])
            for r in range(BRANCHES):
                part = []
                for h8 in range(NH // 2):
                    h = hh * (NH // 2) + h8
                    g = h // (NH // KVH)
                    gate = gates[:, :, r * NH + h:r * NH + h + 1].rearrange("p m o -> p (m o)")
                    if r == 0:
                        u = attn(qT[:, h8, :], kcmpT[:, g, :], NCMP, lambda t, o, g=g: vcmp[:, g, :], "bias",
                                 cmp_mask[:, :, :], gate)
                    else:
                        kk, vv = ((ksT, v_slc), (kwT, v_win))[r - 1]
                        u = attn(qT[:, h8, :], kk[:, g, :], T,
                                 lambda t, o, g=g, vv=vv: vv[:, t, g * DH:(g + 1) * DH], "bias",
                                 causal[:, :, :], gate)
                    u.update(fin="gate", r=r, h=h, h8=h8)
                    part.append(u)
                nsa[hh].append(part)
        na = [attn(nqT[:, h, :], nkT[:, h, :], T, lambda t, o, h=h: nv[:, t, h * DH:(h + 1) * DH], "bias",
                   table[:, h, :].rearrange("p (q k) -> p q k", q=MT), fin="copy", to=nqT[:, h, :])
              for h in range(H8)]
        xat = [[attn(xqT[:, h, :], mem_kT[:, l, h, :], T,
                     lambda t, o, h=h, l=l: mem_v[:, l, t, h * DH:(h + 1) * DH], "plain",
                     fin="copy", to=xoT[:, h, :]) for h in range(XH)] for l in range(DEPTH)]
        dif = [attn(dqT[:, 2 * h + c, :], dkT[:, 2 * h + c, :], T,
                    lambda t, o, h=h: dv[:, t, h * T + o * DH:h * T + (o + 1) * DH], "alibi",
                    bias=2.0 ** (-8.0 * (h + 1) / H8), gate=lam[:, 7:8].to_broadcast([P, MT]) if c else None,
                    first=c == 0, last=c == 1, halves=2, fin="copy", to=dqT[:, 2 * h:2 * h + 2, :])
               for h in range(H8) for c in range(2)]
        groups = units = 0
        for part in (*nsa[0], *nsa[1], na, xat[0], dif, xat[1]):
            for u in part:
                u["n"], u["group"] = units, groups
                units += 1
                groups += u["last"]

        def pairs(v, n, g):
            return [dict(x=v[:, k:k + 2, :], g=[g, g], wide=False) for k in range(0, n, 2)]

        norm_mem = [u for l in range(DEPTH) for u in pairs(mem_kT[:, l], XH, C_XK + l)]
        norm_ret = pairs(rqT, H8, C_RET)
        norm_na = pairs(nqT, H8, C_NAQ) + pairs(nkT, H8, C_NAK)
        norm_x = [pairs(xqT, XH, C_XQ + l) for l in range(DEPTH)]
        norm_c = pairs(dqT, NH, C_DQ) + pairs(dkT, NH, C_DK)
        norm_do = [dict(x=dqT[:, k:k + 2, :], g=[C_DO, C_DO + 1], wide=True) for k in range(0, NH, 2)]
        n = 0
        for part in (norm_mem, norm_ret, norm_na, norm_x[0], norm_c, norm_do, norm_x[1]):
            for u in part:
                u["n"] = n
                n += 1

        TURN_MEM, TURN_X, TURN_LN1, TURN_MIX, TURN_XA, TURN_FFN = (0, 1), 2, 3, (4, 7), (5, 8), (6, 9)
        RMS_MEM, LN1, LN2, RMS_MIX, RMS_XA, RMS_FFN = 0, 1, 2, (3, 6), (4, 7), (5, 8)
        SCALED = {RMS_MEM: 1, RMS_MIX[0]: 2, RMS_XA[0]: 3, RMS_FFN[0]: 4, RMS_MIX[1]: 5, RMS_XA[1]: 6,
                  RMS_FFN[1]: 7}
        IN_FLIGHT = len(turn_banks)

        def await_chunks(eng, ph):
            for last in (ph.end - 2, ph.end - 1):
                eng.wait_ge(drained[last % 2], last // 2 + 1)

        def await_turn(eng, call):
            eng.wait_ge(turned_l, FT * (call + 1))

        def drain_chunk(eng, ph, i, c, fn):
            eng.wait_ge(blocks_done, ph.blocks_before(i, c, ph.blocks))
            first = 2 * ph.pair(c)
            src = acc[:, first, :].rearrange("p (f t) -> p f t", t=T) if ph.style == "feat" else \
                acc[:, first:first + 2, :]
            fn(i, c, src).then_inc(drained[ph.pair(c)], 1)

        SPLITS = [(gT, 8, 0), (glT, 8, 0), (oT, NH, 0), (rgT, H8, 0), (nqT, H8, H8), (xoT, XH, 0),
                  (dqT, NH, 0), (xoT, XH, 0)]
        S_GELU, S_GLU, S_NSA, S_RET, S_NA, S_X, S_DIF = 0, 1, 2, 3, 4, (5, 7), 6

        def split_steps(upto):
            return sum(n // 4 for _, n, _ in SPLITS[:upto])

        block = ctx.enter_context(nc.Block())

        @block.sync
        def _(sp):
            sp.dma_start(hs, a["mem_2"][0].rearrange("(m p) d -> p m d", p=P)).then_inc(mem_landed, 16)
            sp.dma_start(xtok[:, :, :], a["x"][0].rearrange("(m p) d -> p m d", p=P)).then_inc(x_landed, 16)

            def fetch(src, ph, slot, number, first):
                if first >= SLOTS:
                    sp.wait_ge(l_made, number * 2 - 2 * (SLOTS - 1))
                dst = ring[:, slot, :]
                if ph is not None:
                    dst = dst.rearrange("p (t n) -> p t n", t=ph)
                sp.dma_start(dst, src).then_inc(landed[slot], 16)

            def stream(ph):
                with rep(sp, ph.iters) as i:
                    for c in range(ph.body):
                        for b in range(ph.blocks):
                            n = ph.block(c, b)
                            fetch(ph.src(i, c, b), ph.kt, n % SLOTS, ph.blocks_before(i, c, b), n)

            def stream_w1(ph, w):
                for b in range(2):
                    n = ph.block0 + b
                    fetch(w.rearrange("(j p) n -> p j n", p=P)[:, b * 16:(b + 1) * 16, :], 16, n % SLOTS, n, n)

            for l in range(DEPTH):
                for ph in kv_mem[l]:
                    stream(ph)
            for ph in (s5_u, s5_z, s5_glu, s5_out, *kv):
                stream(ph)
            stream_w1(cmp_w1[0], a["cmp_w1_k"])
            stream_w1(cmp_w1[1], a["cmp_w1_v"])
            for hh in range(2):
                for ph in (b_q[hh], *b_z[hh]):
                    stream(ph)
            for ph in (b_out, ab_rq, ab_rk, ab_rv, ab_rg, ab_nq, ab_nk, ab_nv, ab_out):
                stream(ph)

            def stream_tail(l):
                xq, xo, parts = layers[l]
                stream(xq)
                stream(xo)
                for ffn_in, ffn_out in parts:
                    stream(ffn_in)
                    stream(ffn_out)

            stream_tail(0)
            for ph in (c_qk, c_v, c_out):
                stream(ph)
            stream_tail(1)
            await_chunks(sp, layers[1][2][-1][1])
            sp.dma_start(out[0].rearrange("(m p) d -> p m d", p=P), xtok[:, :, :]).then_inc(out_done, 16)
            sp.wait_ge(out_done, 16)

        @block.gpsimd
        def _(pool):
            chain = Chain(pool, pool_step)

            rows = [
                (rowsA[A_RE:A_RE + 32, :], a["a_lam_re"][0].rearrange("(j h) p -> j (h p)", h=2)),
                (rowsA[A_IM:A_IM + 32, :], a["a_lam_im"][0].rearrange("(j h) p -> j (h p)", h=2)),
                (rowsA[A_D:A_D + 8, :], a["a_d"][0].rearrange("(j p) -> j p", p=P)),
                (rowsA[A_BGLU:A_BGLU + 8, :], a["a_b_glu"][0].rearrange("(j p) -> j p", p=P)),
                (rowsA[C_RET:C_RET + 1, :], a["ret_out_g_2"]),
                (rowsA[C_NAQ:C_NAQ + 1, :], a["na_q_g_2"]),
                (rowsA[C_NAK:C_NAK + 1, :], a["na_k_g_2"]),
                (rowsA[C_DQ:C_DQ + 1, :], a["diff_q_g_2"]),
                (rowsA[C_DK:C_DK + 1, :], a["diff_k_g_2"]),
                (rowsA[C_DO:C_DO + 2, :], a["diff_out_g_2"][0].rearrange("(j p) -> j p", p=P)),
                (rowsA[C_XQ:C_XQ + 2, :], a["xq_g_2"]),
                (rowsA[C_XK:C_XK + 2, :], a["xk_g_2"]),
                (rowsA[C_LAM:C_LAM + 1, :], a["lambda_q1_2"]),
                (rowsA[C_LAM + 1:C_LAM + 2, :], a["lambda_k1_2"]),
                (rowsA[C_LAM + 2:C_LAM + 3, :], a["lambda_q2_2"]),
                (rowsA[C_LAM + 3:C_LAM + 4, :], a["lambda_k2_2"]),
                (rowsA[C_LAM + 4:C_LAM + 5, :], a["lambda_k2_2"]),
                (rowsC[0:BLOCK, :], a["cmp_pos_k"]),
                (rowsC[BLOCK:2 * BLOCK, :], a["cmp_pos_v"]),
                (w2[:, 0, :], a["cmp_w2_k"]),
                (w2[:, 1, :], a["cmp_w2_v"]),
                (decay[:, 0, 0:8], a["ret_decay_fwd_2"].partition_broadcast(P).rearrange("p o h -> p (o h)")),
                (decay[:, 0, 8:16], a["ret_decay_bwd_2"].partition_broadcast(P).rearrange("p o h -> p (o h)")),
            ]
            for k, name in enumerate(("norm_mix_g_2", "norm_xattn_g_2", "norm_mem_g_2", "norm_ffn_g_2")):
                rows.append((rowsB[32 * k:32 * k + 32, :], a[name].rearrange("l (j p) -> (l j) p", p=P)))
            pool.dma_start(ldt2[64:96, :], a["a_log_dt"][0].rearrange("(j h) -> j h", h=2)).then_inc(ldt_landed, 16)
            for dst, src in rows:
                pool.dma_start(dst, src).then_inc(consts_landed, 16)
            assert len(rows) == N_CONST

            for ap, value in ((ident[:, :], 0.0), (flip[:, :], 0.0), (mean_of[:, :], 1.0 / P), (consts[:, 0:1], RMS_EPS),
                              (consts[:, 1:2], LN_EPS), (consts[:, 2:3], math.pi / 2), (consts[:, 3:4], 1.0),
                              (cmp_mask[:, :, :], 0.0), (row_ok[:, :], 1.0),
                              (col_mask[:, :], 0.0), (group_mask[:, 0, :], 1.0), (group_mask[:, 1, :], -1.0),
                              (rpb_pad[:, :], 0.0)):
                chain.add(pool.memset(ap, value))
            chain.settle()
            pool.affine_select(out=ident[:, :], in_=ident[:, :], compare_op=ALU.not_equal, fill=1.0, base=0,
                               pattern=[[-1, P]], channel_multiplier=1).then_inc(ident_made, 1)
            for at in (GRID - 1, 3 * GRID - 1):
                chain.add(pool.affine_select(out=flip[:, :], in_=flip[:, :], compare_op=ALU.not_equal, fill=1.0,
                                             base=-at, pattern=[[1, P]], channel_multiplier=1))
                chain.settle()
            pool.dma_start(rpb_pad[:, GRID - WIN_C:GRID - WIN_C + RPB_C],
                           a["na_rpb_2"][0].rearrange("h r c -> (h r) c")).then_inc(pad_landed, 16)
            chain.add(pool.affine_select(out=cmp_mask[:, :, :], in_=cmp_mask[:, :, :], compare_op=ALU.is_ge,
                                         fill=NEG, base=-(BLOCK - 1), pattern=[[P, MT], [-STRIDE, NCMP]],
                                         channel_multiplier=1))
            chain.add(pool.affine_select(out=row_ok[:, :], in_=row_ok[:, :], compare_op=ALU.is_ge, fill=0.0,
                                         base=-(BLOCK - 1), pattern=[[P, MT]], channel_multiplier=1))
            for s in range(2):
                chain.add(pool.affine_select(out=group_mask[:, s, :], in_=group_mask[:, s, :],
                                             compare_op=ALU.is_ge, fill=0.0, base=0, pattern=[[-GROUP, 8]],
                                             channel_multiplier=1))
            chain.settle()
            for s in range(2):
                chain.add(pool.affine_select(out=group_mask[:, s, :], in_=group_mask[:, s, :],
                                             compare_op=ALU.is_ge, fill=0.0, base=GROUP - 1,
                                             pattern=[[GROUP, 8]], channel_multiplier=-1))
            chain.settle()
            edge = GRID - WIN_C
            for q in range(2):
                m = col_mask[GRID * q:GRID * (q + 1), :]
                chain.add(pool.affine_select(out=m[:, 0:edge], in_=m[:, 0:edge], compare_op=ALU.is_ge, fill=NEG,
                                             base=WIN_C // 2, pattern=[[1, edge]], channel_multiplier=-1))
                chain.settle()
            for q in range(2):
                m = col_mask[GRID * q:GRID * (q + 1), WIN_C:GRID]
                chain.add(pool.affine_select(out=m, in_=m, compare_op=ALU.is_ge, fill=NEG,
                                             base=WIN_C // 2 - 1 - WIN_C, pattern=[[-1, edge]],
                                             channel_multiplier=1))
                chain.settle()
            chain.add(pool.iota(time_row, [[1, T]], base=0, channel_multiplier=0,
                                allow_small_or_imprecise_dtypes=True))
            chain.settle()
            pool.engine_nop().then_inc(masks_made, 1)
            pool.wait_ge(pad_landed, 16)
            pool.dma_start(rpb_dram, rpb_pad[:, :]).then_inc(pad_stored, 16)

            await_chunks(pool, kv_mem[1][1])
            pool.wait_ge(normed, len(norm_mem))
            for k, name in enumerate(("a_b_re", "a_b_im")):
                pool.dma_start(b_raw[:, k, :].rearrange("p (j c) -> p j c", c=GROUP),
                               a[name][0].rearrange("(j h) q c -> (h q) j c", h=2)).then_inc(b_landed, 16)
            for k, name in enumerate(("a_c_re", "a_c_im")):
                pool.dma_start(c_raw[:, k, :].rearrange("p (f q) -> p f q", q=STATES),
                               a[name][0].rearrange("(f g) c q -> (g c) f q", f=8)).then_inc(b_landed, 16)

            def load_ln(l):
                for k, name in enumerate(("ln_g", "ln_b")):
                    pool.dma_start(ln_rows[:, k, :],
                                   a[name][l:l + 1, :].partition_broadcast(P).rearrange("p o d -> p (o d)"))\
                        .then_inc(ln_landed, 16)

            pool.wait_ge(act_l, split_steps(S_GLU + 1))
            chain.add(pool.memset(causal[:, :, :], 0.0))
            chain.settle()
            pool.affine_select(out=causal[:, :, :], in_=causal[:, :, :], compare_op=ALU.is_ge, fill=NEG, base=0,
                               pattern=[[P, MT], [-1, T]], channel_multiplier=1).then_inc(causal_made, 1)
            load_ln(0)
            pool.dma_start(gate_w, a["b_w_in"][0, :, NH * DH * (1 + BRANCHES):].rearrange(
                "(t p) n -> p t n", p=P)).then_inc(gate_w_landed, 16)

            for hh in range(2):
                for r in range(1, BRANCHES):
                    for u in nsa[hh][r]:
                        pool.wait_ge(o_used, u["group"] + 1)
                        pool.tensor_tensor(oT[:, u["h"], :], oT[:, u["h"], :], zT[:, u["h8"], :], ALU.add)\
                            .then_inc(branch_summed, 1)
            chain.add(pool.iota(later[:, :, :], [[-P, MT], [1, T]], base=0, channel_multiplier=-1,
                                allow_small_or_imprecise_dtypes=True))
            chain.settle()
            chain.add(pool.tensor_scalar(earlier[:, :, :], later[:, :, :], -1.0, 0.0, ALU.mult, ALU.max))
            chain.settle()
            pool.tensor_scalar(later[:, :, :], later[:, :, :], 0.0, None, ALU.max).then_inc(lags_made, 1)
            pool.wait_ge(act_l, split_steps(S_NSA + 1))
            load_ln(1)

            pool.wait_ge(pad_stored, 16)
            pool.wait_ge(ro_copied, H8)
            for r in range(ROWS):
                for h in range(H8):
                    src = bass.AP(tensor=rpb_dram.tensor,
                                  offset=(h * RPB_R + WIN_R - 1 - r) * P,
                                  ap=[[1, GRID], [P, ROWS], [1, GRID]])
                    q = r % 2
                    dst = table[GRID * q:GRID * (q + 1), h, (r // 2) * T:(r // 2 + 1) * T]
                    pool.dma_start(dst.rearrange("p (r c) -> p r c", c=GRID), src).then_inc(bias_landed, 16)

        @block.tensor
        def _(pe):
            def turn(call, src):
                for k in range(FT // 2):
                    n = 8 * call + k
                    if n >= IN_FLIGHT:
                        pe.wait_ge(turned_l, 2 * (n - IN_FLIGHT + 1))
                    bank = turn_banks[n % IN_FLIGHT]
                    for f in range(2):
                        for m in range(MT):
                            ins = pe.transpose(bank[:, (f * MT + m) * P:(f * MT + m + 1) * P],
                                               src[:, m, (2 * k + f) * P:(2 * k + f + 1) * P], ident[:, :])
                    ins.then_inc(turned, 1)

            def dense(ph):
                xH, xL = (hidH, hidL) if ph.hidden else (actH, actL)
                with rep(pe, ph.iters) as i:
                    for c in range(ph.body):
                        if ph.chunk0 + c >= 2:
                            pe.wait_ge(drained[ph.pair(c)], ph.pair_uses(i, c))
                        pair = acc[:, 2 * ph.pair(c):2 * ph.pair(c) + 2, :]
                        for b in range(ph.blocks):
                            pe.wait_ge(l_made, ph.blocks_before(i, c, b) * 2 + 2)
                            s = ph.block(c, b) % SPLIT_SLOTS
                            high, low = (w[:, s, :].rearrange("p (t n) -> p t n", t=ph.kt) for w in (wH, wL))
                            if ph.style == "tok":
                                last_k = ph.blocks * ph.kt - 1
                                for t in range(ph.kt):
                                    k = b * ph.kt + t
                                    for m in range(MT):
                                        rows = slice(m * P, (m + 1) * P)
                                        for n, (x, w) in enumerate(((xH, high), (xH, low), (xL, high))):
                                            ins = pe.matmul(pair[:, m, :], x[:, k, rows], w[:, t, :],
                                                            start=k == 0 and n == 0, stop=k == last_k and n == 2)
                            else:
                                for f in range(ph.cols // P):
                                    dst = pair[:, 0, (b + f) * T:(b + f + 1) * T]
                                    for t in range(ph.kt):
                                        for n, (x, w) in enumerate(((xH, high), (xL, high), (xH, low))):
                                            ins = pe.matmul(dst, w[:, t, f * P:(f + 1) * P], x[:, t, :],
                                                            start=t == 0 and n == 0,
                                                            stop=t == ph.kt - 1 and n == 2)
                            ins.then_inc(blocks_done, 1)

            def head_means(part):
                for u in part:
                    n = u["n"]
                    pe.wait_ge(sq_ready, n + 1)
                    if n >= 2:
                        pe.wait_ge(hroot_ready, n - 1)
                    sq = score[:, n % 2, :]
                    if u["wide"]:
                        pe.matmul(psA[:, n % 2, 0:T], mean_of[:, :], sq[:, 0:T], start=True, stop=False)
                        ins = pe.matmul(psA[:, n % 2, 0:T], mean_of[:, :], sq[:, T:2 * T], start=False, stop=True)
                    else:
                        ins = pe.matmul(psA[:, n % 2, :], mean_of[:, :], sq, start=True, stop=True)
                    ins.then_inc(mean_ready, 1)

            def attend(part):
                for t in range(len(part) + 2):
                    if t < len(part):
                        u = part[t]
                        n = u["n"]
                        if n >= 2:
                            pe.wait_ge(biased, n - 1)
                        for m in range(MT):
                            ins = pe.matmul(psA[:, n % 2, m * T:m * T + u["K"]], u["q"][:, m * P:(m + 1) * P],
                                            u["k"], start=True, stop=True)
                        ins.then_inc(scores_ready, 1)
                    if 0 <= t - 1 < len(part):
                        u = part[t - 1]
                        n, K = u["n"], u["K"]
                        pe.wait_ge(probs_ready, n + 1)
                        if n >= 1:
                            pe.wait_ge(probT_ready, n)
                        for m in range(MT):
                            for kt in range(-(-K // P)):
                                w = min(P, K - kt * P)
                                ins = pe.transpose(psB[0:w, kt * T + m * P:kt * T + (m + 1) * P],
                                                   score[:, n % 2, m * T + kt * P:m * T + kt * P + w],
                                                   ident[:, :])
                        ins.then_inc(probs_turned, 1)
                    if 0 <= t - 2 < len(part):
                        u = part[t - 2]
                        n, K = u["n"], u["K"]
                        pe.wait_ge(probT_ready, n + 1)
                        if u["first"] and u["group"] >= 1:
                            pe.wait_ge(o_used, u["group"])
                        kts = -(-K // P)
                        for o in range(u["halves"]):
                            for kt in range(kts):
                                w = min(P, K - kt * P)
                                ins = pe.matmul(psC[:, o * T:(o + 1) * T], u["v"](kt, o),
                                                probT[0:w, n % 2, kt * T:(kt + 1) * T],
                                                start=u["first"] and kt == 0 and o == 0,
                                                stop=u["last"] and kt == kts - 1,
                                                skip_group_check=u["halves"] == 2)
                        ins.then_inc(o_ready, 1)

            pe.wait_ge(ident_made, 1)
            pe.wait_ge(consts_landed, 16 * N_CONST)
            pe.wait_ge(s5_dt, 1)
            pe.transpose(psA[:, 0, 0:P], rowsA[:, :], ident[:, :])
            pe.transpose(psA[:, 1, 0:P], rowsB[:, :], ident[:, :])
            pe.transpose(psB[:, 0:64], rowsC[:, :], ident[0:64, 0:64]).then_inc(cols_turned, 1)
            pe.wait_ge(lam_prod, 1)
            pe.wait_ge(masks_made, 1)
            pe.matmul(psC[:, 0:2], mean_of[:, :], lam[:, 0:2], start=True, stop=True).then_inc(lam_sum, 1)

            pe.wait_ge(cols_copied, 3)
            pe.wait_ge(lam_exp, 1)
            pe.wait_ge(scaled, 2 * SCALED[RMS_MEM])
            for l in range(DEPTH):
                turn(TURN_MEM[l], hs)
                await_turn(pe, TURN_MEM[l])
                for ph in kv_mem[l]:
                    dense(ph)
            pe.wait_ge(x_landed, 16)
            turn(TURN_X, xtok)
            await_turn(pe, TURN_X)
            head_means(norm_mem)

            dense(s5_u)
            dense(s5_z)
            await_chunks(pe, s5_z)

            def s5_tile(i):
                pe.wait_ge(z_written, i * 6 + 6)
                wait_past(pe, z_copied, i * 2)
                wait_past(pe, y_summed, i)
                for z in range(8):
                    ins = pe.transpose(psA[:, z // 4, (z % 4) * P:(z % 4 + 1) * P], ZB[:, z, :], ident[:, :])
                ins.then_inc(z_turned, 1)
                for z in range(8):
                    bank = (psB, psC)[z // 4]
                    ins = pe.transpose(bank[:, (z % 4) * P:(z % 4 + 1) * P], ZC[:, z, :], ident[:, :])
                ins.then_inc(z_turned, 1)
                pe.wait_ge(z_copied, i * 2 + 1)
                wait_past(pe, bu_read, i * 4)
                for s in range(2):
                    for j in range(4):
                        ins = pe.matmul(acc[:, 2 * s + j // 2, (j % 2) * T:(j % 2 + 1) * T], BT[:, 4 * s + j, :],
                                        uT[:, bass.ts(i, 1), :].rearrange("p a t -> p (a t)"),
                                        start=True, stop=True)
                ins.then_inc(bu_ready, 1)
                pe.wait_ge(z_copied, i * 2 + 2)
                pe.wait_ge(h_ready, i * 2 + 2)
                for s, hx in enumerate((s5_hr, s5_hi)):
                    for j in range(4):
                        ins = pe.matmul(psB[:, 0:T], CT[:, 4 * s + j, :], hx[:, j, :],
                                        start=s == 0 and j == 0, stop=s == 1 and j == 3)
                ins.then_inc(y_ready, 1)

            peeled(pe, SSM_TILES, s5_tile)
            pe.wait_ge(act_l, split_steps(S_GELU + 1))
            dense(s5_glu)
            pe.wait_ge(act_l, split_steps(S_GLU + 1))
            dense(s5_out)
            pe.wait_ge(ln_done, 1)
            turn(TURN_LN1, xtok)
            await_turn(pe, TURN_LN1)

            for ph in kv:
                dense(ph)
            await_chunks(pe, kv[5])
            pe.wait_ge(pos_ready, 4)
            for s, (ph, src) in enumerate(zip(cmp_w1, (kcT, vcT))):
                for b in range(ph.blocks):
                    n = ph.block0 + b
                    pe.wait_ge(l_made, 2 * n + 2)
                    for j in range(16):
                        at = 16 * b + j
                        for part, w in enumerate((wH, wL)):
                            w1 = w[:, n % SPLIT_SLOTS, j * P:(j + 1) * P].bitcast(F32)
                            ins = pe.matmul(psA[:, s, 0:(KVH + 1) * NCMP], w1,
                                            src[:, :, at:at + (NCMP - 1) * STRIDE + 1:STRIDE],
                                            start=at == 0 and part == 0, stop=at == BLOCK - 1 and part == 1)
                    ins.then_inc(blocks_done, 1)
            pe.wait_ge(gate_w_landed, 16)
            for m in range(MT):
                for k in range(FT):
                    for part, x in enumerate((actH, actL)):
                        ins = pe.matmul(psB[:, m * NGATE:(m + 1) * NGATE],
                                        x[:, k, m * P:(m + 1) * P].bitcast(F32), gate_w[:, k, :],
                                        start=k == 0 and part == 0, stop=k == FT - 1 and part == 1)
            ins.then_inc(gate_sum, 1)
            pe.wait_ge(cmp_hid_ready, 2)
            pe.matmul(psC[:, 0:KVH * NCMP], w2[:, 0, :], cmp_hid[:, 0, :], start=True, stop=True)\
                .then_inc(cmp_out, 1)
            pe.wait_ge(cmp_ready, 1)
            for g in range(KVH):
                ins = pe.matmul(psC[0:NCMP, g * DH:(g + 1) * DH], cmp_hid[:, 1, g * NCMP:(g + 1) * NCMP],
                                w2[:, 1, :], start=True, stop=True)
            ins.then_inc(cmp_out, 1)
            pe.wait_ge(cmp_ready, 2)
            pe.wait_ge(gate_ready, 3)
            for hh in range(2):
                dense(b_q[hh])
                await_chunks(pe, b_q[hh])
                for r in range(BRANCHES):
                    dense(b_z[hh][r])
                    attend(nsa[hh][r])
            pe.wait_ge(act_l, split_steps(S_NSA + 1))
            dense(b_out)

            pe.wait_ge(scaled, 2 * SCALED[RMS_MIX[0]])
            turn(TURN_MIX[0], hs)
            await_turn(pe, TURN_MIX[0])
            for ph in (ab_rq, ab_rk, ab_rv, ab_rg):
                dense(ph)
            await_chunks(pe, ab_rg)
            for t in range(H8 + 1):
                if t < H8:
                    if t >= 2:
                        pe.wait_ge(rs_decayed, t - 1)
                    for m in range(MT):
                        ins = pe.matmul(psA[:, t % 2, m * T:(m + 1) * T], rkT[:, t, m * P:(m + 1) * P],
                                        rqT[:, t, :], start=True, stop=True)
                    ins.then_inc(rs_ready, 1)
                if t >= 1:
                    h = t - 1
                    pe.wait_ge(rs_decayed, h + 1)
                    if h >= 1:
                        pe.wait_ge(ro_copied, h)
                    for m in range(MT):
                        ins = pe.matmul(psC[:, 0:T], rv[:, m, h * DH:(h + 1) * DH],
                                        score[:, h % 2, m * T:(m + 1) * T], start=m == 0, stop=m == MT - 1)
                    ins.then_inc(ro_ready, 1)
            head_means(norm_ret)
            for ph in (ab_nq, ab_nk, ab_nv):
                dense(ph)
            await_chunks(pe, ab_nv)
            head_means(norm_na)
            pe.wait_ge(normed, norm_na[-1]["n"] + 1)
            pe.wait_ge(bias_landed, 16 * ROWS * H8)
            for h in range(H8):
                if h >= 2:
                    pe.wait_ge(bias_masked, h - 1)
                pe.matmul(psA[:, h % 2, :], flip[:, :], table[:, h, :], start=True, stop=True)\
                    .then_inc(bias_turned, 1)
            pe.wait_ge(bias_masked, H8)
            attend(na)
            pe.wait_ge(act_l, split_steps(S_NA + 1))
            dense(ab_out)

            def tail_pe(l):
                xq, xo, parts = layers[l]
                pe.wait_ge(scaled, 2 * SCALED[RMS_XA[l]])
                turn(TURN_XA[l], hs)
                await_turn(pe, TURN_XA[l])
                dense(xq)
                head_means(norm_x[l])
                pe.wait_ge(normed, norm_x[l][-1]["n"] + 1)
                attend(xat[l])
                pe.wait_ge(act_l, split_steps(S_X[l] + 1))
                dense(xo)
                pe.wait_ge(scaled, 2 * SCALED[RMS_FFN[l]])
                turn(TURN_FFN[l], hs)
                await_turn(pe, TURN_FFN[l])
                for k, (ffn_in, ffn_out) in enumerate(parts):
                    dense(ffn_in)
                    pe.wait_ge(hid_l, (l * FFN_T + sum(FFN_PARTS[:k + 1])) // 2)
                    dense(ffn_out)

            tail_pe(0)

            pe.wait_ge(scaled, 2 * SCALED[RMS_MIX[1]])
            turn(TURN_MIX[1], hs)
            await_turn(pe, TURN_MIX[1])
            dense(c_qk)
            dense(c_v)
            await_chunks(pe, c_v)
            head_means(norm_c)
            pe.wait_ge(normed, norm_c[-1]["n"] + 1)
            attend(dif)
            head_means(norm_do)
            pe.wait_ge(act_l, split_steps(S_DIF + 1))
            dense(c_out)
            tail_pe(1)

        @block.scalar
        def _(act):
            chain = Chain(act, act_step)

            def root_of_mean_square(call, eps):
                act.wait_ge(ms_ready, call + 1)
                act.activation(root[:, :], mean_sq[:, :], ACT.Sqrt, bias=consts[:, eps:eps + 1])\
                    .then_inc(root_ready, 1)

            def rms_rows(call, src):
                root_of_mean_square(call, 0)
                act.wait_ge(rstd_ready, call + 1)
                act.activation(hs[:, 1, :], src[:, 1, :], ACT.Identity, scale=rstd[:, 1:2]).then_inc(scaled, 1)

            def turn_out(call, gain=None):
                for n in range(8 * call, 8 * call + 8):
                    act.wait_ge(turned, n + 1)
                    for f in range(2):
                        bank = turn_banks[n % IN_FLIGHT][:, f * T:(f + 1) * T]
                        k = 2 * (n - 8 * call) + f
                        scale = 1.0 if gain is None else colsB[:, gain + k:gain + k + 1]
                        act.activation(actH[:, k, :], bank, ACT.Identity, scale=scale).then_inc(turned_h, 1)

            def split(which):
                src, n, first = SPLITS[which]
                for k in range(0, n, 4):
                    act.activation(actH[:, first + k:first + k + 4, :], src[:, k:k + 4, :], ACT.Identity)\
                        .then_inc(act_h, 1)

            def split_weights(slot, split_slot, number, landings, first):
                act.wait_ge(landed[slot], landings)
                if first >= SPLIT_SLOTS:
                    act.wait_ge(blocks_done, number - (SPLIT_SLOTS - 1))
                for k in range(2):
                    cols = slice(k * HALF, (k + 1) * HALF)
                    act.copy(wH[:, split_slot, cols], ring[:, slot, cols]).then_inc(h_made, 1)

            def split_at(n):
                split_weights(n % SLOTS, n % SPLIT_SLOTS, n, 16 * (n // SLOTS + 1), n)

            def dense(ph, fn=None, only=None):
                with rep(act, ph.iters) as i:
                    for c in range(ph.body):
                        for b in range(ph.blocks):
                            n = ph.block(c, b) + 1
                            if n < plan["blocks"]:
                                split_weights(n % SLOTS, n % SPLIT_SLOTS, ph.blocks_before(i, c, b) + 1,
                                              i * (16 * ph.body * ph.blocks // SLOTS) + 16 * (n // SLOTS + 1), n)
                        if fn is not None and (only is None or c in only):
                            drain_chunk(act, ph, i, c, fn)

            def head_roots(part):
                for t in range(len(part) + 1):
                    if t < len(part):
                        u = part[t]
                        n = u["n"]
                        if n >= 2:
                            act.wait_ge(mean_ready, n - 1)
                        act.activation(score[:, n % 2, :], u["x"].rearrange("p a t -> p (a t)"), ACT.Square)\
                            .then_inc(sq_ready, 1)
                    if t >= 1:
                        u = part[t - 1]
                        n = u["n"]
                        w = T if u["wide"] else 2 * T
                        act.wait_ge(mean_ready, n + 1)
                        if n >= 2:
                            act.wait_ge(normed, n - 1)
                        act.activation(probT[:, n % 2, 0:w], psA[:, n % 2, 0:w], ACT.Sqrt,
                                       bias=consts[:, 0:1], scale=0.5 if u["wide"] else 1.0)\
                            .then_inc(hroot_ready, 1)

            def attend(part):
                for t in range(len(part) + 1):
                    if t < len(part):
                        u = part[t]
                        n = u["n"]
                        act.wait_ge(max_ready, n + 1)
                        for m in range(MT):
                            s = score[:, n % 2, m * T:m * T + u["K"]]
                            act.activation(s, s, ACT.Exp, bias=neg_max[:, n % 2, m:m + 1],
                                           scale=SCALE if u["mode"] == "alibi" else 1.0,
                                           accum_out=denom[:, n % 2, m:m + 1]).then_inc(exp_ready, 1)
                    if t >= 1:
                        u = part[t - 1]
                        n, K = u["n"], u["K"]
                        act.wait_ge(probs_turned, n + 1)
                        if n >= 2:
                            act.wait_ge(o_ready, n - 1)
                        w = min(K, P)
                        size = T * -(-K // P)
                        act.copy(probT[0:w, n % 2, 0:size], psB[0:w, 0:size]).then_inc(probT_ready, 1)

            split_at(0)
            act.wait_ge(cols_turned, 1)
            act.copy(colsA[:, :], psA[:, 0, 0:P]).then_inc(cols_copied, 1)
            act.copy(colsB[:, :], psA[:, 1, 0:P]).then_inc(cols_copied, 1)
            act.copy(colsC[:, :], psB[:, 0:64]).then_inc(cols_copied, 1)
            act.wait_ge(lam_sum, 1)
            act.activation(lam[:, 2:4], psC[:, 0:2], ACT.Exp, scale=float(P)).then_inc(lam_exp, 1)
            act.wait_ge(lg_abs, 1)
            chain.add(act.activation(decay[:, 2, :], decay[:, 2, :], ACT.Exp, scale=-1.0))
            chain.settle()
            act.activation(decay[:, 2, :], decay[:, 2, :], ACT.Ln, bias=consts[:, 3:4]).then_inc(lg_ln, 1)
            act.wait_ge(cols_copied, 3)
            chain.add(act.activation(ssm[:, 0, :], colsA[:, A_DT:A_DT + 32], ACT.Exp))
            chain.settle()
            act.wait_ge(s5_exp, 1)
            act.activation(ssm[:, 1, :], ssm[:, 1, :], ACT.Exp).then_inc(s5_exp, 1)
            act.wait_ge(s5_frac0, 1)
            act.activation(ssm[:, 4, :], ssm[:, 3, :], ACT.Sin, scale=TURN).then_inc(s5_trig0, 1)
            chain.add(act.activation(ssm[:, 5, :], ssm[:, 3, :], ACT.Abs))
            chain.settle()
            act.activation(ssm[:, 5, :], ssm[:, 5, :], ACT.Sin, scale=-TURN, bias=consts[:, 2:3])\
                .then_inc(s5_trig0, 1)

            rms_rows(RMS_MEM, hs)
            for l in range(DEPTH):
                turn_out(TURN_MEM[l], G_MEM + 16 * l)
                for ph in kv_mem[l]:
                    dense(ph)
            turn_out(TURN_X)
            await_chunks(act, kv_mem[1][1])
            head_roots(norm_mem)

            dense(s5_u)
            dense(s5_z, lambda i, c, src: act.activation(
                zT5[:, bass.ds(i * 4 + 2 * c, 2), :], src, ACT.Silu))

            def s5_tile(i):
                act.wait_ge(z_turned, i * 2 + 1)
                wait_past(act, bu_ready, i)
                act.copy(BT, psA[:, :, :].rearrange("p a (b s) -> p (a b) s", s=P)).then_inc(z_copied, 1)
                act.wait_ge(z_turned, i * 2 + 2)
                wait_past(act, y_ready, i)
                act.copy(CT[:, 0:4, :], psB[:, :].rearrange("p (b s) -> p b s", s=P)).then_inc(act_step, 1)
                act.wait_ge(act_step, i * 2 + (chain.n + 1))
                act.copy(CT[:, 4:8, :], psC[:, :].rearrange("p (b s) -> p b s", s=P)).then_inc(z_copied, 1)
                act.wait_ge(phase_ready, i + 1)
                wait_past(act, h_ready, i * 2)
                act.activation(s5_sin, s5_frac, ACT.Sin, scale=TURN).then_inc(trig_ready, 1)
                act.activation(s5_cos, s5_frac, ACT.Abs).then_inc(act_step, 1)
                act.wait_ge(act_step, i * 2 + (chain.n + 2))
                act.activation(s5_cos, s5_cos, ACT.Sin, scale=-TURN, bias=consts[:, 2:3]).then_inc(trig_ready, 1)

            peeled(act, SSM_TILES, s5_tile)
            chain.n += 2 * SSM_TILES
            act.wait_ge(y_summed, SSM_TILES)
            act.activation(gT, gT, ACT.Gelu_apprx_tanh).then_inc(gelu_done, 1)

            act.wait_ge(gelu_done, 1)
            split(S_GELU)

            def glu_gate(i, c, src):
                for f in range(2):
                    ft = 2 * c + f
                    ins = act.activation(glT[:, ft, :], src[:, f, :], ACT.Sigmoid,
                                         bias=colsA[:, A_BGLU + ft:A_BGLU + ft + 1])
                    if f == 0:
                        chain.add(ins)
                        chain.settle()
                return ins

            dense(s5_glu, glu_gate)
            act.wait_ge(glu_mixed, 1)
            split(S_GLU)
            dense(s5_out)
            root_of_mean_square(LN1, 1)
            turn_out(TURN_LN1)

            for ph in kv:
                dense(ph)
            for ph in cmp_w1:
                for b in range(ph.blocks):
                    split_at(ph.block0 + b + 1)
            for s in range(2):
                act.wait_ge(cmp_bias_ready, s + 1)
                act.activation(cmp_hid[:, s, :], psA[:, s, 0:KVH * NCMP], ACT.Gelu_apprx_tanh,
                               bias=cmp_bias[:, s:s + 1]).then_inc(cmp_hid_ready, 1)
            act.wait_ge(gate_sum, 1)
            act.activation(gates[:, :, :], psB[:, 0:MT * NGATE].rearrange("p (m n) -> p m n", m=MT),
                           ACT.Sigmoid).then_inc(gate_ready, 1)
            for hh in range(2):
                dense(b_q[hh])
                for r in range(BRANCHES):
                    if r == 1:
                        act.wait_ge(o_used, nsa[hh][0][-1]["group"] + 1)
                    elif hh or r:
                        act.wait_ge(branch_summed, NH * hh + (NH // 2) * (r == 2))
                    dense(b_z[hh][r], lambda i, c, src: act.activation(
                        zT[:, bass.ds(i * 4 + 2 * c, 2), :], src, ACT.Silu))
                    attend(nsa[hh][r])
            act.wait_ge(branch_summed, 2 * NH)
            split(S_NSA)
            dense(b_out)
            root_of_mean_square(LN2, 1)

            rms_rows(RMS_MIX[0], xtok)
            turn_out(TURN_MIX[0], G_MIX)
            for ph in (ab_rq, ab_rk, ab_rv):
                dense(ph)
            dense(ab_rg, lambda i, c, src: act.activation(rgT[:, bass.ds(i * 4 + 2 * c, 2), :], src, ACT.Silu))
            for h in range(H8):
                act.wait_ge(decay_arg, h + 1)
                act.activation(table[:, h, :], table[:, h, :], ACT.Exp).then_inc(decay_ready, 1)
            act.wait_ge(ro_copied, H8)
            head_roots(norm_ret)
            for ph in (ab_nq, ab_nk, ab_nv):
                dense(ph)
            await_chunks(act, ab_nv)
            head_roots(norm_na)
            attend(na)
            act.wait_ge(o_used, na[-1]["group"] + 1)
            split(S_RET)
            split(S_NA)
            dense(ab_out)

            def tail_act(l):
                xq, xo, parts = layers[l]
                rms_rows(RMS_XA[l], xtok)
                turn_out(TURN_XA[l], G_X + 16 * l)
                dense(xq)
                await_chunks(act, xq)
                head_roots(norm_x[l])
                attend(xat[l])
                act.wait_ge(o_used, xat[l][-1]["group"] + 1)
                split(S_X[l])
                dense(xo)
                rms_rows(RMS_FFN[l], xtok)
                turn_out(TURN_FFN[l], G_FFN + 16 * l)
                pairs_done = l * FFN_T // 2
                for ffn_in, ffn_out in parts:
                    def finish(i, c, src):
                        n = i + pairs_done
                        if c == 0:
                            wait_past(act, drained[ffn_in.pair(1)], ffn_in.pair_uses(i, 1))
                            act.activation(silu_g, src, ACT.Silu).then_inc(drained[ffn_in.pair(0)], 1)
                        else:
                            act.wait_ge(drained[ffn_in.pair(1)], ffn_in.pair_uses(i, 1) + 1)
                            act.activation(hidH[:, bass.ts(i, 2), :], hid_f, ACT.Identity).then_inc(hid_h, 1)

                    with rep(act, ffn_in.iters) as i:
                        for c in range(2):
                            for b in range(2):
                                n = ffn_in.block(c, b) + 1
                                split_weights(n % SLOTS, n % SPLIT_SLOTS, ffn_in.blocks_before(i, c, b) + 1,
                                              i * 16 + 16 * (n // SLOTS + 1), n)
                            act.wait_ge(blocks_done, ffn_in.blocks_before(i, c, 2))
                            finish(i, c, acc[:, 2 * ffn_in.pair(c), :].rearrange("p (f t) -> p f t", t=T))
                    pairs_done += ffn_in.iters
                    dense(ffn_out)

            tail_act(0)
            rms_rows(RMS_MIX[1], xtok)
            turn_out(TURN_MIX[1], G_MIX + 16)
            dense(c_qk)
            dense(c_v)
            await_chunks(act, c_v)
            head_roots(norm_c)
            attend(dif)
            act.wait_ge(o_used, dif[-1]["group"] + 1)
            head_roots(norm_do)
            act.wait_ge(normed, norm_do[-1]["n"] + 1)
            split(S_DIF)
            dense(c_out)
            tail_act(1)

        @block.vector
        def _(dve):
            chain = Chain(dve, dve_step)

            def mean_squares(call, src, centred):
                for m in range(MT):
                    for k in range(4):
                        chain.add(dve.bn_stats(stats[:, m, 6 * k:6 * k + 6], src[:, m, k * COLS:(k + 1) * COLS]))
                chain.settle()
                for m in range(MT):
                    chain.add(dve.bn_aggr(moments[:, m, :], stats[:, m, :]))
                chain.settle()
                mean, var = moments[:, :, 0:1].rearrange("p m o -> p (m o)"), \
                    moments[:, :, 1:2].rearrange("p m o -> p (m o)")
                if centred:
                    dve.tensor_copy(mean_sq[:, :], var).then_inc(ms_ready, 1)
                else:
                    chain.add(dve.tensor_tensor(mean_sq[:, :], mean, mean, ALU.mult))
                    chain.settle()
                    dve.tensor_tensor(mean_sq[:, :], mean_sq[:, :], var, ALU.add).then_inc(ms_ready, 1)
                dve.wait_ge(root_ready, call + 1)
                dve.reciprocal(rstd[:, :], root[:, :]).then_inc(rstd_ready, 1)
                dve.wait_ge(rstd_ready, call + 1)

            def rms_rows(call, src):
                mean_squares(call, src, False)
                dve.tensor_scalar(hs[:, 0, :], src[:, 0, :], rstd[:, 0:1], None, ALU.mult).then_inc(scaled, 1)

            def layer_norm(call, l):
                mean_squares(call, xtok, True)
                dve.wait_ge(ln_landed, 32 * (l + 1))
                g, b = ln_rows[:, 0, :], ln_rows[:, 1, :]
                for m in range(MT):
                    chain.add(dve.tensor_scalar(xtok[:, m, :], xtok[:, m, :], moments[:, m, 0:1],
                                                rstd[:, m:m + 1], ALU.subtract, ALU.mult))
                for w, op in ((g, ALU.mult), (b, ALU.add)):
                    chain.settle()
                    for m in range(MT):
                        ins = dve.tensor_tensor(xtok[:, m, :], xtok[:, m, :], w, op)
                        if op == ALU.mult or m == 0:
                            chain.add(ins)
                chain.settle()
                ins.then_inc(ln_done, 1)
                dve.wait_ge(ln_done, l + 1)

            def turn_out(call, gain=None):
                for n in range(8 * call, 8 * call + 8):
                    dve.wait_ge(turned_h, 2 * n + 2)
                    for f in range(2):
                        bank = turn_banks[n % IN_FLIGHT][:, f * T:(f + 1) * T]
                        k = 2 * (n - 8 * call) + f
                        scale = 1.0 if gain is None else colsB[:, gain + k:gain + k + 1]
                        dve.scalar_tensor_tensor(out=actL[:, k, :], in0=bank, scalar=scale,
                                                 in1=actH[:, k, :].bitcast(F32), op0=ALU.mult,
                                                 op1=ALU.subtract).then_inc(turned_l, 1)

            def split(which):
                src, n, first = SPLITS[which]
                for k in range(0, n, 4):
                    dve.wait_ge(act_h, split_steps(which) + k // 4 + 1)
                    dve.tensor_tensor(actL[:, first + k:first + k + 4, :], src[:, k:k + 4, :],
                                      actH[:, first + k:first + k + 4, :].bitcast(F32), ALU.subtract)\
                        .then_inc(act_l, 1)

            def split_weights(slot, split_slot, number):
                for k in range(2):
                    cols = slice(k * HALF, (k + 1) * HALF)
                    dve.wait_ge(h_made, number * 2 + (k + 1))
                    dve.tensor_tensor(wL[:, split_slot, cols], ring[:, slot, cols],
                                      wH[:, split_slot, cols].bitcast(F32), ALU.subtract).then_inc(l_made, 1)

            def dense(ph, fn=None, only=None):
                with rep(dve, ph.iters) as i:
                    for c in range(ph.body):
                        for b in range(ph.blocks):
                            n = ph.block(c, b) + 1
                            if n < plan["blocks"]:
                                split_weights(n % SLOTS, n % SPLIT_SLOTS, ph.blocks_before(i, c, b) + 1)
                        if fn is not None and (only is None or c in only):
                            drain_chunk(dve, ph, i, c, fn)

            def head_norm(part):
                for u in part:
                    n = u["n"]
                    w = T if u["wide"] else 2 * T
                    r = probT[:, n % 2, 0:w]
                    dve.wait_ge(hroot_ready, n + 1)
                    chain.add(dve.reciprocal(r, r))
                    chain.settle()
                    if u["wide"]:
                        x = u["x"]
                        for o in range(2):
                            chain.add(dve.scalar_tensor_tensor(
                                out=x[:, o, :], in0=x[:, o, :], scalar=colsA[:, u["g"][o]:u["g"][o] + 1], in1=r,
                                op0=ALU.mult, op1=ALU.mult))
                        chain.settle()
                        dve.tensor_scalar(x, x, 1.0 - LAM_INIT, None, ALU.mult).then_inc(normed, 1)
                    else:
                        x = u["x"].rearrange("p a t -> p (a t)")
                        dve.scalar_tensor_tensor(out=x, in0=x, scalar=colsA[:, u["g"][0]:u["g"][0] + 1], in1=r,
                                                 op0=ALU.mult, op1=ALU.mult).then_inc(normed, 1)

            def attend(part):
                for t in range(len(part) + 3):
                    if t < len(part):
                        u = part[t]
                        n, K = u["n"], u["K"]
                        src = psA[:, n % 2, :].rearrange("p (m k) -> p m k", m=MT)[:, :, 0:K]
                        s = score[:, n % 2, :].rearrange("p (m k) -> p m k", m=MT)[:, :, 0:K]
                        dve.wait_ge(scores_ready, n + 1)
                        if n >= 2:
                            dve.wait_ge(probs_turned, n - 1)
                        if u["mode"] == "bias":
                            ins = dve.scalar_tensor_tensor(out=s, in0=src, scalar=SCALE, in1=u["bias"],
                                                           op0=ALU.mult, op1=ALU.add)
                        elif u["mode"] == "alibi":
                            ins = dve.scalar_tensor_tensor(out=s, in0=later[:, :, :], scalar=-u["bias"] / SCALE,
                                                           in1=src, op0=ALU.mult, op1=ALU.add)
                        else:
                            ins = dve.tensor_scalar(s, src, SCALE, None, ALU.mult)
                        ins.then_inc(biased, 1)
                        dve.wait_ge(biased, n + 1)
                        ins = dve.tensor_reduce(neg_max[:, n % 2, :], s, AX_X, ALU.max, negate=True)
                        if u["mode"] == "alibi":
                            chain.add(ins)
                            chain.settle()
                            ins = dve.tensor_scalar(neg_max[:, n % 2, :], neg_max[:, n % 2, :], SCALE, None,
                                                    ALU.mult)
                        ins.then_inc(max_ready, 1)
                    if 0 <= t - 1 < len(part):
                        u = part[t - 1]
                        n, K = u["n"], u["K"]
                        s = score[:, n % 2, :].rearrange("p (m k) -> p m k", m=MT)[:, :, 0:K]
                        f = factor[:, n % 2, :]
                        dve.wait_ge(exp_ready, MT * (n + 1))
                        chain.add(dve.tensor_scalar(f, denom[:, n % 2, :], 1e-30, None, ALU.max))
                        chain.settle()
                        chain.add(dve.reciprocal(f, f))
                        chain.settle()
                        if u["gate"] is not None:
                            chain.add(dve.tensor_tensor(f, f, u["gate"], ALU.mult))
                            chain.settle()
                        dve.tensor_tensor(s, s, f.unsqueeze(2).to_broadcast([P, MT, K]), ALU.mult)\
                            .then_inc(probs_ready, 1)
                    if 0 <= t - 3 < len(part) and part[t - 3]["last"]:
                        u = part[t - 3]
                        dve.wait_ge(o_ready, u["n"] + 1)
                        if u["fin"] == "gate":
                            dst = oT[:, u["h"], :] if u["r"] == 0 else zT[:, u["h8"], :]
                            ins = dve.tensor_tensor(dst, psC[:, 0:T], zT[:, u["h8"], :], ALU.mult)
                        elif u["halves"] == 2:
                            ins = dve.tensor_copy(u["to"], psC[:, :].rearrange("p (o t) -> p o t", o=2))
                        else:
                            ins = dve.tensor_copy(u["to"], psC[:, 0:T])
                        ins.then_inc(o_used, 1)

            def residual(ph, factor_):
                def add(i, c, src):
                    x = xtok[:, :, bass.ts(i * ph.body + c, ph.cols)]
                    if factor_ == 1.0:
                        return dve.tensor_tensor(x, x, src, ALU.add)
                    return dve.scalar_tensor_tensor(out=x, in0=x, scalar=factor_, in1=src, op0=ALU.mult,
                                                    op1=ALU.add)
                dense(ph, add)
                await_chunks(dve, ph)

            def keep(ph, dst):
                if ph.style == "feat":
                    dense(ph, lambda i, c, src: dve.tensor_copy(
                        dst[:, bass.ds(i * (2 * ph.body) + 2 * c, 2), :], src))
                else:
                    dense(ph, lambda i, c, src: dve.tensor_copy(
                        dst[:, :, bass.ds(i * (COLS * ph.body) + COLS * c, COLS)], src))

            split_weights(0, 0, 0)
            dve.wait_ge(ldt_landed, 16)
            dve.tensor_copy(rowsA[64:96, :].rearrange("j (h p) -> j h p", h=2),
                            ldt2[64:96, :].unsqueeze(2).to_broadcast([32, 2, STATES])).then_inc(s5_dt, 1)
            dve.wait_ge(cols_copied, 3)
            chain.add(dve.tensor_tensor(lam[:, 0:1], colsA[:, C_LAM:C_LAM + 1], colsA[:, C_LAM + 1:C_LAM + 2],
                                        ALU.mult))
            chain.settle()
            dve.tensor_tensor(lam[:, 1:2], colsA[:, C_LAM + 2:C_LAM + 3], colsA[:, C_LAM + 3:C_LAM + 4],
                              ALU.mult).then_inc(lam_prod, 1)
            dve.wait_ge(lam_exp, 1)
            chain.add(dve.tensor_tensor(lam[:, 4:5], lam[:, 3:4], lam[:, 2:3], ALU.subtract))
            chain.settle()
            chain.add(dve.tensor_scalar(lam[:, 7:8], lam[:, 4:5], -LAM_INIT, None, ALU.add))
            dve.wait_ge(consts_landed, 16 * N_CONST)
            chain.add(dve.tensor_scalar(decay[:, 1, :], decay[:, 0, :], -1.0, None, ALU.mult))
            chain.settle()
            dve.tensor_tensor(decay[:, 2, :], decay[:, 0, :], decay[:, 1, :], ALU.max).then_inc(lg_abs, 1)
            dve.wait_ge(lg_ln, 1)
            chain.add(dve.tensor_scalar(decay[:, 3, :], decay[:, 0, :], 0.0, None, ALU.min))
            chain.settle()
            chain.add(dve.tensor_tensor(decay[:, 3, :], decay[:, 3, :], decay[:, 2, :], ALU.subtract))

            def small(out_, x, y, op):
                chain.add(dve.tensor_tensor(ssm[:, out_, :], x, y, op))
                chain.settle()

            def scaled_by(out_, x, s1, s2, op0, op1):
                chain.add(dve.tensor_scalar(ssm[:, out_, :], x, s1, s2, op0, op1))
                chain.settle()

            def V(k):
                return ssm[:, k, :]

            re, im = colsA[:, A_RE:A_RE + 32], colsA[:, A_IM:A_IM + 32]
            dve.wait_ge(act_step, 2)
            dve.tensor_tensor(V(1), re, V(0), ALU.mult).then_inc(s5_exp, 1)
            small(2, im, V(0), ALU.mult)
            scaled_by(6, V(2), 1.0 / TWO_PI, ROUND, ALU.mult, ALU.add)
            scaled_by(6, V(6), ROUND, None, ALU.subtract, ALU.bypass)
            for c in (PI2_A, PI2_B, PI2_C):
                chain.add(dve.scalar_tensor_tensor(out=V(2), in0=V(6), scalar=-c, in1=V(2), op0=ALU.mult,
                                                   op1=ALU.add))
                chain.settle()
            scaled_by(3, V(2), 1.0 / TWO_PI, 0.5, ALU.mult, ALU.min)
            dve.tensor_scalar(V(3), V(3), -0.5, None, ALU.max).then_inc(s5_frac0, 1)
            dve.wait_ge(s5_trig0, 2)
            dve.wait_ge(s5_exp, 2)
            small(7, V(1), V(5), ALU.mult)
            small(8, V(1), V(4), ALU.mult)
            scaled_by(7, V(7), -1.0, None, ALU.add, ALU.bypass)
            small(9, re, re, ALU.mult)
            small(10, im, im, ALU.mult)
            small(9, V(9), V(10), ALU.add)
            chain.add(dve.reciprocal(V(9), V(9)))
            chain.settle()
            small(10, V(7), re, ALU.mult)
            small(11, V(8), im, ALU.mult)
            small(10, V(10), V(11), ALU.add)
            small(12, V(10), V(9), ALU.mult)
            small(10, V(8), re, ALU.mult)
            small(11, V(7), im, ALU.mult)
            small(10, V(10), V(11), ALU.subtract)
            small(13, V(10), V(9), ALU.mult)

            dve.wait_ge(mem_landed, 16)
            rms_rows(RMS_MEM, hs)
            for l in range(DEPTH):
                turn_out(TURN_MEM[l], G_MEM + 16 * l)
                keep(kv_mem[l][0], mem_kT[:, l])
                keep(kv_mem[l][1], mem_v[:, l])
            turn_out(TURN_X)
            head_norm(norm_mem)

            keep(s5_u, uT)
            dense(s5_z)
            dve.wait_ge(b_landed, 64)
            dve.wait_ge(normed, len(norm_mem))
            def per_state(v):
                return v.unsqueeze(2).to_broadcast([P, 32, GROUP])

            def wide(v):
                return v.rearrange("p (j c) -> p j c", c=GROUP)

            br, bi, t0 = wide(b_raw[:, 0, :]), wide(b_raw[:, 1, :]), s5_t1.rearrange("p a t -> p (a t)")[:, 0:512]
            for k, (x, y, op) in enumerate(((br, bi, ALU.subtract), (bi, br, ALU.add))):
                chain.add(dve.tensor_tensor(wide(bbar[:, k, :]), x, per_state(V(12)), ALU.mult))
                chain.add(dve.tensor_tensor(wide(t0), y, per_state(V(13)), ALU.mult))
                chain.settle()
                chain.add(dve.tensor_tensor(bbar[:, k, :], bbar[:, k, :], t0, op))
                chain.settle()
            await_chunks(dve, s5_z)
            chain.add(dve.memset(ZB, 0.0))
            chain.settle()
            dve.wait_ge(masks_made, 1)
            ZBf = ZB.rearrange("p z s -> p (z s)")
            diagonal = 4 * P
            n0 = chain.n
            per = 16

            def s5_tile(i):
                chain.n = i * per + n0
                wait_past(dve, z_turned, i * 2)
                for s in range(2):
                    for half in range(2):
                        rows_ = slice(64 * half, 64 * half + 64)
                        for_tile = ZBf[rows_, s * diagonal:(s + 1) * diagonal]
                        dst = bass.AP(tensor=for_tile.tensor, offset=for_tile.offset + half * GROUP,
                                      ap=[list(for_tile.ap[0]), [P + 2 * GROUP, 4], [1, GROUP]])
                        src = bbar[rows_, s, bass.ds(i * (4 * GROUP), 4 * GROUP)]
                        dve.tensor_copy(dst, src.rearrange("p (j c) -> p j c", c=GROUP)).then_inc(z_written, 1)
                for s in range(2):
                    src = c_raw[:, s, bass.ts(i, STATES)]
                    dve.tensor_tensor(
                        ZC[:, 4 * s:4 * s + 4, :].rearrange("p j (h q) -> p (j h) q", h=2),
                        src.unsqueeze(1).to_broadcast([P, 8, STATES]),
                        group_mask[:, s, :].unsqueeze(2).to_broadcast([P, 8, STATES]), ALU.mult)\
                        .then_inc(z_written, 1)
                wait_past(dve, trig_ready, i * 2)
                chain.add(dve.tensor_tensor(
                    s5_frac, time_row.unsqueeze(1).to_broadcast([P, 4, T]),
                    ssm[:, 3, bass.ts(i, 4)].unsqueeze(2).to_broadcast([P, 4, T]), ALU.mult))
                chain.settle()
                chain.add(dve.tensor_scalar(s5_t1, s5_frac, ROUND, ROUND, ALU.add, ALU.subtract))
                chain.settle()
                dve.tensor_tensor(s5_frac, s5_frac, s5_t1, ALU.subtract).then_inc(phase_ready, 1)
                dve.wait_ge(phase_ready, i + 1)
                dve.wait_ge(bu_ready, i + 1)
                dve.wait_ge(trig_ready, i * 2 + 2)
                bur, bui = (acc[:, k:k + 2, :].rearrange("p a (b t) -> p (a b) t", t=T) for k in (0, 2))
                dve.tensor_tensor(s5_gr, bur, s5_cos, ALU.mult).then_inc(bu_read, 1)
                dve.tensor_tensor(s5_t1, bui, s5_sin, ALU.mult).then_inc(bu_read, 1)
                dve.tensor_tensor(s5_gi, bui, s5_cos, ALU.mult).then_inc(bu_read, 1)
                dve.tensor_tensor(s5_t2, bur, s5_sin, ALU.mult).then_inc(bu_read, 1)
                dve.wait_ge(bu_read, i * 4 + 4)
                chain.add(dve.tensor_tensor(s5_gr, s5_gr, s5_t1, ALU.add))
                chain.add(dve.tensor_tensor(s5_gi, s5_gi, s5_t2, ALU.subtract))
                chain.settle()
                for j in range(4):
                    mag = ssm[:, 1, bass.ds(i * 4 + j, 1)].to_broadcast([P, T])
                    for g in (s5_gr, s5_gi):
                        ins = dve.tensor_tensor_scan(g[:, j, :], mag, g[:, j, :], 0.0, ALU.mult, ALU.add)
                        chain.add(ins)
                chain.settle()
                wait_past(dve, y_ready, i)
                chain.add(dve.tensor_tensor(s5_hr, s5_gr, s5_cos, ALU.mult))
                chain.add(dve.tensor_tensor(s5_t1, s5_gi, s5_sin, ALU.mult))
                chain.settle()
                dve.tensor_tensor(s5_hr, s5_hr, s5_t1, ALU.subtract).then_inc(h_ready, 1)
                dve.wait_ge(h_ready, i * 2 + 1)
                chain.add(dve.tensor_tensor(s5_hi, s5_gr, s5_sin, ALU.mult))
                dve.tensor_tensor(s5_t1, s5_gi, s5_cos, ALU.mult).then_inc(dve_step, 1)
                chain.n += 1
                chain.settle()
                dve.tensor_tensor(s5_hi, s5_hi, s5_t1, ALU.add).then_inc(h_ready, 1)
                dve.wait_ge(h_ready, i * 2 + 2)
                dve.wait_ge(y_ready, i + 1)
                dve.scalar_tensor_tensor(
                    out=gT[:, bass.ts(i, 1), :].rearrange("p a t -> p (a t)"),
                    in0=uT[:, bass.ts(i, 1), :].rearrange("p a t -> p (a t)"),
                    scalar=colsA[:, bass.ds(i + A_D, 1)], in1=psB[:, 0:T], op0=ALU.mult, op1=ALU.add)\
                    .then_inc(y_summed, 1)

            peeled(dve, SSM_TILES, s5_tile)
            chain.n = n0 + per * SSM_TILES
            split(S_GELU)
            dense(s5_glu)
            await_chunks(dve, s5_glu)
            chain.add(dve.tensor_tensor(glT, glT, gT, ALU.mult))
            chain.settle()
            dve.tensor_tensor(glT, glT, zT5, ALU.mult).then_inc(glu_mixed, 1)
            dve.wait_ge(glu_mixed, 1)
            split(S_GLU)
            residual(s5_out, ALPHA)
            layer_norm(LN1, 0)
            turn_out(TURN_LN1)

            for s, x in enumerate((kcT, vcT)):
                dve.memset(x[:, KVH, BLOCK:T], 0.0).then_inc(pos_ready, 1)
                dve.tensor_copy(x[:, KVH, 0:BLOCK], colsC[:, BLOCK * s:BLOCK * (s + 1)]).then_inc(pos_ready, 1)
            for ph, dst in zip(kv, (kcT, vcT, ksT, v_slc, kwT, v_win)):
                keep(ph, dst)
            for ph in cmp_w1:
                for b in range(ph.blocks):
                    n = ph.block0 + b + 1
                    split_weights(n % SLOTS, n % SPLIT_SLOTS, n)
            for s, ph in enumerate(cmp_w1):
                dve.wait_ge(blocks_done, ph.block0 + ph.blocks)
                dve.tensor_copy(cmp_bias[:, s:s + 1], psA[:, s, KVH * NCMP:KVH * NCMP + 1])\
                    .then_inc(cmp_bias_ready, 1)
            dve.wait_ge(gate_ready, 1)
            for m in range(MT):
                dve.tensor_scalar(gates[:, m, 0:NH], gates[:, m, 0:NH], row_ok[:, m:m + 1], None, ALU.mult)\
                    .then_inc(gate_ready, 1)
            dve.wait_ge(cmp_out, 1)
            dve.tensor_copy(kcmpT[:, :, :], psC[:, 0:KVH * NCMP].rearrange("p (g n) -> p g n", g=KVH))\
                .then_inc(cmp_ready, 1)
            dve.wait_ge(cmp_out, 2)
            dve.tensor_copy(vcmp[:, :, :], psC[0:NCMP, :].rearrange("p (g n) -> p g n", g=KVH))\
                .then_inc(cmp_ready, 1)
            dve.wait_ge(gate_ready, 3)
            for hh in range(2):
                keep(b_q[hh], qT)
                for r in range(BRANCHES):
                    dense(b_z[hh][r])
                    await_chunks(dve, b_z[hh][r])
                    if hh == 0 and r == 0:
                        dve.wait_ge(causal_made, 1)
                    attend(nsa[hh][r])
            dve.wait_ge(branch_summed, 2 * NH)
            split(S_NSA)
            residual(b_out, ALPHA)
            layer_norm(LN2, 1)

            rms_rows(RMS_MIX[0], xtok)
            turn_out(TURN_MIX[0], G_MIX)
            keep(ab_rq, rqT)
            keep(ab_rk, rkT)
            keep(ab_rv, rv)
            dve.wait_ge(lags_made, 1)
            for h in range(H8):
                d = table[:, h, :]
                chain.add(dve.tensor_scalar(d, later[:, :, :].rearrange("p m t -> p (m t)"), decay[:, 3, h:h + 1],
                                            None, ALU.mult))
                chain.settle()
                dve.scalar_tensor_tensor(out=d, in0=earlier[:, :, :].rearrange("p m t -> p (m t)"),
                                         scalar=decay[:, 3, 8 + h:9 + h], in1=d, op0=ALU.mult, op1=ALU.add)\
                    .then_inc(decay_arg, 1)
            dense(ab_rg)
            for t in range(H8 + 1):
                if t < H8:
                    dve.wait_ge(rs_ready, t + 1)
                    dve.wait_ge(decay_ready, t + 1)
                    if t >= 2:
                        dve.wait_ge(ro_ready, t - 1)
                    dve.scalar_tensor_tensor(out=score[:, t % 2, :], in0=psA[:, t % 2, :], scalar=SCALE,
                                             in1=table[:, t, :], op0=ALU.mult, op1=ALU.mult)\
                        .then_inc(rs_decayed, 1)
                if t >= 1:
                    dve.wait_ge(ro_ready, t)
                    dve.tensor_copy(rqT[:, t - 1, :], psC[:, 0:T]).then_inc(ro_copied, 1)
            dve.wait_ge(ro_copied, H8)
            head_norm(norm_ret)
            dve.wait_ge(normed, norm_ret[-1]["n"] + 1)
            dve.tensor_tensor(rgT, rgT, rqT, ALU.mult).then_inc(gated, 1)
            dve.wait_ge(gated, 1)
            keep(ab_nq, nqT)
            keep(ab_nk, nkT)
            keep(ab_nv, nv)
            head_norm(norm_na)
            for h in range(H8):
                dve.wait_ge(bias_turned, h + 1)
                dve.tensor_tensor(table[:, h, :].rearrange("p (n c) -> p n c", c=GRID),
                                  psA[:, h % 2, :].rearrange("p (n c) -> p n c", c=GRID),
                                  col_mask[:, :].unsqueeze(1).to_broadcast([P, MT * ROWS, GRID]), ALU.add)\
                    .then_inc(bias_masked, 1)
            dve.wait_ge(bias_masked, H8)
            attend(na)
            dve.wait_ge(o_used, na[-1]["group"] + 1)
            split(S_RET)
            split(S_NA)
            residual(ab_out, 1.0)

            def tail_dve(l):
                xq, xo, parts = layers[l]
                rms_rows(RMS_XA[l], xtok)
                turn_out(TURN_XA[l], G_X + 16 * l)
                keep(xq, xqT)
                await_chunks(dve, xq)
                head_norm(norm_x[l])
                attend(xat[l])
                dve.wait_ge(o_used, xat[l][-1]["group"] + 1)
                split(S_X[l])
                residual(xo, 1.0)
                rms_rows(RMS_FFN[l], xtok)
                turn_out(TURN_FFN[l], G_FFN + 16 * l)
                pairs_done = l * FFN_T // 2
                for ffn_in, ffn_out in parts:
                    with rep(dve, ffn_in.iters) as i:
                        for c in range(2):
                            for b in range(2):
                                n = ffn_in.block(c, b) + 1
                                split_weights(n % SLOTS, n % SPLIT_SLOTS, ffn_in.blocks_before(i, c, b) + 1)
                        dve.wait_ge(drained[ffn_in.pair(0)], ffn_in.pair_uses(i, 0) + 1)
                        dve.wait_ge(blocks_done, ffn_in.blocks_before(i, 1, 2))
                        dve.tensor_tensor(hid_f, silu_g,
                                          acc[:, 2 * ffn_in.pair(1), :].rearrange("p (f t) -> p f t", t=T),
                                          ALU.mult).then_inc(drained[ffn_in.pair(1)], 1)
                        dve.wait_ge(drained[ffn_in.pair(1)], ffn_in.pair_uses(i, 1) + 1)
                        dve.wait_ge(hid_h, i + (pairs_done + 1))
                        dve.tensor_tensor(hidL[:, bass.ts(i, 2), :], hid_f,
                                          hidH[:, bass.ts(i, 2), :].bitcast(F32), ALU.subtract)\
                            .then_inc(hid_l, 1)
                    pairs_done += ffn_in.iters
                    residual(ffn_out, 1.0)

            tail_dve(0)
            rms_rows(RMS_MIX[1], xtok)
            turn_out(TURN_MIX[1], G_MIX + 16)
            chain.add(dve.tensor_tensor(later[:, :, :], later[:, :, :], earlier[:, :, :], ALU.add))
            chain.settle()
            keep(c_qk, area(0, 2 * NH, T))
            keep(c_v, dv)
            await_chunks(dve, c_v)
            head_norm(norm_c)
            attend(dif)
            dve.wait_ge(o_used, dif[-1]["group"] + 1)
            head_norm(norm_do)
            dve.wait_ge(normed, norm_do[-1]["n"] + 1)
            split(S_DIF)
            residual(c_out, 1.0)
            tail_dve(1)


N_CONST = 27
_IN = ['x', 'a_w_in', 'a_lam_re', 'a_lam_im', 'a_log_dt', 'a_b_re', 'a_b_im', 'a_c_re', 'a_c_im', 'a_d',
       'a_w_glu', 'a_b_glu', 'a_w_out', 'kv_w', 'cmp_pos_k', 'cmp_w1_k', 'cmp_w2_k', 'cmp_pos_v', 'cmp_w1_v',
       'cmp_w2_v', 'b_w_in', 'b_w_out', 'ln_g', 'ln_b', 'mem_2', 'norm_mix_g_2', 'norm_xattn_g_2',
       'norm_mem_g_2', 'norm_ffn_g_2', 'w_in_ab_2', 'ret_decay_fwd_2', 'ret_decay_bwd_2', 'ret_out_g_2',
       'na_q_g_2', 'na_k_g_2', 'na_rpb_2', 'w_out_ab_2', 'w_in_c_2', 'diff_q_g_2', 'diff_k_g_2',
       'lambda_q1_2', 'lambda_k1_2', 'lambda_q2_2', 'lambda_k2_2', 'diff_out_g_2', 'w_out_c_2', 'w_xq_2',
       'w_xkv_2', 'w_xo_2', 'xq_g_2', 'xk_g_2', 'w_ffn_in_2', 'w_ffn_out_2']


def kernel(**inputs):
    import numpy as _np
    import concourse.bacc as _bacc
    from concourse.bass_utils import run_bass_kernel_spmd as _run

    nc = _bacc.Bacc("TRN2", target_bir_lowering=False, num_devices=1)
    arrays, aps = {}, {}
    for name in _IN:
        x = _np.ascontiguousarray(inputs[name])
        arrays[f"in_{name}"] = x
        aps[name] = nc.dram_tensor(f"in_{name}", x.shape, mybir.dt.from_np(x.dtype), kind="ExternalInput").ap()
    out = nc.dram_tensor("out_x", (1, T, D), F32, kind="ExternalOutput").ap()
    program(nc, aps, out)
    r = _run(nc, [arrays], core_ids=[0])
    return r.results[0]["out_x"]
```

```python
import math
from itertools import chain as join
from contextlib import ExitStack, contextmanager

import numpy as np

import concourse.bass as bass
from concourse import mybir

F32 = mybir.dt.float32
F32R = mybir.dt.float32r
ALU = mybir.AluOpType
ACT = mybir.ActivationFunctionType
AX_X = mybir.AxisListType.X

P = 128
D = 2048
T = 256
MT = T // P
FT = D // P
SLOTS = 4
SPLIT_SLOTS = 2
SLOT = 2048
HALF = SLOT // 2
COLS = 512

SSM_TILES = 8
STATES = 64
GROUP = 16
NH = 16
DH = 128
KVH = 4
BLOCK, STRIDE = 32, 16
NCMP = (T - BLOCK) // STRIDE + 1
BRANCHES = 3
NGATE = BRANCHES * NH
H8 = 8
GRID = 64
ROWS = T // GRID
WIN_R, WIN_C = 8, 16
RPB_R, RPB_C = 2 * WIN_R - 1, 2 * WIN_C - 1
XH = 4
FFN = 5632
FFN_T = FFN // P
FFN_PARTS = (16, 16, 12)
DEPTH = 2
ALPHA = (2 * DEPTH) ** 0.25
LN_EPS, RMS_EPS = 1e-5, 1e-6
SCALE = DH ** -0.5
NEG = -1e30
LAM_INIT = 0.8 - 0.6 * math.exp(-0.3)
ROUND = 1.5 * 2.0 ** 23
TWO_PI = 2 * math.pi
PI2_A = 6.28125
PI2_B = float(np.float32(TWO_PI - PI2_A))
PI2_C = float(np.float32(TWO_PI - PI2_A - PI2_B))
TURN = float(np.nextafter(np.float32(TWO_PI), np.float32(0)))


@contextmanager
def rep(eng, n):
    if n == 1:
        yield 0
    else:
        with eng.Fori(0, n) as i:
            yield i


def in_pairs(eng, n, body):
    body(0, 0)
    body(1, 1)
    with eng.Fori(1, n // 2) as i:
        body(i * 2, 0)
        body(i * 2 + 1, 1)


def alternate(steps, blocks=None, counts=()):
    for k, _ in enumerate(steps):
        for _ in range(counts[k] if k < len(counts) else 0):
            next(blocks)


def wait_past(eng, sem, value):
    if not isinstance(value, int) or value > 0:
        eng.wait_ge(sem, value)


class Chain:

    def __init__(self, eng, sem):
        self.eng, self.sem, self.n = eng, sem, 0

    def add(self, ins):
        ins.then_inc(self.sem, 1)
        self.n += 1

    def settle(self):
        self.eng.wait_ge(self.sem, self.n)


class Dense:

    def __init__(self, plan, src, kt, cols, blocks, chunks, style, iters=1, hidden=False):
        self.src, self.kt, self.cols, self.blocks, self.style = src, kt, cols, blocks, style
        self.iters, self.body, self.hidden = iters, chunks // iters, hidden
        self.block0, self.chunk0 = plan["blocks"], plan["chunks"]
        plan["blocks"] += chunks * blocks
        plan["chunks"] += chunks
        self.end = plan["chunks"]
        assert kt * cols == SLOT
        assert iters == 1 or (self.body * blocks % SLOTS == 0 and self.body % 2 == 0)

    def pair(self, c):
        return (self.chunk0 + c) % 2

    def block(self, c, b):
        return self.block0 + c * self.blocks + b

    def blocks_before(self, i, c, b):
        return i * (self.body * self.blocks) + self.block(c, b)

    def pair_uses(self, i, c):
        return i * (self.body // 2) + (self.chunk0 + c) // 2


class Loose:

    def __init__(self, plan, blocks):
        self.block0, self.blocks = plan["blocks"], blocks
        plan["blocks"] += blocks


def program(nc, a, out):
    ctx = ExitStack()
    with ctx:
        def sb(name, *shape, dt=F32):
            return ctx.enter_context(nc.sbuf_tensor(name, list(shape), dt))

        def ps(name, *shape):
            return ctx.enter_context(nc.psum_tensor(name, list(shape), F32))

        def sem(name):
            return ctx.enter_context(nc.semaphore(name))

        ring = sb("ring", P, SLOTS, SLOT)
        xtok = sb("xtok", P, MT, D)
        wH = sb("wH", P, SPLIT_SLOTS, SLOT, dt=F32R)
        wL = sb("wL", P, SPLIT_SLOTS, SLOT, dt=F32R)
        with nc.sbuf_tensor("s5_scratch", [P, 2 * FT * T], F32) as s5_scratch:
            pass
        actH = sb("actH", P, FT, T, dt=F32R)
        actL = sb("actL", P, FT, T, dt=F32R)
        with ExitStack() as over:
            hidH = over.enter_context(nc.sbuf_tensor("hidH", [P, FFN_PARTS[0], T], F32R))
            hidL = over.enter_context(nc.sbuf_tensor("hidL", [P, FFN_PARTS[0], T], F32R))
            ffn_tmp = over.enter_context(nc.sbuf_tensor("ffn_tmp", [P, 2, 2, T], F32))
        arena = sb("arena", P, 14848)
        mem_kT = sb("mem_kT", P, DEPTH, XH, T)
        mem_v = sb("mem_v", P, DEPTH, MT, XH * DH)
        score = sb("score", P, 2, 512)
        probT = sb("probT", P, 2, 512)
        ident = sb("ident", P, P)
        flip = sb("flip", P, P)
        mean_of = sb("mean_of", P, P)
        causal = sb("causal", P, MT, T)
        earlier = sb("earlier", P, MT, T)
        later = causal
        time_row = earlier[:, 0, :]
        ssm = causal[:, :, :].rearrange("p m t -> p (m t)").rearrange("p (k j) -> p k j", j=32)
        cmp_mask = sb("cmp_mask", P, MT, NCMP)
        row_ok = sb("row_ok", P, MT)
        group_mask = sb("group_mask", P, 2, 8)
        col_mask = sb("col_mask", P, GRID)
        ldt2 = sb("ldt2", 96, 2)
        colsA = sb("colsA", P, P)
        colsB = sb("colsB", P, P)
        colsC = sb("colsC", P, 64)
        consts = sb("consts", P, 5)
        decay = sb("decay", P, 4, 16)
        lam = sb("lam", P, 8)
        gates = sb("gates", P, MT, NGATE)
        w2 = sb("w2", P, 2, P)
        cmp_hid = sb("cmp_hid", P, 2, KVH * NCMP)
        cmp_bias = sb("cmp_bias", P, 2)
        kcmpT = sb("kcmpT", P, KVH, NCMP)
        vcmp = sb("vcmp", NCMP, KVH, DH)
        rpb_pad = sb("rpb_pad", H8 * RPB_R, P)
        stats = sb("stats", P, MT, 24)
        moments = sb("moments", P, MT, 2)
        mean_sq = sb("mean_sq", P, MT)
        root = sb("root", P, MT)
        rstd = sb("rstd", P, MT)
        head_rms = sb("head_rms", P, 2, 4)
        neg_max = sb("neg_max", P, 2, MT)
        denom = sb("denom", P, 2, MT)
        factor = sb("factor", P, 2, MT)
        rpb_dram = nc.dram_tensor("rpb_scratch", [H8 * RPB_R, P], F32, kind="Internal").ap()

        acc = ps("acc", P, 4, 512)
        psA = ps("psA", P, 2, 512)
        psB = ps("psB", P, 512)
        psC = ps("psC", P, 512)
        turn_banks = [psA[:, 0, :], psA[:, 1, :], psB[:, :], psC[:, :]]

        def area(at, *shape):
            n = int(np.prod(shape))
            v = arena[:, at:at + n]
            if len(shape) == 2:
                return v.rearrange("p (a b) -> p a b", a=shape[0])
            if len(shape) == 3:
                return v.rearrange("p (a b c) -> p a b c", a=shape[0], b=shape[1])
            return v

        def scratch(at, *shape):
            n = int(np.prod(shape))
            return s5_scratch[:, at:at + n].rearrange("p (a b) -> p a b", a=shape[0])

        hs = area(10752, MT, D)
        rowsA, rowsB, rowsC = area(8192, P), area(8320, P), area(8448, P)[0:64, :]
        uT, zT5, gT, glT = (area(2048 * k, 8, T) for k in range(4))
        s5_sin0, s5_cos0, s5_frac, s5_t1, s5_t2, s5_gr, s5_gi = (
            area(6144 + 1024 * k, 4, T) for k in range(7))
        b_raw = area(13312, 2, 512)
        s5_hr, s5_hi = scratch(0, 4, T), scratch(1024, 4, T)
        ZB, ZC, BT, CT = (scratch(2048 + 1024 * k, 8, P) for k in range(4))
        s5_sin = [s5_sin0, scratch(6144, 4, T)]
        s5_cos = [s5_cos0, scratch(7168, 4, T)]
        s5_whole = area(13312, 4, T)
        bbar = score
        c_raw = probT
        ln_rows = area(0, 2, D)
        kcT = area(0, KVH + 1, T)
        vcT = area(1280, KVH + 1, T)
        ksT = area(2560, KVH, T)
        kwT = area(3584, KVH, T)
        v_slc = area(4608, MT, 512)
        v_win = area(5632, MT, 512)
        qT = area(6656, NH // 2, T)
        zT = area(8704, NH // 2, T)
        gate_w = area(8704, FT, NGATE)
        oT = area(10752, NH, T)
        rqT, rkT, rgT = (area(2048 * k, H8, T) for k in range(3))
        rv = area(6144, MT, H8 * DH)
        nqT, nkT, nv = area(12288, H8, T), rkT, rv
        table = area(8192, H8, 2 * T)
        dqT, dkT = area(0, NH, T), area(4096, NH, T)
        dv = area(8192, MT, D)
        xqT = area(0, XH, T)
        xoT = area(1024, XH, T)
        silu_g, hid_f = ffn_tmp[:, 0, :, :], ffn_tmp[:, 1, :, :]

        A_RE, A_IM, A_DT, A_D, A_BGLU = 0, 32, 64, 96, 104
        (C_RET, C_NAQ, C_NAK, C_DQ, C_DK, C_DO, C_XQ, C_XK, C_LAM) = (
            112, 113, 114, 115, 116, 117, 119, 121, 123)
        G_MIX, G_X, G_MEM, G_FFN = 0, 32, 64, 96

        landed = [sem(f"weights_landed_{s}") for s in range(SLOTS)]
        blocks_done = sem("weight_blocks_done")
        drained = [sem(f"chunks_drained_{p}") for p in range(2)]
        x_landed, mem_landed, consts_landed = sem("x_landed"), sem("mem_landed"), sem("consts_landed")
        ldt_landed, b_landed, ln_landed = sem("ldt_landed"), sem("b_landed"), sem("ln_landed")
        pad_landed, pad_stored, bias_landed = sem("pad_landed"), sem("pad_stored"), sem("bias_landed")
        masks_made, causal_made, lags_made = sem("masks_made"), sem("causal_made"), sem("lags_made")
        ident_made = sem("ident_made")
        pool_step, dve_step, act_step = sem("pool_step"), sem("dve_step"), sem("act_step")
        cols_turned, cols_copied = sem("cols_turned"), sem("cols_copied")
        stats_ready = sem("row_statistics_ready")
        ms_ready, root_ready, rstd_ready = sem("mean_square_ready"), sem("root_ready"), sem("rstd_ready")
        scaled = [sem(f"rows_scaled_{m}") for m in range(MT)]
        ln_centred = sem("last_tile_centred")
        ln_done = sem("layer_norm_done")
        turned = sem("tiles_turned")
        turned_h, turned_l = sem("turned_tiles_high"), sem("turned_tiles_low")
        h_made, l_made = sem("weight_highs_made"), sem("weight_lows_made")
        act_h, act_l = sem("activation_highs_made"), sem("activation_lows_made")
        hid_h, hid_l = sem("hidden_highs_made"), sem("hidden_lows_made")
        sq_ready, mean_ready, hroot_ready, normed = (
            sem("squares_ready"), sem("head_mean_ready"), sem("head_root_ready"), sem("heads_normed"))
        diag_ready, spread_ready = sem("diagonals_ready"), sem("factors_spread")
        scores_ready, biased, max_ready, exp_ready = (
            sem("scores_ready"), sem("scores_biased"), sem("max_ready"), sem("exp_ready"))
        probs_ready, probs_turned, probT_ready, o_ready, o_used = (
            sem("probs_ready"), sem("probs_turned"), sem("probT_ready"), sem("o_ready"), sem("o_used"))
        branch_summed = sem("branch_summed")
        s5_dt, s5_exp, s5_frac0, s5_trig0 = sem("s5_dt"), sem("s5_theta"), sem("s5_frac0"), sem("s5_trig0")
        s5_begins = sem("s5_scan_begins")
        z_written, z_turned, z_copied = sem("s5_z_written"), sem("s5_z_turned"), sem("s5_z_copied")
        phase_ready, trig_ready, bu_ready, bu_read = (
            sem("s5_phase_ready"), sem("s5_trig_ready"), sem("s5_bu_ready"), sem("s5_bu_read"))
        h_ready, y_ready, y_summed, gelu_done, glu_mixed = (
            sem("s5_h_ready"), sem("s5_y_ready"), sem("s5_y_summed"), sem("s5_gelu_done"), sem("s5_glu_mixed"))
        pos_ready, cmp_sum, cmp_bias_ready, cmp_hid_ready, cmp_out, cmp_ready = (
            sem("pos_ready"), sem("cmp_sum"), sem("cmp_bias_ready"), sem("cmp_hid_ready"), sem("cmp_out"),
            sem("cmp_ready"))
        gate_w_landed = sem("gate_w_landed")
        gate_sum, gate_ready = sem("gate_sum"), sem("gate_ready")
        lg_abs, lg_ln, lg_ready, lam_prod, lam_sum, lam_exp, lam_ready = (
            sem("lg_abs"), sem("lg_ln"), sem("lg_ready"), sem("lam_prod"), sem("lam_sum"), sem("lam_exp"),
            sem("lam_ready"))
        decay_arg, decay_ready = sem("decay_arg"), sem("decay_ready")
        rs_ready, rs_decayed, ro_ready, ro_copied, gated = (
            sem("ret_scores_ready"), sem("ret_scores_decayed"), sem("ret_o_ready"), sem("ret_o_copied"),
            sem("ret_gated"))
        bias_turned, bias_masked = sem("na_bias_turned"), sem("na_bias_masked")
        out_done = sem("out_done")

        plan = {"blocks": 0, "chunks": 0}

        def columns(w, kt, cols):
            v = w.rearrange("(t p) n -> p t n", p=P)
            return lambda j, k=0: v[:, k * kt:(k + 1) * kt, bass.ts(j, cols)]

        def feat(w, first, tiles, iters=1):
            at = columns(w, FT, P)
            chunks = tiles // 2
            body = chunks // iters
            return Dense(plan, lambda i, c, b: at(i * (2 * body) + (first + 2 * c + b)), FT, P, 2, chunks,
                         "feat", iters)

        def tok(w, first, chunks, blocks, iters=1, k0=0, hidden=False):
            at = columns(w, 4, COLS)
            body = chunks // iters
            return Dense(plan, lambda i, c, b: at(i * body + (first + c), k0 + b), 4, COLS, blocks, chunks,
                         "tok", iters, hidden)

        kv_mem = [(feat(a["w_xkv_2"][l], 0, XH), tok(a["w_xkv_2"][l], 1, 1, 4)) for l in range(DEPTH)]
        s5_u = feat(a["a_w_in"][0], 0, 8, 2)
        s5_z = feat(a["a_w_in"][0], 8, 8, 2)
        glu_at = columns(a["a_w_glu"][0], 8, 2 * P)
        s5_glu = Dense(plan, lambda i, c, b: glu_at(c), 8, 2 * P, 1, 4, "feat")
        s5_out = tok(a["a_w_out"][0], 0, 4, 2, 2)
        kv_cmp = [feat(a["kv_w"], 4 * k, KVH) for k in range(2)]
        cmp_w1 = [Loose(plan, 2) for _ in range(2)]
        kv = [feat(a["kv_w"], 4 * k, KVH) if style == "feat" else tok(a["kv_w"], k, 1, 4)
              for k, style in ((2, "feat"), (3, "tok"), (4, "feat"), (5, "tok"))]
        b_q, b_z = [], []
        for hh in range(2):
            b_q.append(feat(a["b_w_in"][0], 8 * hh, 8, 2))
            b_z.append([feat(a["b_w_in"][0], NH * (r + 1) + 8 * hh, 8, 2) for r in range(BRANCHES)])
        nsa_counts = [1] * 16 + [2] * 8 + [1] * 24
        assert sum(nsa_counts) == 7 * 8
        b_out = tok(a["b_w_out"][0], 0, 4, 4, 2)

        w_ab = a["w_in_ab_2"][0]
        ab_rq, ab_rk = feat(w_ab, 0, 8, 2), feat(w_ab, 8, 8, 2)
        ab_rv = tok(w_ab, 4, 2, 4)
        ab_nq, ab_nk, ab_nv = feat(w_ab, 32, 8, 2), feat(w_ab, 40, 8, 2), tok(w_ab, 12, 2, 4)
        ab_rg = feat(w_ab, 24, 8, 2)
        ab_out = tok(a["w_out_ab_2"][0], 0, 4, 4, 2)
        layers = []

        def tail(l):
            xq = feat(a["w_xq_2"][l], 0, XH)
            xo = tok(a["w_xo_2"][l], 0, 4, 1)
            at = columns(a["w_ffn_in_2"][l], FT, P)
            parts, k0 = [], 0
            for n in FFN_PARTS:
                def src(i, c, b, k0=k0):
                    return at(i * 2 + (k0 + c * FFN_T + b))
                ffn_in = Dense(plan, src, FT, P, 2, n, "feat", n // 2)
                ffn_out = tok(a["w_ffn_out_2"][l], 0, 4, n // 4, 2 if n % 8 == 0 else 1, k0 // 4, True)
                parts.append((ffn_in, ffn_out))
                k0 += n
            return xq, xo, parts

        layers.append(tail(0))
        c_q, c_k = feat(a["w_in_c_2"][0], 0, NH, 4), feat(a["w_in_c_2"][0], NH, NH, 4)
        c_v = tok(a["w_in_c_2"][0], 8, 4, 4, 2)
        c_out = tok(a["w_out_c_2"][0], 0, 4, 4, 2)
        layers.append(tail(1))

        def attn(q, k, K, v, mode, bias=None, gate=None, first=True, last=True, halves=1, **more):
            return dict(q=q, k=k, K=K, v=v, mode=mode, bias=bias, gate=gate, first=first, last=last,
                        halves=halves, **more)

        nsa = []
        for hh in range(2):
            nsa.append([])
            for r in range(BRANCHES):
                part = []
                for h8 in range(NH // 2):
                    h = hh * (NH // 2) + h8
                    g = h // (NH // KVH)
                    gate = gates[:, :, r * NH + h:r * NH + h + 1].rearrange("p m o -> p (m o)")
                    if r == 0:
                        u = attn(qT[:, h8, :], kcmpT[:, g, :], NCMP, lambda t, o, g=g: vcmp[:, g, :], "bias",
                                 cmp_mask[:, :, :], gate)
                    else:
                        kk, vv = ((ksT, v_slc), (kwT, v_win))[r - 1]
                        u = attn(qT[:, h8, :], kk[:, g, :], T,
                                 lambda t, o, g=g, vv=vv: vv[:, t, g * DH:(g + 1) * DH], "bias",
                                 causal[:, :, :], gate)
                    u.update(fin="gate", r=r, h=h, h8=h8, output_after=(b_z[hh][r], h8 // 2))
                    if hh == 1 and r == 0 and h8 == 0:
                        u.update(scores_after=b_q[1])
                    part.append(u)
                nsa[hh].append(part)
        nsa_units = [u for half in nsa for part in half for u in part]
        na = [attn(nqT[:, h, :], nkT[:, h, :], T, lambda t, o, h=h: nv[:, t, h * DH:(h + 1) * DH], "bias",
                   table[:, h, :].rearrange("p (q k) -> p q k", q=MT), fin="copy", to=nqT[:, h, :])
              for h in range(H8)]
        xat = [[attn(xqT[:, h, :], mem_kT[:, l, h, :], T,
                     lambda t, o, h=h, l=l: mem_v[:, l, t, h * DH:(h + 1) * DH], "plain",
                     fin="copy", to=xoT[:, h, :]) for h in range(XH)] for l in range(DEPTH)]
        dif = [attn(dqT[:, 2 * h + c, :], dkT[:, 2 * h + c, :], T,
                    lambda t, o, h=h: dv[:, t, h * T + o * DH:h * T + (o + 1) * DH], "alibi",
                    bias=2.0 ** (-8.0 * (h + 1) / H8), gate=lam[:, 7:8].to_broadcast([P, MT]) if c else None,
                    first=c == 0, last=c == 1, halves=2, fin="copy", to=dqT[:, 2 * h:2 * h + 2, :],
                    values_after=(c_v, h // 2))
               for h in range(H8) for c in range(2)]
        groups = units = 0
        for part in (*nsa[0], *nsa[1], na, xat[0], dif, xat[1]):
            for u in part:
                u["n"], u["group"] = units, groups
                units += 1
                groups += u["last"]

        def pairs(v, n, g):
            return [dict(x=v[:, k:k + 2, :], g=[g, g], wide=False) for k in range(0, n, 2)]

        norm_mem = [u for l in range(DEPTH) for u in pairs(mem_kT[:, l], XH, C_XK + l)]
        norm_ret = pairs(rqT, H8, C_RET)
        norm_na = pairs(nqT, H8, C_NAQ) + pairs(nkT, H8, C_NAK)
        norm_x = [pairs(xqT, XH, C_XQ + l) for l in range(DEPTH)]
        norm_c = pairs(dqT, NH, C_DQ) + pairs(dkT, NH, C_DK)
        norm_na[0]["after"], norm_na[H8 // 2]["after"] = ab_nq, ab_nk
        norm_c[0]["after"], norm_c[NH // 2]["after"] = c_q, c_k
        norm_do = [dict(x=dqT[:, k:k + 2, :], g=[C_DO, C_DO + 1], wide=True) for k in range(0, NH, 2)]
        n = 0
        for part in (norm_mem, norm_ret, norm_na, norm_x[0], norm_c, norm_do, norm_x[1]):
            for u in part:
                u["n"] = n
                n += 1

        TURN_MEM, TURN_X, TURN_LN1, TURN_MIX, TURN_XA, TURN_FFN = (0, 1), 2, 3, (4, 7), (5, 8), (6, 9)
        RMS_MEM, LN1, LN2, RMS_MIX, RMS_XA, RMS_FFN = 0, 1, 2, (3, 6), (4, 7), (5, 8)
        SCALED = {RMS_MEM: 1, RMS_MIX[0]: 2, RMS_XA[0]: 3, RMS_FFN[0]: 4, RMS_MIX[1]: 5, RMS_XA[1]: 6,
                  RMS_FFN[1]: 7}
        STATS_IN_DRAIN = [LN1, LN2, RMS_XA[0], RMS_FFN[0], RMS_MIX[1], RMS_XA[1], RMS_FFN[1]]
        IN_FLIGHT = len(turn_banks)
        LN_POOL = 3 * D // 4

        def await_chunks(eng, ph):
            for last in (ph.end - 2, ph.end - 1):
                eng.wait_ge(drained[last % 2], last // 2 + 1)

        def await_chunk(eng, ph, c):
            eng.wait_ge(drained[ph.pair(c)], (ph.chunk0 + c) // 2 + 1)

        def await_turn(eng, call):
            eng.wait_ge(turned_l, FT * (call + 1))

        def drain_chunk(eng, ph, i, c, fn):
            eng.wait_ge(blocks_done, ph.blocks_before(i, c, ph.blocks))
            first = 2 * ph.pair(c)
            src = acc[:, first, :].rearrange("p (f t) -> p f t", t=T) if ph.style == "feat" else \
                acc[:, first:first + 2, :]
            fn(i, c, src).then_inc(drained[ph.pair(c)], 1)

        SPLITS = [(gT, 8, 0), (glT, 8, 0), (oT, NH, 0), (rgT, H8, 0), (nqT, H8, H8), (xoT, XH, 0),
                  (dqT, NH, 0), (xoT, XH, 0)]
        S_GELU, S_GLU, S_NSA, S_RET, S_NA, S_X, S_DIF = 0, 1, 2, 3, 4, (5, 7), 6

        def split_steps(upto):
            return sum(n // 4 for _, n, _ in SPLITS[:upto])

        rows = [
            (rowsA[A_RE:A_RE + 32, :], a["a_lam_re"][0].rearrange("(j h) p -> j (h p)", h=2)),
            (rowsA[A_IM:A_IM + 32, :], a["a_lam_im"][0].rearrange("(j h) p -> j (h p)", h=2)),
            (rowsA[A_D:A_D + 8, :], a["a_d"][0].rearrange("(j p) -> j p", p=P)),
            (rowsA[A_BGLU:A_BGLU + 8, :], a["a_b_glu"][0].rearrange("(j p) -> j p", p=P)),
            (rowsA[C_RET:C_RET + 1, :], a["ret_out_g_2"]),
            (rowsA[C_NAQ:C_NAQ + 1, :], a["na_q_g_2"]),
            (rowsA[C_NAK:C_NAK + 1, :], a["na_k_g_2"]),
            (rowsA[C_DQ:C_DQ + 1, :], a["diff_q_g_2"]),
            (rowsA[C_DK:C_DK + 1, :], a["diff_k_g_2"]),
            (rowsA[C_DO:C_DO + 2, :], a["diff_out_g_2"][0].rearrange("(j p) -> j p", p=P)),
            (rowsA[C_XQ:C_XQ + 2, :], a["xq_g_2"]),
            (rowsA[C_XK:C_XK + 2, :], a["xk_g_2"]),
            (rowsA[C_LAM:C_LAM + 1, :], a["lambda_q1_2"]),
            (rowsA[C_LAM + 1:C_LAM + 2, :], a["lambda_k1_2"]),
            (rowsA[C_LAM + 2:C_LAM + 3, :], a["lambda_q2_2"]),
            (rowsA[C_LAM + 3:C_LAM + 4, :], a["lambda_k2_2"]),
            (rowsA[C_LAM + 4:C_LAM + 5, :], a["lambda_k2_2"]),
            (rowsC[0:BLOCK, :], a["cmp_pos_k"]),
            (rowsC[BLOCK:2 * BLOCK, :], a["cmp_pos_v"]),
            (w2[:, 0, :], a["cmp_w2_k"]),
            (w2[:, 1, :], a["cmp_w2_v"]),
            (decay[:, 0, 0:8], a["ret_decay_fwd_2"].partition_broadcast(P).rearrange("p o h -> p (o h)")),
            (decay[:, 0, 8:16], a["ret_decay_bwd_2"].partition_broadcast(P).rearrange("p o h -> p (o h)")),
        ]
        for k, name in enumerate(("norm_mix_g_2", "norm_xattn_g_2", "norm_mem_g_2", "norm_ffn_g_2")):
            rows.append((rowsB[32 * k:32 * k + 32, :], a[name].rearrange("l (j p) -> (l j) p", p=P)))
        assert len(rows) == N_CONST

        block = ctx.enter_context(nc.Block())

        @block.sync
        def _(sp):
            sp.dma_start(hs, a["mem_2"][0].rearrange("(m p) d -> p m d", p=P)).then_inc(mem_landed, 16)
            sp.dma_start(ldt2[64:96, :], a["a_log_dt"][0].rearrange("(j h) -> j h", h=2)).then_inc(ldt_landed, 16)

            def fetch(src, ph, slot, number, first):
                if first >= SLOTS:
                    sp.wait_ge(l_made, number * 2 - 2 * (SLOTS - 1))
                dst = ring[:, slot, :]
                if ph is not None:
                    dst = dst.rearrange("p (t n) -> p t n", t=ph)
                sp.dma_start(dst, src).then_inc(landed[slot], 16)

            def stream(ph):
                with rep(sp, ph.iters) as i:
                    for c in range(ph.body):
                        for b in range(ph.blocks):
                            n = ph.block(c, b)
                            fetch(ph.src(i, c, b), ph.kt, n % SLOTS, ph.blocks_before(i, c, b), n)

            def stream_w1(ph, w):
                for b in range(2):
                    n = ph.block0 + b
                    fetch(w.rearrange("(j p) n -> p j n", p=P)[:, b * 16:(b + 1) * 16, :], 16, n % SLOTS, n, n)

            for dst, src in rows:
                sp.dma_start(dst, src).then_inc(consts_landed, 16)
            stream(kv_mem[0][0])
            sp.dma_start(xtok[:, :, :], a["x"][0].rearrange("(m p) d -> p m d", p=P)).then_inc(x_landed, 16)
            for ph in (kv_mem[0][1], *kv_mem[1]):
                stream(ph)
            for ph in (s5_u, s5_z, s5_glu, s5_out, *kv_cmp):
                stream(ph)
            stream_w1(cmp_w1[0], a["cmp_w1_k"])
            stream_w1(cmp_w1[1], a["cmp_w1_v"])
            for ph in kv:
                stream(ph)
            for hh in range(2):
                for ph in (b_q[hh], *b_z[hh]):
                    stream(ph)
            for ph in (b_out, ab_rq, ab_rk, ab_rv, ab_nq, ab_nk, ab_nv, ab_rg, ab_out):
                stream(ph)

            def stream_tail(l):
                xq, xo, parts = layers[l]
                stream(xq)
                stream(xo)
                for ffn_in, ffn_out in parts:
                    stream(ffn_in)
                    stream(ffn_out)

            stream_tail(0)
            for ph in (c_q, c_k, c_v, c_out):
                stream(ph)
            stream_tail(1)
            await_chunks(sp, layers[1][2][-1][1])
            sp.dma_start(out[0].rearrange("(m p) d -> p m d", p=P), xtok[:, :, :]).then_inc(out_done, 16)
            sp.wait_ge(out_done, 16)

        @block.gpsimd
        def _(pool):
            chain = Chain(pool, pool_step)

            for ap, value in ((ident[:, :], 0.0), (flip[:, :], 0.0), (mean_of[:, :], 1.0 / P), (consts[:, 0:1], RMS_EPS),
                              (consts[:, 1:2], LN_EPS), (consts[:, 2:3], math.pi / 2), (consts[:, 3:4], 1.0),
                              (consts[:, 4:5], ROUND),
                              (cmp_mask[:, :, :], 0.0), (row_ok[:, :], 1.0),
                              (col_mask[:, :], 0.0), (group_mask[:, 0, :], 1.0), (group_mask[:, 1, :], -1.0),
                              (rpb_pad[:, :], 0.0)):
                chain.add(pool.memset(ap, value))
            chain.settle()
            pool.affine_select(out=ident[:, :], in_=ident[:, :], compare_op=ALU.not_equal, fill=1.0, base=0,
                               pattern=[[-1, P]], channel_multiplier=1).then_inc(ident_made, 1)
            for at in (GRID - 1, 3 * GRID - 1):
                chain.add(pool.affine_select(out=flip[:, :], in_=flip[:, :], compare_op=ALU.not_equal, fill=1.0,
                                             base=-at, pattern=[[1, P]], channel_multiplier=1))
                chain.settle()
            pool.dma_start(rpb_pad[:, GRID - WIN_C:GRID - WIN_C + RPB_C],
                           a["na_rpb_2"][0].rearrange("h r c -> (h r) c")).then_inc(pad_landed, 16)
            chain.add(pool.affine_select(out=cmp_mask[:, :, :], in_=cmp_mask[:, :, :], compare_op=ALU.is_ge,
                                         fill=NEG, base=-(BLOCK - 1), pattern=[[P, MT], [-STRIDE, NCMP]],
                                         channel_multiplier=1))
            chain.add(pool.affine_select(out=row_ok[:, :], in_=row_ok[:, :], compare_op=ALU.is_ge, fill=0.0,
                                         base=-(BLOCK - 1), pattern=[[P, MT]], channel_multiplier=1))
            for s in range(2):
                chain.add(pool.affine_select(out=group_mask[:, s, :], in_=group_mask[:, s, :],
                                             compare_op=ALU.is_ge, fill=0.0, base=0, pattern=[[-GROUP, 8]],
                                             channel_multiplier=1))
            chain.settle()
            for s in range(2):
                chain.add(pool.affine_select(out=group_mask[:, s, :], in_=group_mask[:, s, :],
                                             compare_op=ALU.is_ge, fill=0.0, base=GROUP - 1,
                                             pattern=[[GROUP, 8]], channel_multiplier=-1))
            chain.settle()
            edge = GRID - WIN_C
            for q in range(2):
                m = col_mask[GRID * q:GRID * (q + 1), :]
                chain.add(pool.affine_select(out=m[:, 0:edge], in_=m[:, 0:edge], compare_op=ALU.is_ge, fill=NEG,
                                             base=WIN_C // 2, pattern=[[1, edge]], channel_multiplier=-1))
                chain.settle()
            for q in range(2):
                m = col_mask[GRID * q:GRID * (q + 1), WIN_C:GRID]
                chain.add(pool.affine_select(out=m, in_=m, compare_op=ALU.is_ge, fill=NEG,
                                             base=WIN_C // 2 - 1 - WIN_C, pattern=[[-1, edge]],
                                             channel_multiplier=1))
                chain.settle()
            chain.add(pool.iota(time_row, [[1, T]], base=0, channel_multiplier=0,
                                allow_small_or_imprecise_dtypes=True))
            chain.settle()
            pool.engine_nop().then_inc(masks_made, 1)
            pool.wait_ge(pad_landed, 16)
            pool.dma_start(rpb_dram, rpb_pad[:, :]).then_inc(pad_stored, 16)

            await_chunks(pool, kv_mem[1][1])
            pool.wait_ge(normed, len(norm_mem))
            for k, name in enumerate(("a_b_re", "a_b_im")):
                pool.dma_start(b_raw[:, k, :].rearrange("p (j c) -> p j c", c=GROUP),
                               a[name][0].rearrange("(j h) q c -> (h q) j c", h=2)).then_inc(b_landed, 16)
            for k, name in enumerate(("a_c_re", "a_c_im")):
                pool.dma_start(c_raw[:, k, :].rearrange("p (f q) -> p f q", q=STATES),
                               a[name][0].rearrange("(f g) c q -> (g c) f q", f=8)).then_inc(b_landed, 16)

            pool.wait_ge(b_landed, 64)
            pool.wait_ge(s5_begins, 1)
            n0 = chain.n
            diagonal = 4 * P
            ZBf = ZB.rearrange("p z s -> p (z s)")

            def s5_tile(i, parity):
                chain.n = i * 3 + n0
                if not (isinstance(i, int) and i == 0):
                    pool.wait_ge(z_turned, i * 2 - 1)
                for s in range(2):
                    for half in range(2):
                        rows_ = slice(64 * half, 64 * half + 64)
                        for_tile = ZBf[rows_, s * diagonal:(s + 1) * diagonal]
                        dst = bass.AP(tensor=for_tile.tensor, offset=for_tile.offset + half * GROUP,
                                      ap=[list(for_tile.ap[0]), [P + 2 * GROUP, 4], [1, GROUP]])
                        src = bbar[rows_, s, bass.ds(i * (4 * GROUP), 4 * GROUP)]
                        pool.tensor_copy(dst, src.rearrange("p (j c) -> p j c", c=GROUP)).then_inc(z_written, 1)
                        pool.wait_ge(z_written, i * 6 + (2 * s + half + 1))
                wait_past(pool, trig_ready, i * 2)
                chain.add(pool.tensor_tensor(
                    s5_frac, time_row.unsqueeze(1).to_broadcast([P, 4, T]),
                    ssm[:, 3, bass.ts(i, 4)].unsqueeze(2).to_broadcast([P, 4, T]), ALU.mult))
                chain.settle()
                big = consts[:, 4:5].unsqueeze(2).to_broadcast([P, 4, T])
                chain.add(pool.tensor_tensor(s5_whole, s5_frac, big, ALU.add))
                chain.settle()
                chain.add(pool.tensor_tensor(s5_whole, s5_whole, big, ALU.subtract))
                chain.settle()
                pool.tensor_tensor(s5_frac, s5_frac, s5_whole, ALU.subtract).then_inc(phase_ready, 1)
                wait_past(pool, z_turned, i * 2)
                for s in range(2):
                    src = c_raw[:, s, bass.ts(i, STATES)]
                    pool.tensor_tensor(
                        ZC[:, 4 * s:4 * s + 4, :].rearrange("p j (h q) -> p (j h) q", h=2),
                        src.unsqueeze(1).to_broadcast([P, 8, STATES]),
                        group_mask[:, s, :].unsqueeze(2).to_broadcast([P, 8, STATES]), ALU.mult)\
                        .then_inc(z_written, 1)

            in_pairs(pool, SSM_TILES, s5_tile)
            chain.n = n0 + 3 * SSM_TILES

            def layer_norm(l):
                pool.wait_ge(ln_centred, l + 1)
                pool.wait_ge(ln_landed, 32 * (l + 1))
                x = xtok[:, MT - 1, 0:LN_POOL]
                chain.add(pool.tensor_tensor(x, x, ln_rows[:, 0, 0:LN_POOL], ALU.mult))
                chain.settle()
                pool.tensor_tensor(x, x, ln_rows[:, 1, 0:LN_POOL], ALU.add).then_inc(ln_done, 1)

            def load_ln(l):
                for k, name in enumerate(("ln_g", "ln_b")):
                    pool.dma_start(ln_rows[:, k, :],
                                   a[name][l:l + 1, :].partition_broadcast(P).rearrange("p o d -> p (o d)"))\
                        .then_inc(ln_landed, 16)

            pool.wait_ge(act_l, split_steps(S_GLU + 1))
            chain.add(pool.memset(causal[:, :, :], 0.0))
            chain.settle()
            pool.affine_select(out=causal[:, :, :], in_=causal[:, :, :], compare_op=ALU.is_ge, fill=NEG, base=0,
                               pattern=[[P, MT], [-1, T]], channel_multiplier=1).then_inc(causal_made, 1)
            load_ln(0)
            pool.dma_start(gate_w, a["b_w_in"][0, :, NH * DH * (1 + BRANCHES):].rearrange(
                "(t p) n -> p t n", p=P)).then_inc(gate_w_landed, 16)
            layer_norm(0)

            for hh in range(2):
                for r in range(1, BRANCHES):
                    for u in nsa[hh][r]:
                        pool.wait_ge(o_used, u["group"] + 1)
                        pool.tensor_tensor(oT[:, u["h"], :], oT[:, u["h"], :], zT[:, u["h8"], :], ALU.add)\
                            .then_inc(branch_summed, 1)
            chain.add(pool.iota(later[:, :, :], [[-P, MT], [1, T]], base=0, channel_multiplier=-1,
                                allow_small_or_imprecise_dtypes=True))
            chain.settle()
            chain.add(pool.tensor_scalar(earlier[:, :, :], later[:, :, :], -1.0, 0.0, ALU.mult, ALU.max))
            chain.settle()
            pool.tensor_scalar(later[:, :, :], later[:, :, :], 0.0, None, ALU.max).then_inc(lags_made, 1)
            pool.wait_ge(act_l, split_steps(S_NSA + 1))
            load_ln(1)
            layer_norm(1)

            pool.wait_ge(pad_stored, 16)
            pool.wait_ge(ro_copied, H8)
            for r in range(ROWS):
                for h in range(H8):
                    src = bass.AP(tensor=rpb_dram.tensor,
                                  offset=(h * RPB_R + WIN_R - 1 - r) * P,
                                  ap=[[1, GRID], [P, ROWS], [1, GRID]])
                    q = r % 2
                    dst = table[GRID * q:GRID * (q + 1), h, (r // 2) * T:(r // 2 + 1) * T]
                    pool.dma_start(dst.rearrange("p (r c) -> p r c", c=GRID), src).then_inc(bias_landed, 16)

        @block.tensor
        def _(pe):
            def turn(call, src, rms=None):
                for k in range(FT // 2):
                    if rms is not None and k % (FT // 4) == 0:
                        for m in range(MT):
                            pe.wait_ge(scaled[m], 2 * SCALED[rms] - 1 + k // (FT // 4))
                    n = 8 * call + k
                    if n >= IN_FLIGHT:
                        pe.wait_ge(turned_l, 2 * (n - IN_FLIGHT + 1))
                    bank = turn_banks[n % IN_FLIGHT]
                    for f in range(2):
                        for m in range(MT):
                            ins = pe.transpose(bank[:, (f * MT + m) * P:(f * MT + m + 1) * P],
                                               src[:, m, (2 * k + f) * P:(2 * k + f + 1) * P], ident[:, :])
                    ins.then_inc(turned, 1)

            def one_block(ph, i, c, b, turn_call=None, splits=()):
                xH, xL = (hidH, hidL) if ph.hidden else (actH, actL)
                if b == 0 and ph.chunk0 + c >= 2:
                    pe.wait_ge(drained[ph.pair(c)], ph.pair_uses(i, c))
                pair = acc[:, 2 * ph.pair(c):2 * ph.pair(c) + 2, :]
                pe.wait_ge(l_made, ph.blocks_before(i, c, b) * 2 + 2)
                s = ph.block(c, b) % SPLIT_SLOTS
                high, low = (w[:, s, :].rearrange("p (t n) -> p t n", t=ph.kt) for w in (wH, wL))
                if ph.style == "tok":
                    last_k = ph.blocks * ph.kt - 1
                    if c == 0 and splits:
                        pe.wait_ge(act_l, split_steps(splits[0]) + b + 1)
                    for t in range(ph.kt):
                        k = b * ph.kt + t
                        for m in range(MT):
                            rows = slice(m * P, (m + 1) * P)
                            for n, (x, w) in enumerate(((xH, high), (xH, low), (xL, high))):
                                ins = pe.matmul(pair[:, m, :], x[:, k, rows], w[:, t, :],
                                                start=k == 0 and n == 0, stop=k == last_k and n == 2)
                else:
                    for f in range(ph.cols // P):
                        dst = pair[:, 0, (b + f) * T:(b + f + 1) * T]
                        for t in range(ph.kt):
                            if turn_call is not None and c == 0 and b == 0:
                                pe.wait_ge(turned_l, FT * turn_call + t + 1)
                            for n, (x, w) in enumerate(((xH, high), (xL, high), (xH, low))):
                                ins = pe.matmul(dst, w[:, t, f * P:(f + 1) * P], x[:, t, :],
                                                start=t == 0 and n == 0,
                                                stop=t == ph.kt - 1 and n == 2)
                ins.then_inc(blocks_done, 1)

            def dense(ph, turn_call=None, splits=()):
                with rep(pe, ph.iters) as i:
                    for c in range(ph.body):
                        for b in range(ph.blocks):
                            one_block(ph, i, c, b, turn_call, splits)

            def block_steps(ph):
                for i in range(ph.iters):
                    for c in range(ph.body):
                        for b in range(ph.blocks):
                            one_block(ph, i, c, b)
                            yield

            def head_means(part):
                for t in range(len(part) + 2):
                    yield
                    if t < len(part):
                        u = part[t]
                        n = u["n"]
                        pe.wait_ge(sq_ready, n + 1)
                        if n >= 2:
                            pe.wait_ge(hroot_ready, n - 1)
                        squares = [score[:, n % 2, j * P:(j + 1) * P] for j in range(2 * MT)]
                        if u["wide"]:
                            for m in range(MT):
                                for f in range(2):
                                    ins = pe.matmul(psA[:, n % 2, m:m + 1], squares[f * MT + m],
                                                    mean_of[:, 0:1], start=f == 0, stop=f == 1)
                        else:
                            for j in range(2 * MT):
                                ins = pe.matmul(psA[:, n % 2, j:j + 1], squares[j], mean_of[:, 0:1],
                                                start=True, stop=True)
                        ins.then_inc(mean_ready, 1)
                    if 0 <= t - 1 < len(part):
                        u = part[t - 1]
                        n = u["n"]
                        w = T if u["wide"] else 2 * T
                        pe.wait_ge(diag_ready, n + 1)
                        if n >= 2:
                            pe.wait_ge(normed, n - 1)
                        pe.matmul((psB, psC)[n % 2][:, 0:w], mean_of[:, :], probT[:, n % 2, 0:w], start=True,
                                  stop=True).then_inc(spread_ready, 1)

            def attend(part):
                for t in range(len(part) + 3):
                    if t < len(part):
                        u = part[t]
                        n = u["n"]
                        if "scores_after" in u:
                            await_chunks(pe, u["scores_after"])
                        if n >= 2:
                            pe.wait_ge(biased, n - 1)
                        for m in range(MT):
                            ins = pe.matmul(psA[:, n % 2, m * T:m * T + u["K"]], u["q"][:, m * P:(m + 1) * P],
                                            u["k"], start=True, stop=True)
                        ins.then_inc(scores_ready, 1)
                    yield
                    if 0 <= t - 1 < len(part):
                        u = part[t - 1]
                        n, K = u["n"], u["K"]
                        pe.wait_ge(probs_ready, n + 1)
                        if n >= 1:
                            pe.wait_ge(probT_ready, n)
                        for m in range(MT):
                            for kt in range(-(-K // P)):
                                w = min(P, K - kt * P)
                                ins = pe.transpose(psB[0:w, kt * T + m * P:kt * T + (m + 1) * P],
                                                   score[:, n % 2, m * T + kt * P:m * T + kt * P + w],
                                                   ident[:, :])
                        ins.then_inc(probs_turned, 1)
                    if 0 <= t - 2 < len(part):
                        u = part[t - 2]
                        n, K = u["n"], u["K"]
                        pe.wait_ge(probT_ready, n + 1)
                        if "values_after" in u:
                            await_chunk(pe, *u["values_after"])
                        if u["first"] and u["group"] >= 1:
                            pe.wait_ge(o_used, u["group"])
                        kts = -(-K // P)
                        for o in range(u["halves"]):
                            for kt in range(kts):
                                w = min(P, K - kt * P)
                                ins = pe.matmul(psC[:, o * T:(o + 1) * T], u["v"](kt, o),
                                                probT[0:w, n % 2, kt * T:(kt + 1) * T],
                                                start=u["first"] and kt == 0 and o == 0,
                                                stop=u["last"] and kt == kts - 1,
                                                skip_group_check=u["halves"] == 2)
                        ins.then_inc(o_ready, 1)

            pe.wait_ge(ident_made, 1)
            pe.wait_ge(consts_landed, 16 * N_CONST)
            pe.wait_ge(s5_dt, 1)
            pe.transpose(psA[:, 0, 0:P], rowsA[:, :], ident[:, :])
            pe.transpose(psA[:, 1, 0:P], rowsB[:, :], ident[:, :])
            pe.transpose(psB[:, 0:64], rowsC[:, :], ident[0:64, 0:64]).then_inc(cols_turned, 1)
            pe.wait_ge(lam_prod, 1)
            pe.wait_ge(masks_made, 1)
            pe.matmul(psC[:, 0:2], mean_of[:, :], lam[:, 0:2], start=True, stop=True).then_inc(lam_sum, 1)

            pe.wait_ge(cols_copied, 3)
            pe.wait_ge(lam_exp, 1)
            for l in range(DEPTH):
                turn(TURN_MEM[l], hs, RMS_MEM)
                dense(kv_mem[l][0], TURN_MEM[l])
                dense(kv_mem[l][1])
            pe.wait_ge(x_landed, 16)
            turn(TURN_X, xtok)
            await_turn(pe, TURN_X)
            alternate(head_means(norm_mem), block_steps(s5_u), [2] * 4)

            dense(s5_z)
            await_chunks(pe, s5_z)

            def s5_outputs(i, parity):
                pe.wait_ge(z_copied, i * 2 + 2)
                pe.wait_ge(h_ready, i * 2 + 2)
                for s, hx in enumerate((s5_hr, s5_hi)):
                    for j in range(4):
                        ins = pe.matmul(psB[:, parity * T:(parity + 1) * T], CT[:, 4 * s + j, :], hx[:, j, :],
                                        start=s == 0 and j == 0, stop=s == 1 and j == 3)
                ins.then_inc(y_ready, 1)

            def s5_tile(i, parity):
                pe.wait_ge(z_written, i * 6 + 4)
                wait_past(pe, z_copied, i * 2)
                for z in range(8):
                    ins = pe.transpose(psA[:, z // 4, (z % 4) * P:(z % 4 + 1) * P], ZB[:, z, :], ident[:, :])
                ins.then_inc(z_turned, 1)
                pe.wait_ge(z_copied, i * 2 + 1)
                wait_past(pe, bu_read, i * 4)
                for s in range(2):
                    for j in range(4):
                        ins = pe.matmul(acc[:, 2 * s + j // 2, (j % 2) * T:(j % 2 + 1) * T], BT[:, 4 * s + j, :],
                                        uT[:, bass.ts(i, 1), :].rearrange("p a t -> p (a t)"),
                                        start=True, stop=True)
                ins.then_inc(bu_ready, 1)
                if not (isinstance(i, int) and i == 0):
                    if not (isinstance(i, int) and i == 1):
                        pe.wait_ge(y_summed, i - 1)
                    s5_outputs(i - 1, 1 - parity)
                pe.wait_ge(z_written, i * 6 + 6)
                for z in range(8):
                    ins = pe.transpose(psA[:, z // 4, (z % 4) * P:(z % 4 + 1) * P], ZC[:, z, :], ident[:, :])
                ins.then_inc(z_turned, 1)

            in_pairs(pe, SSM_TILES, s5_tile)
            pe.wait_ge(y_summed, SSM_TILES - 1)
            s5_outputs(SSM_TILES - 1, 1)
            pe.wait_ge(act_l, split_steps(S_GELU + 1))
            dense(s5_glu)
            dense(s5_out, splits=[S_GLU])
            pe.wait_ge(ln_done, 2)
            turn(TURN_LN1, xtok)

            dense(kv_cmp[0], TURN_LN1)
            dense(kv_cmp[1])
            await_chunks(pe, kv_cmp[1])
            pe.wait_ge(pos_ready, 4)
            for s, (ph, src) in enumerate(zip(cmp_w1, (kcT, vcT))):
                for b in range(ph.blocks):
                    n = ph.block0 + b
                    pe.wait_ge(l_made, 2 * n + 2)
                    for j in range(16):
                        at = 16 * b + j
                        for part, w in enumerate((wH, wL)):
                            w1 = w[:, n % SPLIT_SLOTS, j * P:(j + 1) * P].bitcast(F32)
                            ins = pe.matmul(psA[:, s, 0:(KVH + 1) * NCMP], w1,
                                            src[:, :, at:at + (NCMP - 1) * STRIDE + 1:STRIDE],
                                            start=at == 0 and part == 0, stop=at == BLOCK - 1 and part == 1)
                    ins.then_inc(blocks_done, 1)
            dense(kv[0])
            pe.wait_ge(gate_w_landed, 16)
            for m in range(MT):
                for k in range(FT):
                    for part, x in enumerate((actH, actL)):
                        ins = pe.matmul(psB[:, m * NGATE:(m + 1) * NGATE],
                                        x[:, k, m * P:(m + 1) * P].bitcast(F32), gate_w[:, k, :],
                                        start=k == 0 and part == 0, stop=k == FT - 1 and part == 1)
            ins.then_inc(gate_sum, 1)
            pe.wait_ge(cmp_hid_ready, 2)
            pe.matmul(psC[:, 0:KVH * NCMP], w2[:, 0, :], cmp_hid[:, 0, :], start=True, stop=True)\
                .then_inc(cmp_out, 1)
            dense(kv[1])
            pe.wait_ge(cmp_ready, 1)
            for g in range(KVH):
                ins = pe.matmul(psC[0:NCMP, g * DH:(g + 1) * DH], cmp_hid[:, 1, g * NCMP:(g + 1) * NCMP],
                                w2[:, 1, :], start=True, stop=True)
            ins.then_inc(cmp_out, 1)
            dense(kv[2])
            dense(kv[3])
            dense(b_q[0])
            pe.wait_ge(cmp_ready, 2)
            pe.wait_ge(gate_ready, 3)
            await_chunks(pe, b_q[0])
            alternate(attend(nsa_units), join(*(block_steps(ph) for ph in (*b_z[0], b_q[1], *b_z[1]))),
                      nsa_counts)
            dense(b_out, splits=[S_NSA])

            turn(TURN_MIX[0], hs, RMS_MIX[0])
            dense(ab_rq, TURN_MIX[0])
            dense(ab_rk)
            dense(ab_rv)
            await_chunks(pe, ab_rv)

            def retention():
                for t in range(H8 + 1):
                    if t < H8:
                        if t >= 2:
                            pe.wait_ge(rs_decayed, t - 1)
                        for m in range(MT):
                            ins = pe.matmul(psA[:, t % 2, m * T:(m + 1) * T], rkT[:, t, m * P:(m + 1) * P],
                                            rqT[:, t, :], start=True, stop=True)
                        ins.then_inc(rs_ready, 1)
                    yield
                    if t >= 1:
                        h = t - 1
                        pe.wait_ge(rs_decayed, h + 1)
                        if h >= 1:
                            pe.wait_ge(ro_copied, h)
                        for m in range(MT):
                            ins = pe.matmul(psC[:, 0:T], rv[:, m, h * DH:(h + 1) * DH],
                                            score[:, h % 2, m * T:(m + 1) * T], start=m == 0, stop=m == MT - 1)
                        ins.then_inc(ro_ready, 1)

            def turn_biases():
                for h in range(H8):
                    yield
                    if h >= 2:
                        pe.wait_ge(bias_masked, h - 1)
                    pe.matmul(psA[:, h % 2, :], flip[:, :], table[:, h, :], start=True, stop=True)\
                        .then_inc(bias_turned, 1)

            blocks = join(block_steps(ab_nq), block_steps(ab_nk), block_steps(ab_nv))
            alternate(retention(), blocks, [1] * 8)
            alternate(head_means(norm_ret + norm_na), blocks, [1] * 12)
            pe.wait_ge(normed, norm_na[-1]["n"] + 1)
            pe.wait_ge(bias_landed, 16 * ROWS * H8)
            alternate(turn_biases(), blocks, [1] * 4)
            pe.wait_ge(bias_masked, H8)
            await_chunks(pe, ab_nv)
            alternate(attend(na), block_steps(ab_rg), [1] * 8)
            dense(ab_out, splits=[S_RET, S_NA])

            def tail_pe(l):
                xq, xo, parts = layers[l]
                turn(TURN_XA[l], hs, RMS_XA[l])
                dense(xq, TURN_XA[l])
                alternate(head_means(norm_x[l]))
                pe.wait_ge(normed, norm_x[l][-1]["n"] + 1)
                alternate(attend(xat[l]))
                pe.wait_ge(act_l, split_steps(S_X[l] + 1))
                dense(xo)
                turn(TURN_FFN[l], hs, RMS_FFN[l])
                for k, (ffn_in, ffn_out) in enumerate(parts):
                    dense(ffn_in, TURN_FFN[l] if k == 0 else None)
                    pe.wait_ge(hid_l, (l * FFN_T + sum(FFN_PARTS[:k + 1])) // 2)
                    dense(ffn_out)

            tail_pe(0)

            turn(TURN_MIX[1], hs, RMS_MIX[1])
            dense(c_q, TURN_MIX[1])
            blocks = join(block_steps(c_k), block_steps(c_v))
            alternate(head_means(norm_c), blocks, [2] * 8 + [1] * 4)
            pe.wait_ge(normed, norm_c[-1]["n"] + 1)
            alternate(attend(dif), blocks, [1] * 12)
            alternate(head_means(norm_do))
            dense(c_out, splits=[S_DIF])
            tail_pe(1)

        @block.scalar
        def _(act):
            chain = Chain(act, act_step)

            def root_of_mean_square(call, eps):
                act.wait_ge(ms_ready, call + 1)
                act.activation(root[:, :], mean_sq[:, :], ACT.Sqrt, bias=consts[:, eps:eps + 1])\
                    .then_inc(root_ready, 1)

            def rms_rows(call, src):
                root_of_mean_square(call, 0)
                act.wait_ge(rstd_ready, call + 1)
                for k in range(2):
                    cols = slice(k * D // 2, (k + 1) * D // 2)
                    act.activation(hs[:, 1, cols], src[:, 1, cols], ACT.Identity, scale=rstd[:, 1:2])\
                        .then_inc(scaled[1], 1)

            def turn_out(call, gain=None):
                for n in range(8 * call, 8 * call + 8):
                    act.wait_ge(turned, n + 1)
                    for f in range(2):
                        bank = turn_banks[n % IN_FLIGHT][:, f * T:(f + 1) * T]
                        k = 2 * (n - 8 * call) + f
                        scale = 1.0 if gain is None else colsB[:, gain + k:gain + k + 1]
                        act.activation(actH[:, k, :], bank, ACT.Identity, scale=scale).then_inc(turned_h, 1)

            def split(which, ready=None):
                src, n, first = SPLITS[which]
                for k in range(0, n, 4):
                    if ready is not None:
                        act.wait_ge(ready, k // 4 + 1)
                    act.activation(actH[:, first + k:first + k + 4, :], src[:, k:k + 4, :], ACT.Identity)\
                        .then_inc(act_h, 1)

            def split_weights(slot, split_slot, number, landings, first):
                act.wait_ge(landed[slot], landings)
                if first >= SPLIT_SLOTS:
                    act.wait_ge(blocks_done, number - (SPLIT_SLOTS - 1))
                for k in range(2):
                    cols = slice(k * HALF, (k + 1) * HALF)
                    act.copy(wH[:, split_slot, cols], ring[:, slot, cols]).then_inc(h_made, 1)

            def split_at(n):
                split_weights(n % SLOTS, n % SPLIT_SLOTS, n, 16 * (n // SLOTS + 1), n)

            def one_block(ph, i, c, b, fn):
                n = ph.block(c, b) + 1
                if n < plan["blocks"]:
                    split_weights(n % SLOTS, n % SPLIT_SLOTS, ph.blocks_before(i, c, b) + 1,
                                  i * (16 * ph.body * ph.blocks // SLOTS) + 16 * (n // SLOTS + 1), n)
                if b == ph.blocks - 1 and fn is not None:
                    drain_chunk(act, ph, i, c, fn)

            def dense(ph, fn=None):
                with rep(act, ph.iters) as i:
                    for c in range(ph.body):
                        for b in range(ph.blocks):
                            one_block(ph, i, c, b, fn)

            def block_steps(ph, fn=None):
                for i in range(ph.iters):
                    for c in range(ph.body):
                        for b in range(ph.blocks):
                            one_block(ph, i, c, b, fn)
                            yield

            def head_roots(part):
                for t in range(len(part) + 2):
                    if t < len(part):
                        u = part[t]
                        n = u["n"]
                        if "after" in u:
                            await_chunks(act, u["after"])
                        if n >= 2:
                            act.wait_ge(mean_ready, n - 1)
                        act.activation(score[:, n % 2, :], u["x"].rearrange("p a t -> p (a t)"), ACT.Square)\
                            .then_inc(sq_ready, 1)
                    yield
                    if 0 <= t - 1 < len(part):
                        u = part[t - 1]
                        n = u["n"]
                        w = MT if u["wide"] else 2 * MT
                        act.wait_ge(mean_ready, n + 1)
                        if n >= 2:
                            act.wait_ge(diag_ready, n - 1)
                        act.activation(head_rms[:, n % 2, 0:w], psA[:, n % 2, 0:w], ACT.Sqrt,
                                       bias=consts[:, 0:1], scale=0.5 if u["wide"] else 1.0)\
                            .then_inc(hroot_ready, 1)

            def attend(part):
                for t in range(len(part) + 3):
                    if t < len(part):
                        u = part[t]
                        n = u["n"]
                        act.wait_ge(max_ready, n + 1)
                        for m in range(MT):
                            s = score[:, n % 2, m * T:m * T + u["K"]]
                            act.activation(s, s, ACT.Exp, bias=neg_max[:, n % 2, m:m + 1],
                                           scale=SCALE if u["mode"] == "alibi" else 1.0,
                                           accum_out=denom[:, n % 2, m:m + 1]).then_inc(exp_ready, 1)
                    yield
                    if 0 <= t - 1 < len(part):
                        u = part[t - 1]
                        n, K = u["n"], u["K"]
                        act.wait_ge(probs_turned, n + 1)
                        if n >= 2:
                            act.wait_ge(o_ready, n - 1)
                        w = min(K, P)
                        size = T * -(-K // P)
                        act.copy(probT[0:w, n % 2, 0:size], psB[0:w, 0:size]).then_inc(probT_ready, 1)

            act.wait_ge(ident_made, 1)
            rms_rows(RMS_MEM, hs)
            split_at(0)
            act.wait_ge(cols_turned, 1)
            act.copy(colsA[:, :], psA[:, 0, 0:P]).then_inc(cols_copied, 1)
            act.copy(colsB[:, :], psA[:, 1, 0:P]).then_inc(cols_copied, 1)
            act.copy(colsC[:, :], psB[:, 0:64]).then_inc(cols_copied, 1)
            act.wait_ge(lam_sum, 1)
            act.activation(lam[:, 2:4], psC[:, 0:2], ACT.Exp, scale=float(P)).then_inc(lam_exp, 1)

            def small_numbers():
                act.wait_ge(lg_abs, 1)
                chain.add(act.activation(decay[:, 2, :], decay[:, 2, :], ACT.Exp, scale=-1.0))
                chain.settle()
                act.activation(decay[:, 2, :], decay[:, 2, :], ACT.Ln, bias=consts[:, 3:4]).then_inc(lg_ln, 1)
                chain.add(act.activation(ssm[:, 0, :], colsA[:, A_DT:A_DT + 32], ACT.Exp))
                chain.settle()
                yield
                act.wait_ge(s5_exp, 1)
                act.activation(ssm[:, 1, :], ssm[:, 1, :], ACT.Exp).then_inc(s5_exp, 1)
                yield
                act.wait_ge(s5_frac0, 1)
                act.activation(ssm[:, 4, :], ssm[:, 3, :], ACT.Sin, scale=TURN).then_inc(s5_trig0, 1)
                chain.add(act.activation(ssm[:, 5, :], ssm[:, 3, :], ACT.Abs))
                chain.settle()
                act.activation(ssm[:, 5, :], ssm[:, 5, :], ACT.Sin, scale=-TURN, bias=consts[:, 2:3])\
                    .then_inc(s5_trig0, 1)

            numbers = small_numbers()
            for l in range(DEPTH):
                turn_out(TURN_MEM[l], G_MEM + 16 * l)
                for ph in kv_mem[l]:
                    if ph in (kv_mem[0][1], kv_mem[1][0]):
                        for _ in block_steps(ph):
                            next(numbers, None)
                    else:
                        dense(ph)
            turn_out(TURN_X)
            await_chunks(act, kv_mem[1][1])
            alternate(head_roots(norm_mem), block_steps(s5_u), [2] * 4)

            dense(s5_z, lambda i, c, src: act.activation(
                zT5[:, bass.ds(i * 4 + 2 * c, 2), :], src, ACT.Silu))

            def s5_tile(i, parity):
                n = i + (act_steps + 1)
                act.wait_ge(z_turned, i * 2 + 1)
                wait_past(act, bu_ready, i)
                act.copy(BT, psA[:, :, :].rearrange("p a (b s) -> p (a b) s", s=P)).then_inc(z_copied, 1)
                act.wait_ge(phase_ready, i + 1)
                if not (isinstance(i, int) and i < 2):
                    act.wait_ge(h_ready, i * 2 - 2)
                act.activation(s5_cos[parity], s5_frac, ACT.Abs).then_inc(act_step, 1)
                act.activation(s5_sin[parity], s5_frac, ACT.Sin, scale=TURN).then_inc(trig_ready, 1)
                act.wait_ge(act_step, n)
                act.activation(s5_cos[parity], s5_cos[parity], ACT.Sin, scale=-TURN, bias=consts[:, 2:3])\
                    .then_inc(trig_ready, 1)
                act.wait_ge(z_turned, i * 2 + 2)
                wait_past(act, y_ready, i)
                act.copy(CT, psA[:, :, :].rearrange("p a (b s) -> p (a b) s", s=P)).then_inc(z_copied, 1)

            act_steps = chain.n
            in_pairs(act, SSM_TILES, s5_tile)
            chain.n += SSM_TILES
            for k in range(2):
                act.wait_ge(y_summed, SSM_TILES // 2 * (k + 1))
                g = gT[:, 4 * k:4 * k + 4, :]
                act.activation(g, g, ACT.Gelu_apprx_tanh).then_inc(gelu_done, 1)
            split(S_GELU, gelu_done)

            def glu_gate(i, c, src):
                for f in range(2):
                    ft = 2 * c + f
                    ins = act.activation(glT[:, ft, :], src[:, f, :], ACT.Sigmoid,
                                         bias=colsA[:, A_BGLU + ft:A_BGLU + ft + 1])
                    if f == 0:
                        chain.add(ins)
                        chain.settle()
                return ins

            dense(s5_glu, glu_gate)
            split(S_GLU, glu_mixed)
            dense(s5_out)
            root_of_mean_square(LN1, 1)
            turn_out(TURN_LN1)

            for ph in kv_cmp:
                dense(ph)
            for ph in cmp_w1:
                for b in range(ph.blocks):
                    split_at(ph.block0 + b + 1)
            for s in range(2):
                act.wait_ge(cmp_bias_ready, s + 1)
                act.activation(cmp_hid[:, s, :], psA[:, s, 0:KVH * NCMP], ACT.Gelu_apprx_tanh,
                               bias=cmp_bias[:, s:s + 1]).then_inc(cmp_hid_ready, 1)
            dense(kv[0])
            act.wait_ge(gate_sum, 1)
            act.activation(gates[:, :, :], psB[:, 0:MT * NGATE].rearrange("p (m n) -> p m n", m=MT),
                           ACT.Sigmoid).then_inc(gate_ready, 1)
            for ph in kv[1:]:
                dense(ph)
            dense(b_q[0])

            def silu_z(k):
                def fn(i, c, src):
                    tile = 4 * i + 2 * c
                    if k > 0:
                        hh, r = divmod(k - 1, BRANCHES)
                        if r == 0:
                            act.wait_ge(o_used, nsa[hh][0][tile + 1]["group"] + 1)
                        else:
                            act.wait_ge(branch_summed, NH * hh + 8 * (r - 1) + tile + 2)
                    return act.activation(zT[:, tile:tile + 2, :], src, ACT.Silu)
                return fn

            alternate(attend(nsa_units), join(*(
                [block_steps(b_z[0][r], silu_z(r)) for r in range(BRANCHES)] + [block_steps(b_q[1])] +
                [block_steps(b_z[1][r], silu_z(BRANCHES + r)) for r in range(BRANCHES)])), nsa_counts)
            act.wait_ge(branch_summed, 2 * NH)
            split(S_NSA)
            dense(b_out)
            root_of_mean_square(LN2, 1)

            rms_rows(RMS_MIX[0], xtok)
            turn_out(TURN_MIX[0], G_MIX)
            def decays():
                for h in range(H8):
                    yield
                    act.wait_ge(decay_arg, h + 1)
                    act.activation(table[:, h, :], table[:, h, :], ACT.Exp).then_inc(decay_ready, 1)

            dense(ab_rq)
            alternate(decays(), block_steps(ab_rk), [1] * 8)
            dense(ab_rv)
            blocks = join(block_steps(ab_nq), block_steps(ab_nk), block_steps(ab_nv))
            for _ in range(8):
                next(blocks)
            act.wait_ge(ro_copied, H8)
            alternate(head_roots(norm_ret + norm_na), blocks, [1] * 12)
            for _ in range(4):
                next(blocks)
            alternate(attend(na), block_steps(ab_rg, lambda i, c, src: act.activation(
                rgT[:, bass.ds(i * 4 + 2 * c, 2), :], src, ACT.Silu)), [1] * 8)
            act.wait_ge(gated, 1)
            act.wait_ge(o_used, na[-1]["group"] + 1)
            split(S_RET)
            split(S_NA)
            dense(ab_out)

            def tail_act(l):
                xq, xo, parts = layers[l]
                rms_rows(RMS_XA[l], xtok)
                turn_out(TURN_XA[l], G_X + 16 * l)
                dense(xq)
                await_chunks(act, xq)
                alternate(head_roots(norm_x[l]))
                alternate(attend(xat[l]))
                act.wait_ge(o_used, xat[l][-1]["group"] + 1)
                split(S_X[l])
                dense(xo)
                rms_rows(RMS_FFN[l], xtok)
                turn_out(TURN_FFN[l], G_FFN + 16 * l)
                pairs_done = l * FFN_T // 2
                for ffn_in, ffn_out in parts:
                    def finish(i, c, src):
                        n = i + pairs_done
                        if c == 0:
                            wait_past(act, drained[ffn_in.pair(1)], ffn_in.pair_uses(i, 1))
                            act.activation(silu_g, src, ACT.Silu).then_inc(drained[ffn_in.pair(0)], 1)
                        else:
                            act.wait_ge(drained[ffn_in.pair(1)], ffn_in.pair_uses(i, 1) + 1)
                            act.activation(hidH[:, bass.ts(i, 2), :], hid_f, ACT.Identity).then_inc(hid_h, 1)

                    with rep(act, ffn_in.iters) as i:
                        for c in range(2):
                            for b in range(2):
                                n = ffn_in.block(c, b) + 1
                                split_weights(n % SLOTS, n % SPLIT_SLOTS, ffn_in.blocks_before(i, c, b) + 1,
                                              i * 16 + 16 * (n // SLOTS + 1), n)
                            act.wait_ge(blocks_done, ffn_in.blocks_before(i, c, 2))
                            finish(i, c, acc[:, 2 * ffn_in.pair(c), :].rearrange("p (f t) -> p f t", t=T))
                    pairs_done += ffn_in.iters
                    dense(ffn_out)

            tail_act(0)
            rms_rows(RMS_MIX[1], xtok)
            turn_out(TURN_MIX[1], G_MIX + 16)
            dense(c_q)
            blocks = join(block_steps(c_k), block_steps(c_v))
            alternate(head_roots(norm_c), blocks, [2] * 8 + [1] * 4)
            alternate(attend(dif), blocks, [1] * 12)
            act.wait_ge(o_used, dif[-1]["group"] + 1)
            alternate(head_roots(norm_do))
            act.wait_ge(normed, norm_do[-1]["n"] + 1)
            split(S_DIF)
            dense(c_out)
            tail_act(1)

        @block.vector
        def _(dve):
            chain = Chain(dve, dve_step)

            def mean_squares(call, src, centred):
                if call in STATS_IN_DRAIN:
                    dve.wait_ge(stats_ready, (D // COLS) * (STATS_IN_DRAIN.index(call) + 1))
                else:
                    for m in range(MT):
                        for k in range(4):
                            chain.add(dve.bn_stats(stats[:, m, 6 * k:6 * k + 6],
                                                   src[:, m, k * COLS:(k + 1) * COLS]))
                    chain.settle()
                for m in range(MT):
                    chain.add(dve.bn_aggr(moments[:, m, :], stats[:, m, :]))
                chain.settle()
                mean, var = moments[:, :, 0:1].rearrange("p m o -> p (m o)"), \
                    moments[:, :, 1:2].rearrange("p m o -> p (m o)")
                if centred:
                    dve.tensor_copy(mean_sq[:, :], var).then_inc(ms_ready, 1)
                else:
                    chain.add(dve.tensor_tensor(mean_sq[:, :], mean, mean, ALU.mult))
                    chain.settle()
                    dve.tensor_tensor(mean_sq[:, :], mean_sq[:, :], var, ALU.add).then_inc(ms_ready, 1)
                dve.wait_ge(root_ready, call + 1)
                dve.reciprocal(rstd[:, :], root[:, :]).then_inc(rstd_ready, 1)
                dve.wait_ge(rstd_ready, call + 1)

            def rms_rows(call, src):
                mean_squares(call, src, False)
                for k in range(2):
                    cols = slice(k * D // 2, (k + 1) * D // 2)
                    dve.tensor_scalar(hs[:, 0, cols], src[:, 0, cols], rstd[:, 0:1], None, ALU.mult)\
                        .then_inc(scaled[0], 1)

            def layer_norm(call, l):
                mean_squares(call, xtok, True)
                dve.wait_ge(ln_landed, 32 * (l + 1))
                g, b = ln_rows[:, 0, :], ln_rows[:, 1, :]
                for m in reversed(range(MT)):
                    ins = dve.tensor_scalar(xtok[:, m, :], xtok[:, m, :], moments[:, m, 0:1],
                                            rstd[:, m:m + 1], ALU.subtract, ALU.mult)
                    if m == MT - 1:
                        ins.then_inc(ln_centred, 1)
                    else:
                        chain.add(ins)
                chain.settle()
                dve.wait_ge(ln_centred, l + 1)
                for w, op in ((g, ALU.mult), (b, ALU.add)):
                    for m, lo in ((0, 0), (MT - 1, LN_POOL)):
                        x = xtok[:, m, lo:]
                        ins = dve.tensor_tensor(x, x, w[:, lo:], op)
                        if op == ALU.mult or m == 0:
                            chain.add(ins)
                    chain.settle()
                ins.then_inc(ln_done, 1)
                dve.wait_ge(ln_done, 2 * (l + 1))

            def turn_out(call, gain=None):
                for n in range(8 * call, 8 * call + 8):
                    dve.wait_ge(turned_h, 2 * n + 2)
                    for f in range(2):
                        bank = turn_banks[n % IN_FLIGHT][:, f * T:(f + 1) * T]
                        k = 2 * (n - 8 * call) + f
                        scale = 1.0 if gain is None else colsB[:, gain + k:gain + k + 1]
                        dve.scalar_tensor_tensor(out=actL[:, k, :], in0=bank, scalar=scale,
                                                 in1=actH[:, k, :].bitcast(F32), op0=ALU.mult,
                                                 op1=ALU.subtract).then_inc(turned_l, 1)

            def split(which):
                src, n, first = SPLITS[which]
                for k in range(0, n, 4):
                    dve.wait_ge(act_h, split_steps(which) + k // 4 + 1)
                    dve.tensor_tensor(actL[:, first + k:first + k + 4, :], src[:, k:k + 4, :],
                                      actH[:, first + k:first + k + 4, :].bitcast(F32), ALU.subtract)\
                        .then_inc(act_l, 1)

            def split_weights(slot, split_slot, number):
                for k in range(2):
                    cols = slice(k * HALF, (k + 1) * HALF)
                    dve.wait_ge(h_made, number * 2 + (k + 1))
                    dve.tensor_tensor(wL[:, split_slot, cols], ring[:, slot, cols],
                                      wH[:, split_slot, cols].bitcast(F32), ALU.subtract).then_inc(l_made, 1)

            def one_block(ph, i, c, b, fn, then=None):
                n = ph.block(c, b) + 1
                if n < plan["blocks"]:
                    split_weights(n % SLOTS, n % SPLIT_SLOTS, ph.blocks_before(i, c, b) + 1)
                if b == ph.blocks - 1 and fn is not None:
                    drain_chunk(dve, ph, i, c, fn)
                    if then is not None:
                        then(i, c)

            def dense(ph, fn=None, then=None):
                with rep(dve, ph.iters) as i:
                    for c in range(ph.body):
                        for b in range(ph.blocks):
                            one_block(ph, i, c, b, fn, then)

            def block_steps(ph, fn=None):
                for i in range(ph.iters):
                    for c in range(ph.body):
                        for b in range(ph.blocks):
                            one_block(ph, i, c, b, fn)
                            yield

            def head_norm(part):
                for t in range(len(part) + 2):
                    yield
                    if 0 <= t - 1 < len(part):
                        u = part[t - 1]
                        n = u["n"]
                        w = MT if u["wide"] else 2 * MT
                        r = head_rms[:, n % 2, 0:w]
                        dve.wait_ge(hroot_ready, n + 1)
                        chain.add(dve.reciprocal(r, r))
                        chain.settle()
                        dve.scalar_tensor_tensor(
                            out=probT[:, n % 2, 0:w * P].rearrange("p (j t) -> p j t", t=P),
                            in0=ident[:, :].unsqueeze(1).to_broadcast([P, w, P]), scalar=float(P),
                            in1=r.unsqueeze(2).to_broadcast([P, w, P]), op0=ALU.mult, op1=ALU.mult)\
                            .then_inc(diag_ready, 1)
                    if t < 2:
                        continue
                    u = part[t - 2]
                    n = u["n"]
                    x, r = u["x"], (psB, psC)[n % 2]
                    dve.wait_ge(spread_ready, n + 1)
                    if u["wide"]:
                        for o in range(2):
                            chain.add(dve.scalar_tensor_tensor(
                                out=x[:, o, :], in0=x[:, o, :], scalar=colsA[:, u["g"][o]:u["g"][o] + 1],
                                in1=r[:, 0:T], op0=ALU.mult, op1=ALU.mult))
                        chain.settle()
                        dve.tensor_scalar(x, x, 1.0 - LAM_INIT, None, ALU.mult).then_inc(normed, 1)
                    else:
                        x = x.rearrange("p a t -> p (a t)")
                        dve.scalar_tensor_tensor(out=x, in0=x, scalar=colsA[:, u["g"][0]:u["g"][0] + 1],
                                                 in1=r[:, :], op0=ALU.mult, op1=ALU.mult).then_inc(normed, 1)

            def attend(part):
                for t in range(len(part) + 3):
                    if 0 <= t - 1 < len(part):
                        u = part[t - 1]
                        n, K = u["n"], u["K"]
                        s = score[:, n % 2, :].rearrange("p (m k) -> p m k", m=MT)[:, :, 0:K]
                        f = factor[:, n % 2, :]
                        dve.wait_ge(exp_ready, MT * (n + 1))
                        chain.add(dve.tensor_scalar(f, denom[:, n % 2, :], 1e-30, None, ALU.max))
                        chain.settle()
                        chain.add(dve.reciprocal(f, f))
                        chain.settle()
                        if u["gate"] is not None:
                            chain.add(dve.tensor_tensor(f, f, u["gate"], ALU.mult))
                            chain.settle()
                        dve.tensor_tensor(s, s, f.unsqueeze(2).to_broadcast([P, MT, K]), ALU.mult)\
                            .then_inc(probs_ready, 1)
                    if t < len(part):
                        u = part[t]
                        n, K = u["n"], u["K"]
                        src = psA[:, n % 2, :].rearrange("p (m k) -> p m k", m=MT)[:, :, 0:K]
                        s = score[:, n % 2, :].rearrange("p (m k) -> p m k", m=MT)[:, :, 0:K]
                        dve.wait_ge(scores_ready, n + 1)
                        if n >= 2:
                            dve.wait_ge(probs_turned, n - 1)
                        if u["mode"] == "bias":
                            ins = dve.scalar_tensor_tensor(out=s, in0=src, scalar=SCALE, in1=u["bias"],
                                                           op0=ALU.mult, op1=ALU.add)
                        elif u["mode"] == "alibi":
                            ins = dve.scalar_tensor_tensor(out=s, in0=later[:, :, :], scalar=-u["bias"] / SCALE,
                                                           in1=src, op0=ALU.mult, op1=ALU.add)
                        else:
                            ins = dve.tensor_scalar(s, src, SCALE, None, ALU.mult)
                        ins.then_inc(biased, 1)
                        dve.wait_ge(biased, n + 1)
                        ins = dve.tensor_reduce(neg_max[:, n % 2, :], s, AX_X, ALU.max, negate=True)
                        if u["mode"] == "alibi":
                            chain.add(ins)
                            chain.settle()
                            ins = dve.tensor_scalar(neg_max[:, n % 2, :], neg_max[:, n % 2, :], SCALE, None,
                                                    ALU.mult)
                        ins.then_inc(max_ready, 1)
                    yield
                    if 0 <= t - 3 < len(part) and part[t - 3]["last"]:
                        u = part[t - 3]
                        dve.wait_ge(o_ready, u["n"] + 1)
                        if u["fin"] == "gate":
                            await_chunk(dve, *u["output_after"])
                            dst = oT[:, u["h"], :] if u["r"] == 0 else zT[:, u["h8"], :]
                            ins = dve.tensor_tensor(dst, psC[:, 0:T], zT[:, u["h8"], :], ALU.mult)
                        elif u["halves"] == 2:
                            ins = dve.tensor_copy(u["to"], psC[:, :].rearrange("p (o t) -> p o t", o=2))
                        else:
                            ins = dve.tensor_copy(u["to"], psC[:, 0:T])
                        ins.then_inc(o_used, 1)

            def residual(ph, factor_, statistics=True):
                def add(i, c, src):
                    x = xtok[:, :, bass.ts(i * ph.body + c, ph.cols)]
                    if factor_ == 1.0:
                        return dve.tensor_tensor(x, x, src, ALU.add)
                    return dve.scalar_tensor_tensor(out=x, in0=x, scalar=factor_, in1=src, op0=ALU.mult,
                                                    op1=ALU.add)
                def chunk_stats(i, c):
                    dve.wait_ge(drained[ph.pair(c)], ph.pair_uses(i, c) + 1)
                    for m in range(MT):
                        ins = dve.bn_stats(stats[:, m, bass.ds((i * ph.body + c) * 6, 6)],
                                           xtok[:, m, bass.ts(i * ph.body + c, ph.cols)])
                        if m == MT - 1:
                            ins.then_inc(stats_ready, 1)
                dense(ph, add, chunk_stats if statistics else None)
                await_chunks(dve, ph)

            def copy_to(ph, dst):
                if ph.style == "feat":
                    return lambda i, c, src: dve.tensor_copy(
                        dst[:, bass.ds(i * (2 * ph.body) + 2 * c, 2), :], src)
                return lambda i, c, src: dve.tensor_copy(
                    dst[:, :, bass.ds(i * (COLS * ph.body) + COLS * c, COLS)], src)

            def keep(ph, dst):
                dense(ph, copy_to(ph, dst))

            def keep_steps(ph, dst):
                return block_steps(ph, copy_to(ph, dst))

            dve.wait_ge(mem_landed, 16)
            rms_rows(RMS_MEM, hs)
            split_weights(0, 0, 0)
            dve.wait_ge(ldt_landed, 16)
            dve.tensor_copy(rowsA[64:96, :].rearrange("j (h p) -> j h p", h=2),
                            ldt2[64:96, :].unsqueeze(2).to_broadcast([32, 2, STATES])).then_inc(s5_dt, 1)
            dve.wait_ge(cols_copied, 3)
            chain.add(dve.tensor_tensor(lam[:, 0:1], colsA[:, C_LAM:C_LAM + 1], colsA[:, C_LAM + 1:C_LAM + 2],
                                        ALU.mult))
            chain.settle()
            dve.tensor_tensor(lam[:, 1:2], colsA[:, C_LAM + 2:C_LAM + 3], colsA[:, C_LAM + 3:C_LAM + 4],
                              ALU.mult).then_inc(lam_prod, 1)

            def small(out_, x, y, op):
                chain.add(dve.tensor_tensor(ssm[:, out_, :], x, y, op))
                chain.settle()

            def scaled_by(out_, x, s1, s2, op0, op1):
                chain.add(dve.tensor_scalar(ssm[:, out_, :], x, s1, s2, op0, op1))
                chain.settle()

            def V(k):
                return ssm[:, k, :]

            def small_numbers():
                dve.wait_ge(lam_exp, 1)
                chain.add(dve.tensor_tensor(lam[:, 4:5], lam[:, 3:4], lam[:, 2:3], ALU.subtract))
                chain.settle()
                chain.add(dve.tensor_scalar(lam[:, 7:8], lam[:, 4:5], -LAM_INIT, None, ALU.add))
                dve.wait_ge(consts_landed, 16 * N_CONST)
                chain.add(dve.tensor_scalar(decay[:, 1, :], decay[:, 0, :], -1.0, None, ALU.mult))
                chain.settle()
                dve.tensor_tensor(decay[:, 2, :], decay[:, 0, :], decay[:, 1, :], ALU.max).then_inc(lg_abs, 1)
                yield
                dve.wait_ge(lg_ln, 1)
                chain.add(dve.tensor_scalar(decay[:, 3, :], decay[:, 0, :], 0.0, None, ALU.min))
                chain.settle()
                chain.add(dve.tensor_tensor(decay[:, 3, :], decay[:, 3, :], decay[:, 2, :], ALU.subtract))

                re, im = colsA[:, A_RE:A_RE + 32], colsA[:, A_IM:A_IM + 32]
                dve.wait_ge(act_step, 2)
                dve.tensor_tensor(V(1), re, V(0), ALU.mult).then_inc(s5_exp, 1)
                small(2, im, V(0), ALU.mult)
                scaled_by(6, V(2), 1.0 / TWO_PI, ROUND, ALU.mult, ALU.add)
                scaled_by(6, V(6), ROUND, None, ALU.subtract, ALU.bypass)
                for c in (PI2_A, PI2_B, PI2_C):
                    chain.add(dve.scalar_tensor_tensor(out=V(2), in0=V(6), scalar=-c, in1=V(2), op0=ALU.mult,
                                                       op1=ALU.add))
                    chain.settle()
                yield
                scaled_by(3, V(2), 1.0 / TWO_PI, 0.5, ALU.mult, ALU.min)
                dve.tensor_scalar(V(3), V(3), -0.5, None, ALU.max).then_inc(s5_frac0, 1)
                yield
                dve.wait_ge(s5_trig0, 2)
                dve.wait_ge(s5_exp, 2)
                small(7, V(1), V(5), ALU.mult)
                small(8, V(1), V(4), ALU.mult)
                scaled_by(7, V(7), -1.0, None, ALU.add, ALU.bypass)
                small(9, re, re, ALU.mult)
                small(10, im, im, ALU.mult)
                small(9, V(9), V(10), ALU.add)
                chain.add(dve.reciprocal(V(9), V(9)))
                chain.settle()
                yield
                small(10, V(7), re, ALU.mult)
                small(11, V(8), im, ALU.mult)
                small(10, V(10), V(11), ALU.add)
                small(12, V(10), V(9), ALU.mult)
                yield
                small(10, V(8), re, ALU.mult)
                small(11, V(7), im, ALU.mult)
                small(10, V(10), V(11), ALU.subtract)
                small(13, V(10), V(9), ALU.mult)

            numbers = small_numbers()

            for l in range(DEPTH):
                turn_out(TURN_MEM[l], G_MEM + 16 * l)
                for ph, dst in zip(kv_mem[l], (mem_kT[:, l], mem_v[:, l])):
                    if ph in (kv_mem[0][1], kv_mem[1][0]):
                        for _ in keep_steps(ph, dst):
                            next(numbers, None)
                    else:
                        keep(ph, dst)
            turn_out(TURN_X)
            alternate(head_norm(norm_mem), keep_steps(s5_u, uT), [2] * 4)

            dense(s5_z)
            dve.wait_ge(b_landed, 64)
            dve.wait_ge(normed, len(norm_mem))
            def per_state(v):
                return v.unsqueeze(2).to_broadcast([P, 32, GROUP])

            def wide(v):
                return v.rearrange("p (j c) -> p j c", c=GROUP)

            br, bi, t0 = wide(b_raw[:, 0, :]), wide(b_raw[:, 1, :]), s5_t1.rearrange("p a t -> p (a t)")[:, 0:512]
            for k, (x, y, op) in enumerate(((br, bi, ALU.subtract), (bi, br, ALU.add))):
                chain.add(dve.tensor_tensor(wide(bbar[:, k, :]), x, per_state(V(12)), ALU.mult))
                chain.add(dve.tensor_tensor(wide(t0), y, per_state(V(13)), ALU.mult))
                chain.settle()
                chain.add(dve.tensor_tensor(bbar[:, k, :], bbar[:, k, :], t0, op))
                chain.settle()
            await_chunks(dve, s5_z)
            dve.memset(ZB, 0.0).then_inc(s5_begins, 1)
            n0 = chain.n
            per = 14

            def s5_sum(i, parity):
                dve.wait_ge(y_ready, i + 1)
                dve.scalar_tensor_tensor(
                    out=gT[:, bass.ts(i, 1), :].rearrange("p a t -> p (a t)"),
                    in0=uT[:, bass.ts(i, 1), :].rearrange("p a t -> p (a t)"),
                    scalar=colsA[:, bass.ds(i + A_D, 1)], in1=psB[:, parity * T:(parity + 1) * T],
                    op0=ALU.mult, op1=ALU.add).then_inc(y_summed, 1)

            def s5_tile(i, parity):
                chain.n = i * per + n0
                sin, cos = s5_sin[parity], s5_cos[parity]
                wait_past(dve, h_ready, i * 2)
                dve.wait_ge(bu_ready, i + 1)
                dve.wait_ge(trig_ready, i * 2 + 2)
                bur, bui = (acc[:, k:k + 2, :].rearrange("p a (b t) -> p (a b) t", t=T) for k in (0, 2))
                dve.tensor_tensor(s5_gr, bur, cos, ALU.mult).then_inc(bu_read, 1)
                dve.tensor_tensor(s5_t1, bui, sin, ALU.mult).then_inc(bu_read, 1)
                dve.tensor_tensor(s5_gi, bui, cos, ALU.mult).then_inc(bu_read, 1)
                dve.tensor_tensor(s5_t2, bur, sin, ALU.mult).then_inc(bu_read, 1)
                dve.wait_ge(bu_read, i * 4 + 4)
                chain.add(dve.tensor_tensor(s5_gr, s5_gr, s5_t1, ALU.add))
                chain.add(dve.tensor_tensor(s5_gi, s5_gi, s5_t2, ALU.subtract))
                chain.settle()
                for j in range(4):
                    mag = ssm[:, 1, bass.ds(i * 4 + j, 1)].to_broadcast([P, T])
                    for g in (s5_gr, s5_gi):
                        ins = dve.tensor_tensor_scan(g[:, j, :], mag, g[:, j, :], 0.0, ALU.mult, ALU.add)
                        chain.add(ins)
                chain.settle()
                if not (isinstance(i, int) and i == 0):
                    s5_sum(i - 1, 1 - parity)
                chain.add(dve.tensor_tensor(s5_hr, s5_gr, cos, ALU.mult))
                chain.add(dve.tensor_tensor(s5_t1, s5_gi, sin, ALU.mult))
                chain.settle()
                dve.tensor_tensor(s5_hr, s5_hr, s5_t1, ALU.subtract).then_inc(h_ready, 1)
                dve.wait_ge(h_ready, i * 2 + 1)
                chain.add(dve.tensor_tensor(s5_hi, s5_gr, sin, ALU.mult))
                dve.tensor_tensor(s5_t1, s5_gi, cos, ALU.mult).then_inc(dve_step, 1)
                chain.n += 1
                chain.settle()
                dve.tensor_tensor(s5_hi, s5_hi, s5_t1, ALU.add).then_inc(h_ready, 1)
                dve.wait_ge(h_ready, i * 2 + 2)

            in_pairs(dve, SSM_TILES, s5_tile)
            s5_sum(SSM_TILES - 1, 1)
            chain.n = n0 + per * SSM_TILES
            split(S_GELU)
            for c, _ in enumerate(block_steps(s5_glu)):
                x = glT[:, 2 * c:2 * c + 2, :]
                await_chunk(dve, s5_glu, c)
                chain.add(dve.tensor_tensor(x, x, gT[:, 2 * c:2 * c + 2, :], ALU.mult))
                chain.settle()
                ins = dve.tensor_tensor(x, x, zT5[:, 2 * c:2 * c + 2, :], ALU.mult)
                if c % 2 == 0:
                    chain.add(ins)
                    chain.settle()
                else:
                    ins.then_inc(glu_mixed, 1)
            dve.wait_ge(glu_mixed, 2)
            split(S_GLU)
            residual(s5_out, ALPHA)
            layer_norm(LN1, 0)
            turn_out(TURN_LN1)

            for s, x in enumerate((kcT, vcT)):
                dve.memset(x[:, KVH, BLOCK:T], 0.0).then_inc(pos_ready, 1)
                dve.tensor_copy(x[:, KVH, 0:BLOCK], colsC[:, BLOCK * s:BLOCK * (s + 1)]).then_inc(pos_ready, 1)
            for ph, dst in zip(kv_cmp, (kcT, vcT)):
                keep(ph, dst)
            for ph in cmp_w1:
                for b in range(ph.blocks):
                    n = ph.block0 + b + 1
                    split_weights(n % SLOTS, n % SPLIT_SLOTS, n)
            for s, ph in enumerate(cmp_w1):
                dve.wait_ge(blocks_done, ph.block0 + ph.blocks)
                dve.tensor_copy(cmp_bias[:, s:s + 1], psA[:, s, KVH * NCMP:KVH * NCMP + 1])\
                    .then_inc(cmp_bias_ready, 1)
            keep(kv[0], ksT)
            dve.wait_ge(gate_ready, 1)
            for m in range(MT):
                dve.tensor_scalar(gates[:, m, 0:NH], gates[:, m, 0:NH], row_ok[:, m:m + 1], None, ALU.mult)\
                    .then_inc(gate_ready, 1)
            dve.wait_ge(cmp_out, 1)
            dve.tensor_copy(kcmpT[:, :, :], psC[:, 0:KVH * NCMP].rearrange("p (g n) -> p g n", g=KVH))\
                .then_inc(cmp_ready, 1)
            keep(kv[1], v_slc)
            dve.wait_ge(cmp_out, 2)
            dve.tensor_copy(vcmp[:, :, :], psC[0:NCMP, :].rearrange("p (g n) -> p g n", g=KVH))\
                .then_inc(cmp_ready, 1)
            dve.wait_ge(gate_ready, 3)
            keep(kv[2], kwT)
            keep(kv[3], v_win)
            keep(b_q[0], qT)
            dve.wait_ge(causal_made, 1)
            alternate(attend(nsa_units), join(*(
                [block_steps(ph) for ph in b_z[0]] + [keep_steps(b_q[1], qT)] +
                [block_steps(ph) for ph in b_z[1]])), nsa_counts)
            dve.wait_ge(branch_summed, 2 * NH)
            split(S_NSA)
            residual(b_out, ALPHA)
            layer_norm(LN2, 1)

            rms_rows(RMS_MIX[0], xtok)
            turn_out(TURN_MIX[0], G_MIX)
            keep(ab_rq, rqT)

            def decays():
                for h in range(H8):
                    d = table[:, h, :]
                    chain.add(dve.tensor_scalar(d, later[:, :, :].rearrange("p m t -> p (m t)"),
                                                decay[:, 3, h:h + 1], None, ALU.mult))
                    chain.settle()
                    dve.scalar_tensor_tensor(out=d, in0=earlier[:, :, :].rearrange("p m t -> p (m t)"),
                                             scalar=decay[:, 3, 8 + h:9 + h], in1=d, op0=ALU.mult,
                                             op1=ALU.add).then_inc(decay_arg, 1)
                    yield

            dve.wait_ge(lags_made, 1)
            alternate(decays(), keep_steps(ab_rk, rkT), [1] * 8)
            keep(ab_rv, rv)

            def retention():
                for t in range(H8 + 1):
                    if t < H8:
                        dve.wait_ge(rs_ready, t + 1)
                        dve.wait_ge(decay_ready, t + 1)
                        if t >= 2:
                            dve.wait_ge(ro_ready, t - 1)
                        dve.scalar_tensor_tensor(out=score[:, t % 2, :], in0=psA[:, t % 2, :], scalar=SCALE,
                                                 in1=table[:, t, :], op0=ALU.mult, op1=ALU.mult)\
                            .then_inc(rs_decayed, 1)
                    yield
                    if t >= 1:
                        dve.wait_ge(ro_ready, t)
                        dve.tensor_copy(rqT[:, t - 1, :], psC[:, 0:T]).then_inc(ro_copied, 1)

            def mask_biases():
                for h in range(H8):
                    yield
                    dve.wait_ge(bias_turned, h + 1)
                    dve.tensor_tensor(table[:, h, :].rearrange("p (n c) -> p n c", c=GRID),
                                      psA[:, h % 2, :].rearrange("p (n c) -> p n c", c=GRID),
                                      col_mask[:, :].unsqueeze(1).to_broadcast([P, MT * ROWS, GRID]), ALU.add)\
                        .then_inc(bias_masked, 1)

            blocks = join(keep_steps(ab_nq, nqT), keep_steps(ab_nk, nkT), keep_steps(ab_nv, nv))
            alternate(retention(), blocks, [1] * 8)
            dve.wait_ge(ro_copied, H8)
            alternate(head_norm(norm_ret + norm_na), blocks, [1] * 12)
            alternate(mask_biases(), blocks, [1] * 4)
            dve.wait_ge(bias_masked, H8)
            alternate(attend(na), block_steps(ab_rg), [1] * 8)
            await_chunks(dve, ab_rg)
            dve.tensor_tensor(rgT, rgT, rqT, ALU.mult).then_inc(gated, 1)
            dve.wait_ge(gated, 1)
            dve.wait_ge(o_used, na[-1]["group"] + 1)
            split(S_RET)
            split(S_NA)
            residual(ab_out, 1.0)

            def tail_dve(l):
                xq, xo, parts = layers[l]
                rms_rows(RMS_XA[l], xtok)
                turn_out(TURN_XA[l], G_X + 16 * l)
                keep(xq, xqT)
                await_chunks(dve, xq)
                alternate(head_norm(norm_x[l]))
                alternate(attend(xat[l]))
                dve.wait_ge(o_used, xat[l][-1]["group"] + 1)
                split(S_X[l])
                residual(xo, 1.0)
                rms_rows(RMS_FFN[l], xtok)
                turn_out(TURN_FFN[l], G_FFN + 16 * l)
                pairs_done = l * FFN_T // 2
                for ffn_in, ffn_out in parts:
                    with rep(dve, ffn_in.iters) as i:
                        for c in range(2):
                            for b in range(2):
                                n = ffn_in.block(c, b) + 1
                                split_weights(n % SLOTS, n % SPLIT_SLOTS, ffn_in.blocks_before(i, c, b) + 1)
                        dve.wait_ge(drained[ffn_in.pair(0)], ffn_in.pair_uses(i, 0) + 1)
                        dve.wait_ge(blocks_done, ffn_in.blocks_before(i, 1, 2))
                        dve.tensor_tensor(hid_f, silu_g,
                                          acc[:, 2 * ffn_in.pair(1), :].rearrange("p (f t) -> p f t", t=T),
                                          ALU.mult).then_inc(drained[ffn_in.pair(1)], 1)
                        dve.wait_ge(drained[ffn_in.pair(1)], ffn_in.pair_uses(i, 1) + 1)
                        dve.wait_ge(hid_h, i + (pairs_done + 1))
                        dve.tensor_tensor(hidL[:, bass.ts(i, 2), :], hid_f,
                                          hidH[:, bass.ts(i, 2), :].bitcast(F32), ALU.subtract)\
                            .then_inc(hid_l, 1)
                    pairs_done += ffn_in.iters
                    residual(ffn_out, 1.0, statistics=ffn_out is parts[-1][1] and l == 0)

            tail_dve(0)
            rms_rows(RMS_MIX[1], xtok)
            turn_out(TURN_MIX[1], G_MIX + 16)
            chain.add(dve.tensor_tensor(later[:, :, :], later[:, :, :], earlier[:, :, :], ALU.add))
            chain.settle()
            keep(c_q, dqT)
            blocks = join(keep_steps(c_k, dkT), keep_steps(c_v, dv))
            alternate(head_norm(norm_c), blocks, [2] * 8 + [1] * 4)
            alternate(attend(dif), blocks, [1] * 12)
            dve.wait_ge(o_used, dif[-1]["group"] + 1)
            alternate(head_norm(norm_do))
            dve.wait_ge(normed, norm_do[-1]["n"] + 1)
            split(S_DIF)
            residual(c_out, 1.0)
            tail_dve(1)


N_CONST = 27
_IN = ['x', 'a_w_in', 'a_lam_re', 'a_lam_im', 'a_log_dt', 'a_b_re', 'a_b_im', 'a_c_re', 'a_c_im', 'a_d',
       'a_w_glu', 'a_b_glu', 'a_w_out', 'kv_w', 'cmp_pos_k', 'cmp_w1_k', 'cmp_w2_k', 'cmp_pos_v', 'cmp_w1_v',
       'cmp_w2_v', 'b_w_in', 'b_w_out', 'ln_g', 'ln_b', 'mem_2', 'norm_mix_g_2', 'norm_xattn_g_2',
       'norm_mem_g_2', 'norm_ffn_g_2', 'w_in_ab_2', 'ret_decay_fwd_2', 'ret_decay_bwd_2', 'ret_out_g_2',
       'na_q_g_2', 'na_k_g_2', 'na_rpb_2', 'w_out_ab_2', 'w_in_c_2', 'diff_q_g_2', 'diff_k_g_2',
       'lambda_q1_2', 'lambda_k1_2', 'lambda_q2_2', 'lambda_k2_2', 'diff_out_g_2', 'w_out_c_2', 'w_xq_2',
       'w_xkv_2', 'w_xo_2', 'xq_g_2', 'xk_g_2', 'w_ffn_in_2', 'w_ffn_out_2']


def kernel(**inputs):
    import numpy as _np
    import concourse.bacc as _bacc
    from concourse.bass_utils import run_bass_kernel_spmd as _run

    nc = _bacc.Bacc("TRN2", target_bir_lowering=False, num_devices=1)
    arrays, aps = {}, {}
    for name in _IN:
        x = _np.ascontiguousarray(inputs[name])
        arrays[f"in_{name}"] = x
        aps[name] = nc.dram_tensor(f"in_{name}", x.shape, mybir.dt.from_np(x.dtype), kind="ExternalInput").ap()
    out = nc.dram_tensor("out_x", (1, T, D), F32, kind="ExternalOutput").ap()
    program(nc, aps, out)
    r = _run(nc, [arrays], core_ids=[0])
    return r.results[0]["out_x"]
```
